# Optimizing a Trainium2 kernel written in Bass

```python
import jax, jax.numpy as jnp
from jax import lax
import numpy as np

D_MODEL = 1024
BATCH = 1
SEQ = 512
DEPTH = 2

CHUNK = 64
N_MEM = 256
N_MIXERS = 4
EPS = 1e-6
ROPE_THETA = 10000.0

A_EXPAND = 128
A_HEADS = D_MODEL // A_EXPAND
A_KDIM = A_EXPAND
A_VDIM = D_MODEL // A_HEADS
A_WIDTH = A_HEADS * A_KDIM
B_KERNEL = 31
B_WIDTH = D_MODEL
C_HEAD_DIM = 64
C_Q_HEADS = D_MODEL // C_HEAD_DIM
C_GROUP = 8
C_KV_HEADS = C_Q_HEADS // C_GROUP
C_WINDOW = 128
C_WINDOW_CHUNKS = C_WINDOW // CHUNK
C_Q_WIDTH = C_Q_HEADS * C_HEAD_DIM
C_KV_WIDTH = C_KV_HEADS * C_HEAD_DIM
D_HEAD_DIM = 64
D_HEADS = D_MODEL // D_HEAD_DIM
D_WIDTH = D_HEADS * D_HEAD_DIM
D_QBLOCK = 128
X_HEADS = 4
X_HEAD_DIM = 128
X_WIDTH = X_HEADS * X_HEAD_DIM
MIX_WIDTH = D_MODEL
OUT_IN = MIX_WIDTH + X_WIDTH
A_IN = 4 * A_WIDTH + X_WIDTH
B_IN = 2 * B_WIDTH + X_WIDTH
C_IN = C_Q_WIDTH + 2 * C_KV_WIDTH + X_WIDTH
D_IN = 3 * D_WIDTH + D_HEADS + X_WIDTH
FFN_HIDDEN = -(-8 * D_MODEL // (3 * 256)) * 256

kernel_name = "hybrid_interleaved_streaming_trunk"

F32 = jnp.float32

def _n_using(m):
    return (DEPTH - m + N_MIXERS - 1) // N_MIXERS

def rmsnorm(x, g):
    xf = x.astype(F32)
    y = xf * lax.rsqrt(jnp.mean(xf * xf, axis=-1, keepdims=True) + EPS)
    return (y * g.astype(F32)).astype(x.dtype)

def rope_tables(positions, dim):
    inv = 1.0 / (ROPE_THETA ** (jnp.arange(0, dim, 2, dtype=F32) / dim))
    ang = positions.astype(F32)[..., None] * inv
    return jnp.cos(ang), jnp.sin(ang)

def apply_rope(x, cos, sin):
    half = x.shape[-1] // 2
    x1, x2 = x[..., :half], x[..., half:]
    c = cos[:, :, None, :].astype(x.dtype)
    s = sin[:, :, None, :].astype(x.dtype)
    return jnp.concatenate([x1 * c - x2 * s, x2 * c + x1 * s], axis=-1)

def hgrn2_mixer(h, lb, onorm_g):
    B, S, _ = h.shape
    nC = S // CHUNK
    q, fz, i, g = jnp.split(h, 4, axis=-1)
    q = jax.nn.silu(q.astype(F32))
    lbf = lb.astype(F32)
    f = lbf + (1.0 - lbf) * jax.nn.sigmoid(fz.astype(F32))
    logf = jnp.log(f)
    k = 1.0 - f
    v = i.astype(F32)

    def to_chunks(t, d):
        return t.reshape(B, nC, CHUNK, A_HEADS, d).transpose(1, 0, 3, 2, 4)

    qc, kc, vc = to_chunks(q, A_KDIM), to_chunks(k, A_KDIM), to_chunks(v, A_VDIM)
    bc = jnp.cumsum(to_chunks(logf, A_KDIM), axis=3)
    causal = jnp.tril(jnp.ones((CHUNK, CHUNK), dtype=bool))

    def step(state, inp):
        q_, k_, v_, b_ = inp
        o_inter = jnp.einsum('bhck,bhkv->bhcv', q_ * jnp.exp(b_), state)
        diff = b_[:, :, :, None, :] - b_[:, :, None, :, :]
        decay = jnp.exp(jnp.where(causal[None, None, :, :, None], diff, -jnp.inf))
        att = jnp.einsum('bhtk,bhsk,bhtsk->bhts', q_, k_, decay)
        o = o_inter + jnp.einsum('bhts,bhsv->bhtv', att, v_)
        b_last = b_[:, :, -1:, :]
        k_dec = k_ * jnp.exp(b_last - b_)
        state = jnp.exp(b_last[:, :, 0, :])[..., None] * state + jnp.einsum('bhck,bhcv->bhkv', k_dec, v_)
        return state, o

    state0 = jnp.zeros((B, A_HEADS, A_KDIM, A_VDIM), F32)
    _, oc = lax.scan(step, state0, (qc, kc, vc, bc))
    o = oc.transpose(1, 0, 3, 2, 4).reshape(B, S, A_HEADS, A_VDIM)
    o = o * lax.rsqrt(jnp.mean(o * o, axis=-1, keepdims=True) + EPS) * onorm_g.astype(F32)
    o = o * jax.nn.silu(g.astype(F32).reshape(B, S, A_HEADS, A_VDIM))
    return o.reshape(B, S, A_WIDTH).astype(h.dtype)

def conv_mixer(h, dw_w, dw_b, ln_g, ln_b):
    a, gate = jnp.split(h, 2, axis=-1)
    u = a * jax.nn.sigmoid(gate)
    y = lax.conv_general_dilated(
        u, dw_w[:, None, :].astype(u.dtype), window_strides=(1,),
        padding=[(B_KERNEL - 1, 0)], dimension_numbers=('NWC', 'WIO', 'NWC'),
        feature_group_count=B_WIDTH) + dw_b
    yf = y.astype(F32)
    mu = jnp.mean(yf, axis=-1, keepdims=True)
    var = jnp.mean(jnp.square(yf - mu), axis=-1, keepdims=True)
    yn = (yf - mu) * lax.rsqrt(var + EPS) * ln_g.astype(F32) + ln_b.astype(F32)
    return jax.nn.silu(yn).astype(h.dtype)

def _window_blocks(t):
    nC = t.shape[1]
    tp = jnp.pad(t, ((0, 0), (C_WINDOW_CHUNKS - 1, 0), (0, 0), (0, 0), (0, 0)))
    return jnp.concatenate([tp[:, j:j + nC] for j in range(C_WINDOW_CHUNKS)], axis=2)

def swa_mixer(h, sinks, cos, sin):
    B, S, _ = h.shape
    nC = S // CHUNK
    q = h[..., :C_Q_WIDTH].reshape(B, S, C_Q_HEADS, C_HEAD_DIM)
    k = h[..., C_Q_WIDTH:C_Q_WIDTH + C_KV_WIDTH].reshape(B, S, C_KV_HEADS, C_HEAD_DIM)
    v = h[..., C_Q_WIDTH + C_KV_WIDTH:].reshape(B, S, C_KV_HEADS, C_HEAD_DIM)
    q = apply_rope(q, cos, sin)
    k = apply_rope(k, cos, sin)
    qb = q.reshape(B, nC, CHUNK, C_KV_HEADS, C_GROUP, C_HEAD_DIM)
    kw = _window_blocks(k.reshape(B, nC, CHUNK, C_KV_HEADS, C_HEAD_DIM))
    vw = _window_blocks(v.reshape(B, nC, CHUNK, C_KV_HEADS, C_HEAD_DIM))
    s = jnp.einsum('bnqhgd,bnkhd->bhgnqk', qb, kw).astype(F32) * (C_HEAD_DIM ** -0.5)
    key_chunk = jnp.arange(nC)[:, None] + (jnp.arange(C_WINDOW_CHUNKS * CHUNK) // CHUNK)[None, :] - (C_WINDOW_CHUNKS - 1)
    valid = key_chunk >= 0
    s = jnp.where(valid[None, None, None, :, None, :], s, -jnp.inf)
    sink = jnp.broadcast_to(sinks.astype(F32).reshape(1, C_KV_HEADS, C_GROUP, 1, 1, 1), s.shape[:-1] + (1,))
    p = jax.nn.softmax(jnp.concatenate([s, sink], axis=-1), axis=-1)[..., :-1]
    o = jnp.einsum('bhgnqk,bnkhd->bnqhgd', p.astype(vw.dtype), vw)
    return o.reshape(B, S, C_Q_WIDTH)

def fox_mixer(h):
    B, S, _ = h.shape
    q = h[..., :D_WIDTH].reshape(B, S, D_HEADS, D_HEAD_DIM)
    k = h[..., D_WIDTH:2 * D_WIDTH].reshape(B, S, D_HEADS, D_HEAD_DIM)
    v = h[..., 2 * D_WIDTH:3 * D_WIDTH].reshape(B, S, D_HEADS, D_HEAD_DIM)
    logf = jax.nn.log_sigmoid(h[..., 3 * D_WIDTH:].astype(F32))
    c = jnp.cumsum(logf, axis=1).transpose(0, 2, 1)
    scale = D_HEAD_DIM ** -0.5
    outs = []
    for blk in range(S // D_QBLOCK):
        lo, hi = blk * D_QBLOCK, (blk + 1) * D_QBLOCK
        s = jnp.einsum('bqhd,bkhd->bhqk', q[:, lo:hi], k[:, :hi]).astype(F32) * scale
        s = s + c[:, :, lo:hi, None] - c[:, :, None, :hi]
        mask = jnp.arange(hi)[None, :] <= (lo + jnp.arange(D_QBLOCK))[:, None]
        p = jax.nn.softmax(jnp.where(mask[None, None], s, -jnp.inf), axis=-1)
        outs.append(jnp.einsum('bhqk,bkhd->bqhd', p.astype(v.dtype), v[:, :hi]))
    return jnp.concatenate(outs, axis=1).reshape(B, S, D_WIDTH)

def cross_attn(xq, mem_k, mem_v):
    B, S, _ = xq.shape
    q = xq.reshape(B, S, X_HEADS, X_HEAD_DIM)
    k = mem_k.reshape(B, -1, X_HEADS, X_HEAD_DIM)
    v = mem_v.reshape(B, -1, X_HEADS, X_HEAD_DIM)
    s = jnp.einsum('bshd,bmhd->bhsm', q, k).astype(F32) * (X_HEAD_DIM ** -0.5)
    p = jax.nn.softmax(s, axis=-1)
    o = jnp.einsum('bhsm,bmhd->bshd', p.astype(v.dtype), v)
    return o.reshape(B, S, X_WIDTH)

def setup_inputs(seed: int = 0) -> dict:
    key = jax.random.key(seed)
    ks = jax.random.split(key, 40)
    nrm = lambda k, shape, scale: jax.random.normal(k, shape, F32) * scale
    gain = lambda k, shape: 1.0 + 0.05 * jax.random.normal(k, shape, F32)
    n_a, n_b, n_c, n_d = _n_using(0), _n_using(1), _n_using(2), _n_using(3)
    start = jax.random.randint(ks[2], (BATCH, 1), 0, 4096, dtype=jnp.int32)
    positions = start + jnp.arange(SEQ, dtype=jnp.int32)[None, :]
    return {
        "x": nrm(ks[0], (BATCH, SEQ, D_MODEL), 1.0),
        "mem": nrm(ks[1], (BATCH, N_MEM, D_MODEL), 1.0),
        "positions": positions,
        "norm_mix_g": gain(ks[3], (DEPTH, D_MODEL)),
        "norm_ffn_g": gain(ks[4], (DEPTH, D_MODEL)),
        "w_out": nrm(ks[5], (DEPTH, OUT_IN, D_MODEL), OUT_IN ** -0.5),
        "xattn_w_kv": nrm(ks[6], (DEPTH, D_MODEL, 2 * X_WIDTH), D_MODEL ** -0.5),
        "ffn_w_gu": nrm(ks[7], (DEPTH, D_MODEL, 2 * FFN_HIDDEN), D_MODEL ** -0.5),
        "ffn_w_down": nrm(ks[8], (DEPTH, FFN_HIDDEN, D_MODEL), FFN_HIDDEN ** -0.5),
        "mem_norm_g": gain(ks[9], (D_MODEL,)),
        "final_norm_g": gain(ks[10], (D_MODEL,)),
        "a_w_in": nrm(ks[11], (n_a, D_MODEL, A_IN), D_MODEL ** -0.5),
        "a_b_in": nrm(ks[12], (n_a, A_IN), 0.02),
        "a_lb_table": nrm(ks[13], (DEPTH + 1, A_WIDTH), 0.5),
        "a_onorm_g": gain(ks[14], (n_a, A_VDIM)),
        "b_w_in": nrm(ks[15], (n_b, D_MODEL, B_IN), D_MODEL ** -0.5),
        "b_b_in": nrm(ks[16], (n_b, B_IN), 0.02),
        "b_dw_w": nrm(ks[17], (n_b, B_KERNEL, B_WIDTH), B_KERNEL ** -0.5),
        "b_dw_b": nrm(ks[18], (n_b, B_WIDTH), 0.02),
        "b_ln_g": gain(ks[19], (n_b, B_WIDTH)),
        "b_ln_b": nrm(ks[20], (n_b, B_WIDTH), 0.02),
        "c_w_in": nrm(ks[21], (n_c, D_MODEL, C_IN), D_MODEL ** -0.5),
        "c_b_in": nrm(ks[22], (n_c, C_IN), 0.02),
        "c_sinks": nrm(ks[23], (n_c, C_Q_HEADS), 0.5),
        "d_w_in": nrm(ks[24], (n_d, D_MODEL, D_IN), D_MODEL ** -0.5),
        "d_b_in": nrm(ks[25], (n_d, D_IN), 0.02),
    }

def reference(x, mem, positions, norm_mix_g, norm_ffn_g, w_out, xattn_w_kv, ffn_w_gu, ffn_w_down,
              mem_norm_g, final_norm_g, a_w_in, a_b_in, a_lb_table, a_onorm_g,
              b_w_in, b_b_in, b_dw_w, b_dw_b, b_ln_g, b_ln_b,
              c_w_in, c_b_in, c_sinks, d_w_in, d_b_in):
    cos, sin = rope_tables(positions, C_HEAD_DIM)
    mem_n = rmsnorm(mem, mem_norm_g)
    lb_all = jnp.cumsum(jax.nn.softmax(a_lb_table.astype(F32), axis=0), axis=0)
    for layer in range(DEPTH):
        mixer = layer % N_MIXERS
        j = layer // N_MIXERS
        hn = rmsnorm(x, norm_mix_g[layer])
        if mixer == 0:
            proj = hn @ a_w_in[j] + a_b_in[j]
            m_out = hgrn2_mixer(proj[..., :-X_WIDTH], lb_all[layer], a_onorm_g[j])
        elif mixer == 1:
            proj = hn @ b_w_in[j] + b_b_in[j]
            m_out = conv_mixer(proj[..., :-X_WIDTH], b_dw_w[j], b_dw_b[j], b_ln_g[j], b_ln_b[j])
        elif mixer == 2:
            proj = hn @ c_w_in[j] + c_b_in[j]
            m_out = swa_mixer(proj[..., :-X_WIDTH], c_sinks[j], cos, sin)
        else:
            proj = hn @ d_w_in[j] + d_b_in[j]
            m_out = fox_mixer(proj[..., :-X_WIDTH])
        xq = proj[..., -X_WIDTH:]
        kv = mem_n @ xattn_w_kv[layer]
        x_out = cross_attn(xq, kv[..., :X_WIDTH], kv[..., X_WIDTH:])
        x = x + jnp.concatenate([m_out, x_out], axis=-1) @ w_out[layer]
        hn = rmsnorm(x, norm_ffn_g[layer])
        gu = hn @ ffn_w_gu[layer]
        x = x + (jax.nn.silu(gu[..., :FFN_HIDDEN]) * gu[..., FFN_HIDDEN:]) @ ffn_w_down[layer]
    return rmsnorm(x, final_norm_g)


_drawn_inputs = setup_inputs


def setup_inputs(seed=0):
    import zlib

    import numpy as np

    out = dict(_drawn_inputs(seed))
    spreads = {}
    factors = {'mem_norm_g': 8.0,
     'a_lb_table': 7.636,
     'b_b_in': 6.766,
     'b_dw_b': 16.408,
     'b_ln_b': 31.619,
     'a_onorm_g': 4.123,
     'b_ln_g': 8.0,
     'norm_ffn_g': 3.234}
    for name, (base, spread) in spreads.items():
        noise = np.random.default_rng([zlib.crc32(name.encode()), seed]).standard_normal(out[name].shape)
        drawn = base * np.exp(spread * noise) if base else spread * noise
        out[name] = __import__('jax').numpy.asarray(drawn.astype(out[name].dtype))
    for name, factor in factors.items():
        out[name] = (out[name] * factor).astype(out[name].dtype)
    return out
```

```python
from contextlib import ExitStack

import concourse.bass as bass
from concourse import mybir

F32 = mybir.dt.float32
F32R = mybir.dt.float32r
U32 = mybir.dt.uint32
ALU = mybir.AluOpType
ACT = mybir.ActivationFunctionType
AX_X = mybir.AxisListType.X

P = 128
EPS = 1e-6
CHUNK = 1024


def trunk(nc, x, mem, g_mix, g_ffn, w_out, w_kv, w_gu, w_down, g_mem, g_fin,
          a_w, a_b, a_lb, a_on, b_w, b_b, b_dw, b_dwb, b_lng, b_lnb, out):
    S, D = x.shape[1], x.shape[2]
    M = mem.shape[1]
    KT = D // P
    ST = S // P
    MT = M // P
    XH = 4
    XW = XH * P
    NH = D // P
    FH = w_down.shape[1]
    FT = FH // P
    MIXT = KT + XH
    TAPS = b_dw.shape[1]
    PAD = TAPS - 1
    NLB = a_lb.shape[0]
    GT = 4
    LV = 10
    MASKED = 8
    XSCALE = float(P) ** -0.5

    sizes = [("kv0", 2 * XH), ("kv1", 2 * XH), ("xq0", XH), ("val", 2 * GT), ("head", 3 * NH),
             ("out0", MIXT), ("gu0", 2 * FT), ("down0", FT),
             ("xq1", XH), ("conv", 2 * KT), ("out1", MIXT), ("gu1", 2 * FT), ("down1", FT)]
    first, NCH = {}, 0
    for name, n in sizes:
        first[name] = NCH
        NCH += n
    tile0, nt = {}, 0
    for name, n in (("kv0", XH), ("kv1", XH), ("xq0", XH), ("head", 3 * NH), ("gu0", 2 * FT),
                    ("xq1", XH), ("conv", 2 * KT), ("gu1", 2 * FT)):
        tile0[name] = nt
        nt += n
    X_PAIRS = list(range(KT // 2, MIXT // 2))
    M_PAIRS = list(range(KT // 2))
    out_order = [[(g, k) for g in range(2) for k in X_PAIRS + M_PAIRS],
                 [(0, k) for k in X_PAIRS + M_PAIRS] + [(1, k) for k in X_PAIRS + M_PAIRS]]

    vec_rows, col, at = [], {}, 0
    for name, ap in (("mix0", g_mix[0]), ("mix1", g_mix[1]), ("ffn0", g_ffn[0]), ("ffn1", g_ffn[1]),
                     ("mem", g_mem), ("fin", g_fin), ("a_b", a_b[0]), ("lb0", a_lb[0]), ("lb1", a_lb[1]),
                     ("lb2", a_lb[2]), ("a_on", a_on[0])):
        n = ap.shape[0] // P
        vec_rows.append((0, at, ap.rearrange("(r c) -> r c", c=P), n))
        col[name] = at
        at += n
    rows_in = [at]
    base = at
    at = 0
    for name, ap in (("b_b", b_b[0]), ("dwb", b_dwb[0]), ("lng", b_lng[0]), ("lnb", b_lnb[0])):
        n = ap.shape[0] // P
        vec_rows.append((1, at, ap.rearrange("(r c) -> r c", c=P), n))
        col[name] = base + at
        at += n
    rows_in.append(at)
    base += at
    dw_rows = b_dw[0].rearrange("t (r c) -> (t r) c", c=P)
    half = TAPS * KT // 2
    for g in range(2):
        vec_rows.append((2 + g, 0, dw_rows[g * half:(g + 1) * half], half))
        rows_in.append(half)
    col["dw"] = base
    NCOL = base + 2 * half

    with ExitStack() as ctx:
        where = [nc.sbuf_base + (-nc.sbuf_base) % 64]

        def place(name, shape, dt=F32, at=None):
            size = 4
            for n in shape[1:]:
                size *= n
            at = at and at + (-at) % 32
            if at is None:
                at = where[0]
                where[0] += size + (-size) % 32
            return nc.alloc_sbuf_tensor_at(name, shape, dt, offset=at)

        def sem(name):
            return ctx.enter_context(nc.semaphore(name))

        ident = place("ident", [P, P])
        ones = place("ones", [P, P])
        mask = place("mask", [P, MASKED, P])
        cst = place("cst", [P, NCOL])
        headc = place("headc", [P, 6, NH])
        hc = place("hc", [P, 2, 6])
        small = place("small", [P, 128])
        xT = place("xT", [P, KT, S])
        xgH = place("xgH", [P, KT, S], F32R)
        xgL = place("xgL", [P, KT, S], F32R)
        raw = place("raw", [P, 2, CHUNK])
        wH = place("wH", [P, 2, CHUNK], F32R)
        wL = place("wL", [P, 2, CHUNK], F32R)
        rinv = place("rinv", [P, S])
        msq = place("msq", [P, S])
        sqsum = place("sqsum", [P, S])
        sq = place("sq", [P, 2, S])
        xgt = place("xgt", [P, 2, S])
        evt = place("evt", [P, 2, S])
        at_kv = where[0]
        KTs = [place(f"memK{i}", [P, XH, M]) for i in range(1)]
        VMs = [place(f"memV{i}", [P, MT, XW]) for i in range(1)]
        KTs.append(place("memK1", [P, XH, M]))
        VMs.append(place("memV1", [P, MT, XW]))
        arena = where[0]
        actH = place("actH", [P, FT, S], F32R, at=arena)
        actL = place("actL", [P, FT, S], F32R, at=arena + 4 * FT * S)
        mixH = place("mixH", [P, MIXT, S], F32R)
        mixL = place("mixL", [P, MIXT, S], F32R)
        at_val = where[0]
        val = place("val", [P, ST, D])
        at_heads = where[0]
        qb = place("qb", [P, 2, S])
        fb = place("fb", [P, 2, S])
        kb = place("kb", [P, 2, S])
        gb = place("gb", [P, 2, S])
        at_tail = where[0]
        tb = place("tb", [P, S])
        vh = place("vh", [P, 2, ST, P])
        osq = place("osq", [P, S])
        oinv = place("oinv", [P, S])
        mixt = place("mixt", [P, S])
        att = place("att", [P, ST, S], at=at_kv)
        vbias = place("vbias", [P, D], at=at_tail)
        xq = place("xq", [P, XH, S], at=at_heads)
        prob = place("prob", [P, ST, M], at=at_heads + 4 * XH * S)
        probT = place("probT", [P, MT, S], at=at_heads + 4 * XH * S + 4 * ST * M)
        memH = place("memH", [P, KT, M], F32R, at=arena)
        memL = place("memL", [P, KT, M], F32R, at=arena + 4 * KT * M)
        mrow = place("mrow", [P, MT, D], at=arena + 8 * KT * M)
        xrow = place("xrow", [P, ST, D], at=arena + 8 * KT * M + 4 * MT * D)
        vrow = place("vrow", [P, 4, P], at=arena + 8 * KT * M + 4 * MT * D + 4 * ST * D)
        mtmp = place("mtmp", [P, 2, M], at=at_val)
        msc = place("msc", [P, MT, D], at=at_val + 8 * M)
        y = place("y", [P, KT, S], at=at_val)
        upad = place("upad", [P, 2, PAD + S], at=at_tail)
        gate = place("gate", [P, 2, S], at=at_tail + 8 * (PAD + S) + 32)
        mu = place("mu", [P, S], at=at_tail + 8 * (PAD + S) + 32 + 8 * S)
        hcv = place("hcv", [P, 2, TAPS + 3])
        orow = place("orow", [P, ST, D], at=at_val)
        yT = place("yT", [P, KT, S], at=arena)
        assert max(where[0], arena + 8 * FT * S) <= nc.sbuf_usable_end, (where, nc.sbuf_usable_end)

        ps = ctx.enter_context(nc.psum_tensor("ps", [P, 8, 512], F32))

        landed = [sem("landed0"), sem("landed1")]
        hi_ready = sem("hi_ready")
        lo_ready = sem("lo_ready")
        chunk_done = sem("chunk_done")
        tile_free = sem("tile_free")
        s_rows, s_mem, s_x, s_vb = sem("s_rows"), sem("s_mem"), sem("s_x"), sem("s_vb")
        s_const, s_zero, s_pool = sem("s_const"), sem("s_zero"), sem("s_pool")
        s_tr, s_cst = sem("s_tr"), sem("s_cst")
        m_ss, m_ms, m_inv, m_row = sem("m_ss"), sem("m_ms"), sem("m_inv"), sem("m_row")
        m_tr, m_g, m_hi, m_lo = sem("m_tr"), sem("m_g"), sem("m_hi"), sem("m_lo")
        lbc = sem("lbc")
        lbe = sem("lbe")
        x_tr = sem("x_tr")
        kv_done = sem("kv_done")
        x_upd = sem("x_upd")
        xg_ready, xg_hi, xg_lo = sem("xg_ready"), sem("xg_hi"), sem("xg_lo")
        sq_ready, sq_sum = sem("sq_ready"), sem("sq_sum")
        stat_done = sem("stat_done")
        ms_ready = sem("ms_ready")
        r_ready = sem("r_ready")
        xq_ready = sem("xq_ready")
        sc_done, mx_ready, p_exp, p_norm = sem("sc_done"), sem("mx_ready"), sem("p_exp"), sem("p_norm")
        pt_done, pt_ready, xo_done, xo_hi, xo_lo = (sem("pt_done"), sem("pt_ready"), sem("xo_done"),
                                                    sem("xo_hi"), sem("xo_lo"))
        v_done = sem("v_done")
        hc_ready = sem("hc_ready")
        h_act = sem("h_act")
        k_ready = sem("k_ready")
        lv_ready, lv_done, lv_taken = sem("lv_ready"), sem("lv_done"), sem("lv_taken")
        t_ready = sem("t_ready")
        o_done, o_sq, o_stat, o_ms, o_inv = sem("o_done"), sem("o_sq"), sem("o_stat"), sem("o_ms"), sem("o_inv")
        o_step = sem("o_step")
        mix_lo = sem("mix_lo")
        mix_hi = sem("mix_hi")
        silu_ready = sem("silu_ready")
        act_step, act_lo = sem("act_step"), sem("act_lo")
        c_gate, c_sig, c_u, c_tap, c_y = sem("c_gate"), sem("c_sig"), sem("c_u"), sem("c_tap"), sem("c_y")
        c_pool, c_mu, c_cent, c_sq, c_var, c_act, c_norm = (sem("c_pool"), sem("c_mu"), sem("c_cent"), sem("c_sq"),
                                                            sem("c_var"), sem("c_act"), sem("c_norm"))
        f_y, f_tr, f_row, s_out = sem("f_y"), sem("f_tr"), sem("f_row"), sem("s_out")

        block = ctx.enter_context(nc.Block())

        HEADS_LOOP = (NH - 2) // 2

        @block.sync
        def _(sp):
            def fetch(n, source, shape):
                num, par = n
                if not isinstance(source.offset, int):
                    sp.lower_val(source.offset * 4)
                if not (isinstance(num, int) and num < 2):
                    sp.wait_ge(lo_ready, num - 1)
                sp.dma_start(raw[:, par, :].rearrange("p (k c) -> p k c", c=shape), source).then_inc(landed[par], 16)

            def columns(w, c0):
                return w.rearrange("(k p) c -> p k c", p=P)[:, :, bass.ds(c0, P)]

            def rows(w, k0, c0):
                return w.rearrange("(k p) c -> p k c", p=P)[:, bass.ds(k0, 2), c0:c0 + 512]

            sp.dma_start(mrow[:, :, :], mem[0].rearrange("(t p) d -> p t d", p=P)).then_inc(s_mem, 16)
            for layer in range(2):
                for c in range(2 * XH):
                    n = first[f"kv{layer}"] + c
                    if c < XH:
                        fetch((n, n % 2), columns(w_kv[layer], c * P), P)
                    else:
                        fetch((n, n % 2), rows(w_kv[layer], 2 * (c - XH), XW), 512)
                    if n == 1:
                        for t in range(ST):
                            sp.dma_start(xrow[:, t, :], x[0, t * P:(t + 1) * P, :]).then_inc(s_x, 16)
                        sp.dma_start(vbias[:, :], a_b[0:1, 2 * D:3 * D].partition_broadcast(P)[:, 0, :]).then_inc(s_vb, 16)
            for layer in range(2):
                n = first[f"xq{layer}"]
                w_in, xcol = (a_w[0], 4 * D) if layer == 0 else (b_w[0], 2 * D)
                for c in range(XH):
                    fetch((n + c, c % 2), columns(w_in, xcol + c * P), P)
                if layer == 0:
                    n = first["val"]
                    for c in range(2 * GT):
                        fetch((n + c, c % 2), rows(w_in, 2 * (c % GT), 2 * D + 512 * (c // GT)), 512)
                    n = first["head"]
                    with sp.Fori(0, NH // 2) as i:
                        for h in range(2):
                            for j, kind in enumerate((1, 0, 3)):
                                c = 3 * h + j
                                fetch((n + c + i * 6, c % 2), columns(w_in, kind * D + h * P + i * (2 * P)), P)
                else:
                    n = first["conv"]
                    with sp.Fori(0, KT) as i:
                        for j in range(2):
                            fetch((n + j + i * 2, j), columns(w_in, (1 - j) * D + i * P), P)
                n = first[f"out{layer}"]
                for c, (g, k) in enumerate(out_order[layer]):
                    fetch((n + c, c % 2), rows(w_out[layer], 2 * k, 512 * g), 512)
                n = first[f"gu{layer}"]
                with sp.Fori(0, FT) as i:
                    for j in range(2):
                        fetch((n + j + i * 2, j), columns(w_gu[layer], j * FH + i * P), P)
                n = first[f"down{layer}"]
                pairs = FT // 2
                with sp.Fori(0, (pairs - 1) // 2) as i:
                    for j in range(2):
                        fetch((n + j + i * 2, j), rows(w_down[layer], (2 * j) + i * 4, 0), 512)
                fetch((n + pairs - 1, 0), rows(w_down[layer], 2 * (pairs - 1), 0), 512)
                fetch((n + pairs, 1), rows(w_down[layer], 0, 512), 512)
                with sp.Fori(0, (pairs - 1) // 2) as i:
                    for j in range(2):
                        fetch((n + pairs + 1 + j + i * 2, j), rows(w_down[layer], 2 + (2 * j) + i * 4, 512), 512)
            for t in range(ST):
                sp.wait_ge(f_row, KT)
                sp.dma_start(out[0, t * P:(t + 1) * P, :], orow[:, t, :]).then_inc(s_out, 16)
            sp.wait_ge(s_out, 16 * ST)

        @block.gpsimd
        def _(pool):
            step = [0]

            def link(ins):
                step[0] += 1
                ins.then_inc(s_pool, 1)
                pool.wait_ge(s_pool, step[0])

            link(nc.gpsimd.memset(ident[:, :], 1.0))
            link(nc.gpsimd.affine_select(out=ident[:, :], in_=ident[:, :], compare_op=ALU.is_equal, fill=0.0,
                                         base=0, pattern=[[-1, P]], channel_multiplier=1))
            nc.gpsimd.memset(ones[:, :], 1.0).then_inc(s_const, 1)
            link(nc.gpsimd.memset(mask[:, :, :], 0.0))
            link(nc.gpsimd.tensor_copy(mask[:, 0, :], ident[:, :]))
            for lv in range(1, MASKED):
                L = 1 << (lv - 1)
                nb = P // (2 * L)
                odd = mask[:, lv, :].rearrange("p (n two l) -> p n two l", two=2, l=L)[:, :, 1, :]
                link(nc.gpsimd.memset(odd, 1.0))
                link(nc.gpsimd.affine_select(out=odd, in_=odd, compare_op=ALU.is_ge, fill=0.0, base=0,
                                             pattern=[[-2 * L, nb], [0, L]], channel_multiplier=1))
                link(nc.gpsimd.affine_select(out=odd, in_=odd, compare_op=ALU.is_ge, fill=0.0, base=L - 1,
                                             pattern=[[2 * L, nb], [0, L]], channel_multiplier=-1))
            nc.gpsimd.memset(small[:, 127:128], 0.0).then_inc(s_const, 1)

            def sum_squares(norm, k0, k1):
                for k in range(max(k0, 1), k1):
                    pool.wait_ge(sq_ready, KT * norm + k + 1)
                    if k > 1:
                        pool.wait_ge(sq_sum, (KT - 1) * norm + k - 1)
                    nc.gpsimd.tensor_tensor(sqsum[:, :], sqsum[:, :], sq[:, k % 2, :], ALU.add).then_inc(sq_sum, 1)

            sum_squares(0, 0, KT)
            pool.wait_ge(xo_lo, XH)
            pool.wait_ge(xo_done, XH)
            nc.gpsimd.memset(att[:, :, :], 0.0).then_inc(s_zero, 1)
            sum_squares(1, 0, KT)
            sum_squares(2, 0, KT)
            pool.wait_ge(mix_lo, NH)
            nc.gpsimd.memset(upad[:, :, 0:PAD], 0.0).then_inc(s_zero, 1)
            n = first["conv"]
            pool.wait_ge(lo_ready, n + 2)
            for i in range(KT):
                for j in range(2):
                    pool.wait_ge(hi_ready, n + 2 * i + j + 3)
                    nc.gpsimd.tensor_tensor(wL[:, j, :], raw[:, j, :], wH[:, j, :].bitcast(F32),
                                            ALU.subtract).then_inc(lo_ready, 1)
                if i >= 2:
                    pool.wait_ge(c_y, i)
                    if i > 2:
                        pool.wait_ge(c_pool, i - 2)
                    nc.gpsimd.tensor_tensor(mu[:, :], (y[:, 0, :] if i == 2 else mu[:, :]), y[:, i - 1, :],
                                            ALU.add).then_inc(c_pool, 1)
            pool.wait_ge(c_y, KT)
            pool.wait_ge(c_pool, KT - 2)
            nc.gpsimd.tensor_tensor(mu[:, :], mu[:, :], y[:, KT - 1, :], ALU.add).then_inc(c_pool, 1)
            sum_squares(3, 0, KT)
            sum_squares(4, 0, KT)

        def at_chunk(base, i=0, k=0):
            return base + i * k, base // 2 + i * (k // 2), base % 2

        @block.scalar
        def _(act):
            def hi(base, i=0, k=0):
                num, half, par = at_chunk(base, i, k)
                if isinstance(num, int) and num >= NCH:
                    return
                act.wait_ge(landed[par], half * 16 + 16)
                if not isinstance(num, int) or num >= 2:
                    act.wait_ge(chunk_done, num - 1)
                nc.scalar.activation(wH[:, par, :], raw[:, par, :], ACT.Copy).then_inc(hi_ready, 1)

            def prep(norm, k):
                done = KT * norm + k
                if norm < 4:
                    act.wait_ge(xg_ready, done + 1)
                    nc.scalar.activation(xgH[:, k, :], xgt[:, k % 2, :], ACT.Copy).then_inc(xg_hi, 1)
                else:
                    act.wait_ge(x_upd, done + 1)
                if k == 0:
                    if norm:
                        act.wait_ge(stat_done, norm)
                elif k >= 3:
                    act.wait_ge(sq_sum, (KT - 1) * norm + k - 2)
                nc.scalar.activation(sqsum[:, :] if k == 0 else sq[:, k % 2, :], xT[:, k, :],
                                     ACT.Square).then_inc(sq_ready, 1)

            def root(norm):
                act.wait_ge(ms_ready, norm + 1)
                if norm == 0:
                    nc.scalar.activation(small[:, 68:68 + ST], small[:, 64:64 + ST], ACT.Sqrt)
                nc.scalar.activation(rinv[:, :], msq[:, :], ACT.Sqrt).then_inc(r_ready, 1)

            def attn_exp(layer, h):
                a = XH * layer + h
                act.wait_ge(mx_ready, a + 1)
                if a:
                    act.wait_ge(pt_done, a)
                for t in range(ST):
                    ins = nc.scalar.activation(prob[:, t, :], ps[:, 6 + t // 2, (t % 2) * M:(t % 2 + 1) * M], ACT.Exp,
                                               bias=small[:, 80 + t:81 + t], scale=XSCALE,
                                               accum_out=small[:, 84 + t:85 + t])
                ins.then_inc(p_exp, 1)

            def attn_pt(layer, h):
                a = XH * layer + h
                act.wait_ge(pt_done, a + 1)
                if a:
                    act.wait_ge(xo_done, a)
                nc.scalar.activation(probT[:, :, :], ps[:, 4:6, :], ACT.Copy).then_inc(pt_ready, 1)

            def attn_out(layer, h):
                a = XH * layer + h
                act.wait_ge(xo_done, a + 1)
                nc.scalar.activation(mixH[:, KT + h, :], ps[:, 4, :], ACT.Copy).then_inc(xo_hi, 1)

            for group, row, rows, n in vec_rows:
                act.dma_start(vrow[row:row + n, group, :], rows).then_inc(s_rows, 16)
            act.wait_ge(s_mem, 16)
            for t in range(MT):
                nc.scalar.activation(msc[:, t, :], mrow[:, t, :], ACT.Square,
                                     accum_out=small[:, t:t + 1]).then_inc(m_ss, 1)
            hi(0)
            hi(1)
            act.wait_ge(m_ms, 1)
            nc.scalar.activation(small[:, 4:4 + MT], small[:, 2:2 + MT], ACT.Sqrt).then_inc(m_inv, 1)
            for k in range(KT):
                act.wait_ge(m_g, k + 1)
                nc.scalar.activation(memH[:, k, :], mtmp[:, k % 2, :], ACT.Copy).then_inc(m_hi, 1)
            act.wait_ge(lbc, 3 + NLB)
            nc.scalar.activation(small[:, 16:16 + NLB * NH], small[:, 16:16 + NLB * NH], ACT.Exp).then_inc(lbe, 1)
            for c in range(2 * XH):
                hi(first["kv0"] + c + 2)
            for c in range(2 * XH):
                hi(first["kv1"] + c + 2)
                prep(0, c)

            for layer in range(2):
                n = first[f"xq{layer}"]
                for c in range(XH):
                    hi(n + c + 2)
                    if c == 0:
                        root(2 * layer)
                    act.wait_ge(tile_free, tile0[f"xq{layer}"] + c + 1)
                    bias = cst[:, (col["a_b"] + 4 * KT if layer == 0 else col["b_b"] + 2 * KT) + c:][:, 0:1]
                    nc.scalar.activation(xq[:, c, :], evt[:, c % 2, :], ACT.Identity, bias=bias).then_inc(xq_ready, 1)

                if layer == 0:
                    n = first["val"]
                    for h in range(XH):
                        attn_exp(0, h)
                        hi(n + 2 * h + 2)
                        attn_pt(0, h)
                        hi(n + 2 * h + 3)
                        attn_out(0, h)

                    def head_out(h):
                        act.wait_ge(o_done, h + 1)
                        nc.scalar.activation(osq[:, :], ps[:, 4, :], ACT.Square).then_inc(o_sq, 1)
                        act.wait_ge(o_ms, h + 1)
                        nc.scalar.activation(oinv[:, :], oinv[:, :], ACT.Sqrt).then_inc(o_inv, 1)

                    def head(b, i=0, k=0):
                        h, q = b + i * k, b % 2
                        if b >= 2:
                            head_out(h - 2)
                        for j, (func, dst, c) in enumerate(((ACT.Sigmoid, fb, 1), (ACT.Silu, qb, 0), (ACT.Silu, gb, 3))):
                            hi(first["head"] + 3 * b + j + 2, i, 3 * k)
                            if b >= 2 and j == 0:
                                act.wait_ge(lv_taken, (h - 1) * LV)
                            if b >= 2 and j == 2:
                                act.wait_ge(mix_lo, h - 1)
                            if j == 0:
                                act.wait_ge(hc_ready, h + 1)
                            act.wait_ge(tile_free, tile0["head"] + 3 * h + j + 1)
                            nc.scalar.activation(dst[:, q, :], evt[:, (b + j) % 2, :], func,
                                                 bias=hc[:, q, c:c + 1]).then_inc(h_act, 1)

                    head(0)
                    head(1)
                    with act.Fori(0, HEADS_LOOP) as i:
                        head(2, i, 2)
                        head(3, i, 2)
                else:
                    n = first["conv"]

                    def pair(b, i=0, k=0):
                        j, u = b + i * k, b % 2
                        if b < XH:
                            attn_exp(1, b)
                        hi(n + 2 * b + 2, i, 2 * k)
                        act.wait_ge(tile_free, tile0["conv"] + 2 * j + 1)
                        if b >= 2:
                            act.wait_ge(c_u, j - 1)
                        act.wait_ge(c_gate, j + 1)
                        nc.scalar.activation(gate[:, u, :], evt[:, 0, :], ACT.Sigmoid,
                                             bias=hcv[:, u, TAPS + 1:TAPS + 2]).then_inc(c_sig, 1)
                        if b < XH:
                            attn_pt(1, b)
                        hi(n + 2 * b + 3, i, 2 * k)
                        if b < XH:
                            attn_out(1, b)

                    for b in range(XH):
                        pair(b)
                    with act.Fori(0, (KT - XH) // 2) as i:
                        pair(XH, i, 2)
                        pair(XH + 1, i, 2)

                n = first[f"out{layer}"]
                NG = MIXT // 2
                for c in range(2 * NG):
                    if layer == 0 and c == 0:
                        head_out(NH - 2)
                    if layer == 0 and c == 3:
                        head_out(NH - 1)
                    hi(n + c + 2)
                    if layer == 1 and c == 1:
                        for k in range(KT):
                            act.wait_ge(c_cent, k + 1)
                            if k >= 2:
                                act.wait_ge(c_sq, k)
                                act.wait_ge(c_var, k - 1)
                            nc.scalar.activation(sq[:, k % 2, :], y[:, k, :], ACT.Square).then_inc(c_sq, 1)
                        act.wait_ge(c_norm, 1)
                        nc.scalar.activation(mu[:, :], msq[:, :], ACT.Sqrt).then_inc(c_act, 1)
                    if layer == 1 and 1 <= c <= 3:
                        for k in {1: range(0, 6), 2: range(6, 8), 3: range(0)}[c]:
                            act.wait_ge(c_norm, k + 2)
                            if k >= 2:
                                act.wait_ge(mix_lo, NH + k - 1)
                            nc.scalar.activation(evt[:, k % 2, :], xgt[:, k % 2, :], ACT.Silu,
                                                 scale=cst[:, col["lng"] + k:col["lng"] + k + 1],
                                                 bias=cst[:, col["lnb"] + k:col["lnb"] + k + 1]).then_inc(c_act, 1)
                            act.wait_ge(c_act, k + 2)
                            nc.scalar.activation(mixH[:, k, :], evt[:, k % 2, :], ACT.Copy).then_inc(mix_hi, 1)
                    for k in {NG - 1: (0, 1), NG: (2, 3), 2 * NG - 1: range(GT, KT)}.get(c, ()):
                        prep(2 * layer + 1, k)

                def ffn(b, i):
                    j = b + i
                    hi(first[f"gu{layer}"] + 2 * b + 2, i, 2)
                    if b == 0:
                        root(2 * layer + 1)
                    act.wait_ge(tile_free, tile0[f"gu{layer}"] + 2 * j + 1)
                    if b or layer:
                        act.wait_ge(act_step, 2 * (FT * layer + j) - 1)
                    nc.scalar.activation(xgt[:, 0, :], evt[:, 0, :], ACT.Silu).then_inc(silu_ready, 1)
                    hi(first[f"gu{layer}"] + 2 * b + 3, i, 2)

                ffn(0, 0)
                with act.Fori(0, FT - 1) as i:
                    ffn(1, i)

                n = first[f"down{layer}"]
                pairs = FT // 2
                norm = 2 * layer + 2
                with act.Fori(0, (pairs - 1) // 2) as i:
                    hi(n + 2, i, 2)
                    hi(n + 3, i, 2)
                hi(n + pairs - 1 + 2)
                prep(norm, 0)
                prep(norm, 1)
                hi(n + pairs + 2)
                prep(norm, 2)
                prep(norm, 3)
                with act.Fori(0, (pairs - 3) // 2) as i:
                    hi(n + pairs + 1 + 2, i, 2)
                    hi(n + pairs + 2 + 2, i, 2)
                hi(n + 2 * pairs)
                hi(n + 2 * pairs + 1)
                for k in range(GT, KT):
                    prep(norm, k)
            root(4)
            for k in range(KT):
                act.wait_ge(f_tr, k + 1)
                nc.scalar.activation(orow[:, :, k * P:(k + 1) * P], ps[:, 4 + k % 4, :].rearrange("p (t c) -> p t c", c=P),
                                     ACT.Copy).then_inc(f_row, 1)

        @block.vector
        def _(dve):
            V = nc.vector
            own = [0]

            def link(ins):
                own[0] += 1
                ins.then_inc(lbc, 1)
                dve.wait_ge(lbc, own[0])

            def lo(base, i=0, k=0):
                num, half, par = at_chunk(base, i, k)
                if isinstance(num, int) and num >= NCH:
                    return
                dve.wait_ge(hi_ready, num + 1)
                V.tensor_tensor(wL[:, par, :], raw[:, par, :], wH[:, par, :].bitcast(F32),
                                ALU.subtract).then_inc(lo_ready, 1)

            def gain(norm, k):
                done = KT * norm + k
                if norm == 4:
                    return
                name = ("mix0", "ffn0", "mix1", "ffn1")[norm]
                dve.wait_ge(x_upd, done + 1)
                if done >= 2:
                    dve.wait_ge(xg_hi, done - 1)
                    dve.wait_ge(xg_lo, done - 1)
                V.tensor_scalar(xgt[:, k % 2, :], xT[:, k, :], cst[:, col[name] + k:col[name] + k + 1], None,
                                ALU.mult).then_inc(xg_ready, 1)

            def gain_lo(norm, k):
                if norm == 4:
                    return
                dve.wait_ge(xg_hi, KT * norm + k + 1)
                V.tensor_tensor(xgL[:, k, :], xgt[:, k % 2, :], xgH[:, k, :].bitcast(F32),
                                ALU.subtract).then_inc(xg_lo, 1)

            def renew(norm, ks):
                for k in ks:
                    V.tensor_tensor(xT[:, k, :], ps[:, k, :], xT[:, k, :], ALU.add).then_inc(x_upd, 1)
                    gain(norm, k)
                    if k > ks[0]:
                        gain_lo(norm, k - 1)
                gain_lo(norm, ks[-1])

            def mean_square(norm):
                dve.wait_ge(stat_done, norm + 1)
                if norm == 0:
                    link(V.tensor_scalar(small[:, 64:64 + ST], ps[:, 3, 0:ST], 1.0 / D, EPS, ALU.mult, ALU.add))
                    V.reciprocal(small[:, 64:64 + ST], small[:, 64:64 + ST])
                link(V.tensor_scalar(msq[:, :], ps[:, 2, :], 1.0 / D, EPS, ALU.mult, ALU.add))
                V.reciprocal(msq[:, :], msq[:, :]).then_inc(ms_ready, 1)

            def scaled(par):
                return V.tensor_tensor(evt[:, par, :], ps[:, par, :], rinv[:, :], ALU.mult)

            def attn_max(layer, h):
                a = XH * layer + h
                dve.wait_ge(sc_done, a + 1)
                link(V.reduce_max(small[:, 88:88 + ST], ps[:, 6:8, :].rearrange("p b (t m) -> p (b t) m", m=M), AX_X))
                V.tensor_scalar(small[:, 80:80 + ST], small[:, 88:88 + ST], -XSCALE, None,
                                ALU.mult).then_inc(mx_ready, 1)

            def attn_norm(layer, h):
                a = XH * layer + h
                dve.wait_ge(p_exp, a + 1)
                link(V.reciprocal(small[:, 92:92 + ST], small[:, 84:84 + ST]))
                V.tensor_tensor(prob[:, :, :], prob[:, :, :],
                                small[:, 92:92 + ST].unsqueeze(2).broadcast_to([P, ST, M]),
                                ALU.mult).then_inc(p_norm, 1)

            def attn_lo(layer, h):
                a = XH * layer + h
                dve.wait_ge(xo_hi, a + 1)
                V.tensor_tensor(mixL[:, KT + h, :], ps[:, 4, :], mixH[:, KT + h, :].bitcast(F32),
                                ALU.subtract).then_inc(xo_lo, 1)

            dve.wait_ge(m_ss, MT)
            link(V.tensor_scalar(small[:, 2:2 + MT], small[:, 0:MT], 1.0 / D, EPS, ALU.mult, ALU.add))
            V.reciprocal(small[:, 2:2 + MT], small[:, 2:2 + MT]).then_inc(m_ms, 1)
            dve.wait_ge(s_tr, 1)
            V.tensor_copy(cst[:, :], ps[:, 3, 0:NCOL]).then_inc(s_cst, 1)
            dve.wait_ge(m_inv, 1)
            for t in range(MT):
                V.tensor_scalar(mrow[:, t, :], mrow[:, t, :], small[:, 4 + t:5 + t], None, ALU.mult).then_inc(m_row, 1)
            lo(0)
            lo(1)
            dve.wait_ge(s_cst, 1)
            for k in range(KT):
                dve.wait_ge(m_tr, k + 1)
                if k >= 2:
                    dve.wait_ge(m_lo, k - 1)
                V.tensor_scalar(mtmp[:, k % 2, :], ps[:, 4 + k % 4, 0:M], cst[:, col["mem"] + k:col["mem"] + k + 1],
                                None, ALU.mult).then_inc(m_g, 1)
                dve.wait_ge(m_hi, k + 1)
                V.tensor_tensor(memL[:, k, :], mtmp[:, k % 2, :], memH[:, k, :].bitcast(F32),
                                ALU.subtract).then_inc(m_lo, 1)
            table = [cst[:, col[f"lb{r}"]:col[f"lb{r}"] + NH] for r in range(NLB)]
            shifted = small[:, 16:16 + NLB * NH].rearrange("p (r h) -> p r h", h=NH)
            top = small[:, 8:8 + NH]
            link(V.tensor_tensor(top, table[0], table[1], ALU.max))
            link(V.tensor_tensor(top, top, table[2], ALU.max))
            for r in range(NLB):
                link(V.tensor_tensor(shifted[:, r, :], table[r], top, ALU.subtract))
            dve.wait_ge(lbe, 1)
            link(V.tensor_tensor(top, shifted[:, 0, :], shifted[:, 1, :], ALU.add))
            link(V.tensor_tensor(top, top, shifted[:, 2, :], ALU.add))
            link(V.reciprocal(top, top))
            link(V.tensor_tensor(headc[:, 4, :], shifted[:, 0, :], top, ALU.mult))
            link(V.tensor_scalar(headc[:, 5, :], headc[:, 4, :], -1.0, 1.0, ALU.mult, ALU.add))
            link(V.tensor_copy(headc[:, 0:4, :], cst[:, col["a_b"]:col["a_b"] + 4 * NH].rearrange("p (k h) -> p k h", h=NH)))

            for layer in range(2):
                for c in range(2 * XH):
                    n = first[f"kv{layer}"] + c
                    lo(n + 2)
                    dve.wait_ge(chunk_done, n + 1)
                    if c < XH:
                        V.tensor_copy(KTs[layer][:, c, :], ps[:, c % 2, 0:M]).then_inc(tile_free, 1)
                    elif c == 2 * XH - 1:
                        V.tensor_copy(VMs[layer][:, :, :], ps[:, 4:4 + MT, :]).then_inc(kv_done, 1)
                    if layer == 1:
                        dve.wait_ge(x_tr, c + 1)
                        V.tensor_copy(xT[:, c, :], ps[:, 2 + c % 2, :]).then_inc(x_upd, 1)
                        gain(0, c)
                        gain_lo(0, c)

            for layer in range(2):
                n = first[f"xq{layer}"]
                for c in range(XH):
                    lo(n + c + 2)
                    if c == 0:
                        mean_square(2 * layer)
                        dve.wait_ge(r_ready, 2 * layer + 1)
                        if layer:
                            dve.wait_ge(silu_ready, FT)
                    if c >= 2:
                        dve.wait_ge(xq_ready, XH * layer + c - 1)
                    dve.wait_ge(chunk_done, n + c + 1)
                    scaled(c % 2).then_inc(tile_free, 1)

                if layer == 0:
                    n = first["val"]
                    dve.wait_ge(s_vb, 16)
                    for h in range(XH):
                        attn_max(0, h)
                        attn_norm(0, h)
                        lo(n + 2 * h + 2)
                        lo(n + 2 * h + 3)
                        c = 2 * h + 1
                        if c % GT == GT - 1:
                            dve.wait_ge(chunk_done, n + c + 1)
                            for t in range(ST):
                                V.scalar_tensor_tensor(out=val[:, t, 512 * (c // GT):512 * (c // GT + 1)], in0=ps[:, t, :],
                                                       scalar=small[:, 68 + t:69 + t],
                                                       in1=vbias[:, 512 * (c // GT):512 * (c // GT + 1)],
                                                       op0=ALU.mult, op1=ALU.add).then_inc(v_done, 1)
                        attn_lo(0, h)

                    def sums(lv):
                        o = sum(S >> m for m in range(1, lv))
                        return tb[:, o:o + (S >> lv)]

                    def level(lv, h, q):
                        if lv == 0:
                            dve.wait_ge(s_zero, 1)
                        else:
                            dve.wait_ge(lv_taken, h * LV + lv)
                        dve.wait_ge(lv_done, h * LV + lv + 1)
                        A, B = qb[:, q, :], kb[:, q, :]
                        if lv == 0:
                            V.tensor_tensor(A, A, fb[:, q, :], ALU.mult).then_inc(lv_ready, 1)
                        elif lv <= 8:
                            L = 1 << (lv - 1)
                            nb = S // (2 * L)
                            T = (fb[:, q, :] if lv == 1 else sums(lv - 1)).rearrange("p (n two) -> p n two", two=2)
                            Ao = A.rearrange("p (n two l) -> p n two l", two=2, l=L)[:, :, 1, :]
                            Be = B.rearrange("p (n two l) -> p n two l", two=2, l=L)[:, :, 0, :]
                            V.tensor_tensor(Ao, Ao, T[:, :, 0:1].broadcast_to([P, nb, L]), ALU.mult)
                            ins = V.tensor_tensor(Be, Be, T[:, :, 1:2].broadcast_to([P, nb, L]), ALU.mult)
                            if lv <= 7:
                                ins = V.tensor_tensor(sums(lv), T[:, :, 0], T[:, :, 1], ALU.mult)
                            ins.then_inc(lv_ready, 1)
                        bank = ps[:, 6 + lv % 2, :]
                        if lv < MASKED:
                            V.copy_predicated(att_view(0, ST * P + P, ST), mask[:, lv, :].bitcast(U32).unsqueeze(1).broadcast_to([P, ST, P]),
                                              bank.rearrange("p (b t) -> p b t", t=P)).then_inc(lv_taken, 1)
                        elif lv == MASKED:
                            V.tensor_copy(att_view(P, 2 * (S + P), 2), bank[:, 0:2 * P].rearrange("p (b t) -> p b t", t=P)).then_inc(lv_taken, 1)
                        else:
                            V.tensor_copy(att[:, 0:2, 2 * P:4 * P], bank.rearrange("p (b t) -> p b t", t=2 * P)).then_inc(lv_taken, 1)

                    def att_view(offset, step, count):
                        return bass.AP(tensor=att[:, :, :].tensor, offset=offset, ap=[[ST * S, P], [step, count], [1, P]])

                    def out_ms(h):
                        dve.wait_ge(o_stat, h + 1)
                        V.tensor_scalar(oinv[:, :], ps[:, 5, :], 1.0 / P, EPS, ALU.mult, ALU.add).then_inc(o_step, 1)
                        dve.wait_ge(o_step, 4 * h + 1)
                        V.reciprocal(oinv[:, :], oinv[:, :]).then_inc(o_ms, 1)

                    def out_split(h, q):
                        dve.wait_ge(o_inv, h + 1)
                        V.tensor_tensor(mixt[:, :], ps[:, 4, :], oinv[:, :], ALU.mult).then_inc(o_step, 1)
                        dve.wait_ge(o_step, 4 * h + 2)
                        V.scalar_tensor_tensor(out=mixt[:, :], in0=mixt[:, :], scalar=cst[:, col["a_on"]:col["a_on"] + 1],
                                               in1=gb[:, q, :], op0=ALU.mult, op1=ALU.mult).then_inc(o_step, 1)
                        dve.wait_ge(o_step, 4 * h + 3)
                        V.tensor_scalar(mixH[:, bass.ds(h, 1), :], mixt[:, :].unsqueeze(1), 1.0, None, ALU.mult).then_inc(o_step, 1)
                        dve.wait_ge(o_step, 4 * h + 4)
                        V.tensor_tensor(mixL[:, bass.ds(h, 1), :], mixt[:, :].unsqueeze(1),
                                        mixH[:, bass.ds(h, 1), :].bitcast(F32), ALU.subtract).then_inc(mix_lo, 1)

                    def head(b, i=0, k=0):
                        h, q = b + i * k, b % 2
                        if b >= 2:
                            dve.wait_ge(h_act, 3 * h - 3)
                        V.tensor_scalar(hc[:, q, :].unsqueeze(2), headc[:, :, bass.ds(h, 1)], 1.0, None, ALU.mult).then_inc(hc_ready, 1)
                        if b == 0:
                            dve.wait_ge(xq_ready, XH)
                            dve.wait_ge(v_done, 2 * ST)
                        for j in range(3):
                            for lv in range(4 * j, min(4 * j + 4, LV)) if b else ():
                                level(lv, h - 1, 1 - q)
                                if b >= 2 and lv == 0:
                                    out_ms(h - 2)
                                if b >= 2 and lv == 2:
                                    out_split(h - 2, q)
                                if lv == 5:
                                    forget(h, q)
                            lo(first["head"] + 3 * b + j + 2, i, 3 * k)
                            if 3 * b + j >= 2:
                                dve.wait_ge(h_act, 3 * h + j - 1)
                            dve.wait_ge(chunk_done, first["head"] + 3 * h + j + 1)
                            scaled((b + j) % 2).then_inc(tile_free, 1)
                            if b == 0 and j == 1:
                                forget(h, q)
                        V.tensor_scalar(vh[:, q, :, :], val[:, :, bass.ds(h * P, P)], 1.0, None, ALU.mult).then_inc(k_ready, 1)

                    def forget(h, q):
                        dve.wait_ge(hc_ready, h + 1)
                        dve.wait_ge(h_act, 3 * h + 1)
                        V.tensor_scalar(fb[:, q, :], fb[:, q, :], hc[:, q, 5:6], hc[:, q, 4:5], ALU.mult, ALU.add).then_inc(t_ready, 1)
                        dve.wait_ge(t_ready, h + 1)
                        V.tensor_scalar(kb[:, q, :], fb[:, q, :], -1.0, 1.0, ALU.mult, ALU.add)

                    head(0)
                    head(1)
                    with dve.Fori(0, HEADS_LOOP) as i:
                        head(2, i, 2)
                        head(3, i, 2)
                else:
                    n = first["conv"]

                    def pair(b, i=0, k=0):
                        j, u = b + i * k, b % 2
                        if b >= 2:
                            dve.wait_ge(c_sig, j - 1)
                            dve.wait_ge(c_y, j - 1)
                        for dst, src in ((hcv[:, u, 0:TAPS].unsqueeze(2),
                                          cst[:, col["dw"]:col["dw"] + TAPS * KT].rearrange("p (t k) -> p t k", k=KT)[:, :, bass.ds(j, 1)]),
                                         (hcv[:, u, TAPS:TAPS + 1], cst[:, bass.ds(col["b_b"] + j, 1)]),
                                         (hcv[:, u, TAPS + 1:TAPS + 2], cst[:, bass.ds(col["b_b"] + KT + j, 1)]),
                                         (hcv[:, u, TAPS + 2:TAPS + 3], cst[:, bass.ds(col["dwb"] + j, 1)])):
                            ins = V.tensor_scalar(dst, src, 1.0, None, ALU.mult)
                        ins.then_inc(c_gate, 1)
                        if b < XH:
                            attn_max(1, b)
                        if b == 0:
                            dve.wait_ge(xq_ready, 2 * XH)
                            dve.wait_ge(s_zero, 2)
                        else:
                            dve.wait_ge(c_sig, j)
                        dve.wait_ge(chunk_done, n + 2 * j + 1)
                        scaled(0).then_inc(tile_free, 1)
                        if b < XH:
                            attn_norm(1, b)
                        if b:
                            dve.wait_ge(c_u, j)
                        dve.wait_ge(chunk_done, n + 2 * j + 2)
                        scaled(1).then_inc(tile_free, 1)
                        dve.wait_ge(c_gate, j + 1)
                        dve.wait_ge(c_sig, j + 1)
                        dve.wait_ge(tile_free, tile0["conv"] + 2 * j + 2)
                        V.scalar_tensor_tensor(out=upad[:, u, PAD:PAD + S], in0=evt[:, 1, :], scalar=hcv[:, u, TAPS:TAPS + 1],
                                               in1=gate[:, u, :], op0=ALU.add, op1=ALU.mult).then_inc(c_u, 1)
                        dve.wait_ge(c_u, j + 1)
                        dst = y[:, bass.ds(j, 1), :]
                        V.tensor_scalar(dst, upad[:, u, 0:S].unsqueeze(1), hcv[:, u, 0:1], hcv[:, u, TAPS + 2:TAPS + 3],
                                        ALU.mult, ALU.add).then_inc(c_tap, 1)
                        for t in range(1, TAPS):
                            dve.wait_ge(c_tap, j * (TAPS - 1) + t)
                            V.scalar_tensor_tensor(out=dst, in0=upad[:, u, t:t + S].unsqueeze(1), scalar=hcv[:, u, t:t + 1], in1=dst,
                                                   op0=ALU.mult, op1=ALU.add).then_inc(c_tap if t < TAPS - 1 else c_y, 1)
                        if b < XH:
                            attn_lo(1, b)

                    for b in range(XH):
                        pair(b)
                    with dve.Fori(0, (KT - XH) // 2) as i:
                        pair(XH, i, 2)
                        pair(XH + 1, i, 2)

                n = first[f"out{layer}"]
                NG = MIXT // 2
                for c in range(2 * NG):
                    if layer == 0 and c < 3:
                        for lv in range(4 * c, min(4 * c + 4, LV)):
                            level(lv, NH - 1, (NH - 1) % 2)
                            if lv == 0:
                                out_ms(NH - 2)
                            if lv == 2:
                                out_split(NH - 2, NH % 2)
                    if layer == 0 and c == 3:
                        out_ms(NH - 1)
                        out_split(NH - 1, (NH - 1) % 2)
                    if layer == 1 and c == 0:
                        dve.wait_ge(lo_ready, n + c + 2)
                    lo(n + c + 2)
                    if layer == 1 and c == 1:
                        dve.wait_ge(c_mu, 1)
                        link(V.tensor_scalar(mu[:, :], ps[:, 4, :], 1.0 / D, None, ALU.mult))
                        for k in range(KT):
                            V.tensor_tensor(y[:, k, :], y[:, k, :], mu[:, :], ALU.subtract).then_inc(c_cent, 1)
                        dve.wait_ge(c_var, KT)
                        link(V.tensor_scalar(msq[:, :], ps[:, 5, :], 1.0 / D, EPS, ALU.mult, ALU.add))
                        V.reciprocal(msq[:, :], msq[:, :]).then_inc(c_norm, 1)
                        dve.wait_ge(c_act, 1)
                    if layer == 1 and 1 <= c <= 2:
                        for k in {1: range(0, 6), 2: range(6, 8)}[c]:
                            if k >= 2:
                                dve.wait_ge(c_act, k)
                            V.tensor_tensor(xgt[:, k % 2, :], y[:, k, :], mu[:, :], ALU.mult).then_inc(c_norm, 1)
                            if k >= 1:
                                dve.wait_ge(mix_hi, k)
                                V.tensor_tensor(mixL[:, k - 1, :], evt[:, (k - 1) % 2, :], mixH[:, k - 1, :].bitcast(F32),
                                                ALU.subtract).then_inc(mix_lo, 1)
                        if c == 2:
                            dve.wait_ge(mix_hi, KT)
                            V.tensor_tensor(mixL[:, KT - 1, :], evt[:, (KT - 1) % 2, :], mixH[:, KT - 1, :].bitcast(F32),
                                            ALU.subtract).then_inc(mix_lo, 1)
                    ks = {NG - 1: (0, 1), NG: (2, 3), 2 * NG - 1: tuple(range(GT, KT))}.get(c)
                    if ks:
                        dve.wait_ge(chunk_done, n + c + 1 if c != NG else n + NG)
                        renew(2 * layer + 1, ks)

                def ffn(b, i):
                    j = b + i
                    m = FT * layer + j
                    lo(first[f"gu{layer}"] + 2 * b + 2, i, 2)
                    if b == 0:
                        mean_square(2 * layer + 1)
                        dve.wait_ge(r_ready, 2 * layer + 2)
                        if layer == 0:
                            dve.wait_ge(h_act, 3 * NH)
                        else:
                            dve.wait_ge(mix_hi, KT)
                    else:
                        dve.wait_ge(silu_ready, m)
                    dve.wait_ge(chunk_done, first[f"gu{layer}"] + 2 * j + 1)
                    scaled(0).then_inc(tile_free, 1)
                    lo(first[f"gu{layer}"] + 2 * b + 3, i, 2)
                    dve.wait_ge(chunk_done, first[f"gu{layer}"] + 2 * j + 2)
                    scaled(1).then_inc(tile_free, 1)
                    dve.wait_ge(silu_ready, m + 1)
                    dve.wait_ge(tile_free, tile0[f"gu{layer}"] + 2 * j + 2)
                    V.tensor_tensor(xgt[:, 1, :], evt[:, 1, :], xgt[:, 0, :], ALU.mult).then_inc(act_step, 1)
                    dve.wait_ge(act_step, 2 * m + 1)
                    V.tensor_scalar(actH[:, bass.ds(j, 1), :], xgt[:, 1, :].unsqueeze(1), 1.0, None, ALU.mult).then_inc(act_step, 1)
                    dve.wait_ge(act_step, 2 * m + 2)
                    V.tensor_tensor(actL[:, bass.ds(j, 1), :], xgt[:, 1, :].unsqueeze(1), actH[:, bass.ds(j, 1), :].bitcast(F32),
                                    ALU.subtract).then_inc(act_lo, 1)
                    dve.wait_ge(act_lo, m + 1)

                ffn(0, 0)
                with dve.Fori(0, FT - 1) as i:
                    ffn(1, i)

                n = first[f"down{layer}"]
                pairs = FT // 2
                norm = 2 * layer + 2
                with dve.Fori(0, (pairs - 1) // 2) as i:
                    lo(n + 2, i, 2)
                    lo(n + 3, i, 2)
                lo(n + pairs - 1 + 2)
                dve.wait_ge(chunk_done, n + pairs)
                renew(norm, (0, 1))
                lo(n + pairs + 2)
                renew(norm, (2, 3))
                with dve.Fori(0, (pairs - 3) // 2) as i:
                    lo(n + pairs + 1 + 2, i, 2)
                    lo(n + pairs + 2 + 2, i, 2)
                lo(n + 2 * pairs)
                lo(n + 2 * pairs + 1)
                dve.wait_ge(chunk_done, n + 2 * pairs)
                renew(norm, tuple(range(GT, KT)))
            mean_square(4)
            dve.wait_ge(r_ready, 5)
            for k in range(KT):
                V.scalar_tensor_tensor(out=yT[:, k, :], in0=xT[:, k, :], scalar=cst[:, col["fin"] + k:col["fin"] + k + 1],
                                       in1=rinv[:, :], op0=ALU.mult, op1=ALU.mult).then_inc(f_y, 1)

        @block.tensor
        def _(pe):
            mm = nc.tensor.matmul

            def exact(out_ap, left, right, start, stop):
                mm(out_ap, left[0], right[0], start=start, stop=False)
                mm(out_ap, left[0], right[1], start=False, stop=False)
                return mm(out_ap, left[1], right[0], start=False, stop=stop)

            def tile_chunk(base, number, i=0, k=0, other=None, width=S, enter=None, between=None, ready=None):
                num, half, par = at_chunk(base, i, k)
                H, L = other or (xgH, xgL)
                if not isinstance(number, int) or number >= 2:
                    pe.wait_ge(tile_free, number - 1)
                pe.wait_ge(lo_ready, num + 1)
                for kt in range(KT):
                    if ready is not None:
                        pe.wait_ge(xg_lo, KT * ready + kt + 1)
                    w = slice(kt * P, (kt + 1) * P)
                    ins = exact(ps[:, par, 0:width], (wH[:, par, w], wL[:, par, w]), (H[:, kt, :], L[:, kt, :]),
                                kt == 0, kt == KT - 1)
                    if kt == KT - 1:
                        ins.then_inc(chunk_done, 1)
                    if between is not None:
                        between(kt)

            def group_chunk(base, bank, acts, start, stop, i=0, k=0, between=None):
                num, half, par = at_chunk(base, i, k)
                pe.wait_ge(lo_ready, num + 1)
                for kk in range(2):
                    right = acts(kk)
                    for t in range(GT):
                        w = slice(kk * 512 + t * P, kk * 512 + (t + 1) * P)
                        ins = exact(ps[:, bank + t, :], (wH[:, par, w], wL[:, par, w]), right,
                                    start and kk == 0, stop and kk == 1)
                        if kk == 1 and t == GT - 1:
                            ins.then_inc(chunk_done, 1)
                        if between is not None and t % 2:
                            between(2 * kk + t // 2)

            def stat(norm):
                pe.wait_ge(sq_sum, (KT - 1) * (norm + 1))
                if norm == 0:
                    for t in range(ST):
                        mm(ps[:, 3, t:t + 1], sqsum[:, t * P:(t + 1) * P], ones[:, 0:1], start=True, stop=True)
                mm(ps[:, 2, :], ones[:, :], sqsum[:, :], start=True, stop=True).then_inc(stat_done, 1)

            def attn_scores(layer, h):
                a = XH * layer + h
                pe.wait_ge(xq_ready, a + 1)
                if a:
                    pe.wait_ge(p_norm, a)
                for t in range(ST):
                    ins = mm(ps[:, 6 + t // 2, (t % 2) * M:(t % 2 + 1) * M], xq[:, h, t * P:(t + 1) * P], KTs[layer][:, h, :],
                             start=True, stop=True)
                ins.then_inc(sc_done, 1)

            def attn_turn(layer, h):
                a = XH * layer + h
                pe.wait_ge(p_norm, a + 1)
                if a:
                    pe.wait_ge(xo_lo, a)
                for m in range(MT):
                    for t in range(ST):
                        ins = nc.tensor.transpose(ps[:, 4 + m, t * P:(t + 1) * P], prob[:, t, m * P:(m + 1) * P], ident[:, :])
                ins.then_inc(pt_done, 1)

            def attn_values(layer, h):
                a = XH * layer + h
                pe.wait_ge(pt_ready, a + 1)
                for m in range(MT):
                    ins = mm(ps[:, 4, :], VMs[layer][:, m, h * P:(h + 1) * P], probT[:, m, :], start=(m == 0), stop=(m == MT - 1))
                ins.then_inc(xo_done, 1)

            pe.wait_ge(s_const, 1)
            pe.wait_ge(s_rows, 16 * len(vec_rows))
            o = 0
            for g, n in enumerate(rows_in):
                ins = nc.tensor.transpose(ps[:, 3, o:o + n], vrow[0:n, g, :], ident[0:n, 0:n])
                o += n
            ins.then_inc(s_tr, 1)
            pe.wait_ge(m_row, MT)
            for k in range(KT):
                if k >= 4:
                    pe.wait_ge(m_g, k - 3)
                for t in range(MT):
                    ins = nc.tensor.transpose(ps[:, 4 + k % 4, t * P:(t + 1) * P], mrow[:, t, k * P:(k + 1) * P], ident[:, :])
                ins.then_inc(m_tr, 1)
            pe.wait_ge(m_lo, KT)
            for layer in range(2):
                n = first[f"kv{layer}"]
                for c in range(2 * XH):
                    if layer == 1:
                        if c == 0:
                            pe.wait_ge(s_x, 16 * ST)
                            pe.wait_ge(s_cst, 1)
                        if c >= 2:
                            pe.wait_ge(x_upd, c - 1)
                        for t in range(ST):
                            ins = nc.tensor.transpose(ps[:, 2 + c % 2, t * P:(t + 1) * P], xrow[:, t, c * P:(c + 1) * P], ident[:, :])
                        ins.then_inc(x_tr, 1)
                    if c < XH:
                        tile_chunk(n + c, tile0[f"kv{layer}"] + c, other=(memH, memL), width=M)
                    else:
                        pe.wait_ge(lo_ready, n + c + 1)
                        if c == XH and layer:
                            pe.wait_ge(kv_done, layer)
                        for kk in range(2):
                            k = 2 * (c - XH) + kk
                            par = c % 2
                            w = slice(kk * 512, (kk + 1) * 512)
                            for t in range(MT):
                                f = slice(t * P, (t + 1) * P)
                                ins = exact(ps[:, 4 + t, :], (memH[:, k, f], memL[:, k, f]), (wH[:, par, w], wL[:, par, w]),
                                            k == 0, k == KT - 1)
                        ins.then_inc(chunk_done, 1)

            for layer in range(2):
                n = first[f"xq{layer}"]
                for c in range(XH):
                    tile_chunk(n + c, tile0[f"xq{layer}"] + c, ready=2 * layer if c == 0 else None)
                    if c == 0:
                        stat(2 * layer)
                if layer == 0:
                    n = first["val"]
                    pe.wait_ge(tile_free, tile0["head"])
                    pe.wait_ge(ms_ready, 1)
                    pe.wait_ge(kv_done, 2)
                    for c in range(2 * GT):
                        if c % 2 == 0:
                            attn_scores(0, c // 2)
                        else:
                            attn_turn(0, c // 2)
                        if c == GT:
                            pe.wait_ge(v_done, ST)
                        pe.wait_ge(lo_ready, n + c + 1)
                        par = c % 2
                        for kk in range(2):
                            k = 2 * (c % GT) + kk
                            w = slice(kk * 512, (kk + 1) * 512)
                            for t in range(ST):
                                f = slice(t * P, (t + 1) * P)
                                ins = exact(ps[:, t, :], (xgH[:, k, f], xgL[:, k, f]), (wH[:, par, w], wL[:, par, w]),
                                            k == 0, k == KT - 1)
                        ins.then_inc(chunk_done, 1)
                        if c % 2:
                            attn_values(0, c // 2)
                    pe.wait_ge(v_done, 2 * ST)
                    pe.wait_ge(xo_lo, XH)

                    def level(lv, h, q, first_head):
                        if lv == 0:
                            pe.wait_ge(k_ready, h + 1)
                            pe.wait_ge(h_act, 3 * h + 2)
                            if not first_head:
                                pe.wait_ge(lv_taken, h * LV)
                        else:
                            pe.wait_ge(lv_ready, h * (LV - 1) + lv)
                        bank = ps[:, 6 + lv % 2, :]
                        A, B = qb[:, q, :], kb[:, q, :]
                        if lv < MASKED:
                            for b in range(ST):
                                f = slice(b * P, (b + 1) * P)
                                ins = mm(bank[:, f], B[:, f], A[:, f], start=True, stop=True)
                        elif lv == MASKED:
                            for b in range(2):
                                ins = mm(bank[:, b * P:(b + 1) * P], B[:, 2 * b * P:(2 * b + 1) * P],
                                         A[:, (2 * b + 1) * P:(2 * b + 2) * P], start=True, stop=True)
                        else:
                            for b in range(2):
                                ins = mm(bank[:, 2 * b * P:2 * (b + 1) * P], B[:, b * P:(b + 1) * P], A[:, 2 * P:4 * P],
                                         start=True, stop=True)
                        ins.then_inc(lv_done, 1)

                    def head_values(h, q, first_head):
                        pe.wait_ge(lv_taken, (h + 1) * LV)
                        if not first_head:
                            pe.wait_ge(mix_lo, h)
                        for t in range(ST):
                            ins = mm(ps[:, 4, t * P:S], vh[:, q, t, :], att[:, t, t * P:S], start=(t == 0), stop=(t == ST - 1))
                        ins.then_inc(o_done, 1)

                    def head_stat(h, first_head):
                        pe.wait_ge(o_sq, h + 1)
                        if not first_head:
                            pe.wait_ge(o_ms, h)
                        mm(ps[:, 5, :], ones[:, :], osq[:, :], start=True, stop=True).then_inc(o_stat, 1)

                    def places(place, h, b):
                        if b >= 2 and place == 0:
                            head_stat(h - 2, b == 2 and isinstance(h, int))
                        if b >= 1 and place < LV:
                            level(place, h - 1, 1 - b % 2, b == 1)
                        if b >= 1 and place == 11:
                            head_values(h - 1, 1 - b % 2, b == 1)

                    def head(b, i=0, k=0):
                        h = b + i * k
                        for j in range(3):
                            tile_chunk(first["head"] + 3 * b + j, tile0["head"] + 3 * h + j, i, 3 * k,
                                       between=lambda kt: places(4 * j + kt // 2, h, b) if kt % 2 else None)

                    head(0)
                    head(1)
                    with pe.Fori(0, HEADS_LOOP) as i:
                        head(2, i, 2)
                        head(3, i, 2)
                else:
                    n = first["conv"]

                    def pair(b, i=0, k=0):
                        j = b + i * k
                        for side in range(2):
                            if b < XH:
                                (attn_turn if side else attn_scores)(1, b)
                            tile_chunk(n + 2 * b + side, tile0["conv"] + 2 * j + side, i, 2 * k)
                        if b < XH:
                            attn_values(1, b)

                    for b in range(XH):
                        pair(b)
                    with pe.Fori(0, (KT - XH) // 2) as i:
                        pair(XH, i, 2)
                        pair(XH + 1, i, 2)

                n = first[f"out{layer}"]
                NG = MIXT // 2
                pe.wait_ge(tile_free, tile0[f"gu{layer}"])
                for c, (g, kp) in enumerate(out_order[layer]):
                    if kp >= KT // 2:
                        pe.wait_ge(xo_lo, XH * layer + 2 * (kp - KT // 2) + 2)
                    else:
                        pe.wait_ge(mix_lo, NH * layer + 2 * kp + 2)
                    beside = None
                    if layer == 0 and c < 3:
                        beside = lambda p: places(4 * c + p, NH, NH)
                    if layer == 0 and c == 3:
                        beside = lambda p: head_stat(NH - 1, False) if p == 0 else None
                    group_chunk(n + c, GT * g, lambda kk: (mixH[:, 2 * kp + kk, :], mixL[:, 2 * kp + kk, :]),
                                c % NG == 0, c % NG == NG - 1, between=beside)
                    if layer == 1 and c == 1:
                        pe.wait_ge(c_pool, KT - 1)
                        mm(ps[:, 4, :], ones[:, :], mu[:, :], start=True, stop=True).then_inc(c_mu, 1)
                        for k in range(KT):
                            pe.wait_ge(c_sq, k + 1)
                            mm(ps[:, 5, :], ones[:, :], sq[:, k % 2, :], start=(k == 0), stop=(k == KT - 1)).then_inc(c_var, 1)

                n = first[f"gu{layer}"]
                t0 = tile0[f"gu{layer}"]
                tile_chunk(n, t0, ready=2 * layer + 1)
                stat(2 * layer + 1)
                tile_chunk(n + 1, t0 + 1)
                with pe.Fori(0, FT - 1) as i:
                    tile_chunk(n + 2, t0 + 2 + 2 * i, i, 2)
                    tile_chunk(n + 3, t0 + 3 + 2 * i, i, 2)

                n = first[f"down{layer}"]
                pairs = FT // 2

                def hidden(kp):
                    return lambda kk: (actH[:, kp * 2 + kk, :], actL[:, kp * 2 + kk, :])

                def hidden_at(base, i):
                    return lambda kk: tuple(a[:, bass.ds(i * 4 + base + kk, 1), :].rearrange("p a s -> p (a s)") for a in (actH, actL))

                pe.wait_ge(tile_free, t0 + 2 * FT)
                pe.wait_ge(act_lo, FT * layer + FT - 1)
                group_chunk(n, 0, hidden(0), True, False)
                pe.wait_ge(act_lo, FT * layer + FT)
                group_chunk(n + 1, 0, hidden(1), False, False)
                with pe.Fori(0, (pairs - 3) // 2) as i:
                    group_chunk(n + 2, 0, hidden_at(4, i), False, False, i, 2)
                    group_chunk(n + 3, 0, hidden_at(6, i), False, False, i, 2)
                group_chunk(n + pairs - 1, 0, hidden(pairs - 1), False, True)
                group_chunk(n + pairs, GT, hidden(0), True, False)
                with pe.Fori(0, (pairs - 3) // 2) as i:
                    group_chunk(n + pairs + 1, GT, hidden_at(2, i), False, False, i, 2)
                    group_chunk(n + pairs + 2, GT, hidden_at(4, i), False, False, i, 2)
                group_chunk(n + 2 * pairs - 2, GT, hidden(pairs - 2), False, False)
                group_chunk(n + 2 * pairs - 1, GT, hidden(pairs - 1), False, True)
            stat(4)
            for k in range(KT):
                if k == 0:
                    pe.wait_ge(x_upd, 5 * KT)
                if k >= 4:
                    pe.wait_ge(f_row, k - 3)
                pe.wait_ge(f_y, k + 1)
                for t in range(ST):
                    ins = nc.tensor.transpose(ps[:, 4 + k % 4, t * P:(t + 1) * P], yT[:, k, t * P:(t + 1) * P], ident[:, :])
                ins.then_inc(f_tr, 1)


_INS = ["x", "mem", "norm_mix_g", "norm_ffn_g", "w_out", "xattn_w_kv", "ffn_w_gu", "ffn_w_down", "mem_norm_g",
        "final_norm_g", "a_w_in", "a_b_in", "a_lb_table", "a_onorm_g", "b_w_in", "b_b_in", "b_dw_w", "b_dw_b",
        "b_ln_g", "b_ln_b"]


def kernel(**inputs):
    import numpy as np
    import concourse.bacc as bacc
    from concourse.bass_utils import run_bass_kernel_spmd

    nc = bacc.Bacc("TRN2", target_bir_lowering=False, num_devices=1)
    arrays, args = {}, []
    for name in _INS:
        a = np.ascontiguousarray(inputs[name])
        arrays[f"in_{name}"] = a
        args.append(nc.dram_tensor(f"in_{name}", a.shape, mybir.dt.from_np(a.dtype), kind="ExternalInput").ap())
    shape = np.asarray(inputs["x"]).shape
    args.append(nc.dram_tensor("out_0", shape, F32, kind="ExternalOutput").ap())
    trunk(nc, *args)
    r = run_bass_kernel_spmd(nc, [arrays], core_ids=[0])
    return r.results[0]["out_0"]
```

```python
from contextlib import ExitStack

import concourse.bass as bass
from concourse import mybir

F32 = mybir.dt.float32
F32R = mybir.dt.float32r
U32 = mybir.dt.uint32
ALU = mybir.AluOpType
ACT = mybir.ActivationFunctionType
AX_X = mybir.AxisListType.X

P = 128
EPS = 1e-6
CHUNK = 1024


def trunk(nc, x, mem, g_mix, g_ffn, w_out, w_kv, w_gu, w_down, g_mem, g_fin,
          a_w, a_b, a_lb, a_on, b_w, b_b, b_dw, b_dwb, b_lng, b_lnb, out):
    S, D = x.shape[1], x.shape[2]
    M = mem.shape[1]
    KT = D // P
    ST = S // P
    MT = M // P
    XH = 4
    XW = XH * P
    NH = D // P
    FH = w_down.shape[1]
    FT = FH // P
    MIXT = KT + XH
    TAPS = b_dw.shape[1]
    PAD = TAPS - 1
    NLB = a_lb.shape[0]
    GT = 4
    LV = 10
    MASKED = 8
    XSCALE = float(P) ** -0.5

    extra = [[(kv, k), ("q", c), (kv, k + 1)] for kv, k, c in (("K", 0, 0), ("K", 2, 1), ("V", 0, 2), ("V", 2, 3))]
    extra += [[]] * (KT - XH)
    rounds, pos = [], 0
    for r in range(KT):
        kinds = [("gate", r), ("value", r)] + extra[r]
        rounds.append([(pos + i, kind, c) for i, (kind, c) in enumerate(kinds)])
        pos += len(kinds)
    MID = KT // 2
    centre = [[]] * 5 + [[0, 1], [2, 3, 4], [5, 6]]
    pe_taps = [4, 3, 3, 3, 7, 8, 8, 8]
    sizes = [("kv0", 2 * XH), ("xq0", XH), ("val", 2 * GT), ("head", 3 * NH),
             ("out0", MIXT), ("gu0", 2 * FT), ("down0", FT),
             ("mix1", pos), ("out1", MIXT), ("gu1", 2 * FT), ("down1", FT)]
    first, NCH = {}, 0
    for name, n in sizes:
        first[name] = NCH
        NCH += n
    tile0, nt = {}, 0
    for name, n in (("kv0", XH), ("xq0", XH), ("head", 3 * NH), ("gu0", 2 * FT),
                    ("mix1", 2 * KT), ("gu1", 2 * FT)):
        tile0[name] = nt
        nt += n
    X_PAIRS = list(range(KT // 2, MIXT // 2))
    M_PAIRS = list(range(KT // 2))
    out_order = [[(g, k) for g in range(2) for k in X_PAIRS + M_PAIRS],
                 [(0, k) for k in X_PAIRS + M_PAIRS] + [(1, k) for k in X_PAIRS + M_PAIRS]]

    vec_rows, col, at = [], {}, 0
    for name, ap in (("mix0", g_mix[0]), ("mix1", g_mix[1]), ("ffn0", g_ffn[0]), ("ffn1", g_ffn[1]),
                     ("mem", g_mem), ("fin", g_fin), ("a_b", a_b[0]), ("lb0", a_lb[0]), ("lb1", a_lb[1]),
                     ("lb2", a_lb[2]), ("a_on", a_on[0])):
        n = ap.shape[0] // P
        vec_rows.append((0, at, ap.rearrange("(r c) -> r c", c=P), n))
        col[name] = at
        at += n
    rows_in = [at]
    base = at
    at = 0
    for name, ap in (("b_b", b_b[0]), ("dwb", b_dwb[0]), ("lng", b_lng[0]), ("lnb", b_lnb[0])):
        n = ap.shape[0] // P
        vec_rows.append((1, at, ap.rearrange("(r c) -> r c", c=P), n))
        col[name] = base + at
        at += n
    rows_in.append(at)
    base += at
    dw_rows = b_dw[0].rearrange("t (r c) -> (t r) c", c=P)
    half = TAPS * KT // 2
    for g in range(2):
        vec_rows.append((2 + g, 0, dw_rows[g * half:(g + 1) * half], half))
        rows_in.append(half)
    col["dw"] = base
    NCOL = base + 2 * half

    with ExitStack() as ctx:
        where = [nc.sbuf_base + (-nc.sbuf_base) % 64]

        def place(name, shape, dt=F32, at=None):
            size = 4
            for n in shape[1:]:
                size *= n
            at = at and at + (-at) % 32
            if at is None:
                at = where[0]
                where[0] += size + (-size) % 32
            return nc.alloc_sbuf_tensor_at(name, shape, dt, offset=at)

        def sem(name):
            return ctx.enter_context(nc.semaphore(name))

        ident = place("ident", [P, P])
        ones = place("ones", [P, P])
        at_mask = where[0]
        mask = place("mask", [P, MASKED, P])
        cst = place("cst", [P, NCOL])
        headc = place("headc", [P, 6, NH])
        hc = place("hc", [P, 2, 6])
        small = place("small", [P, 128])
        xT = place("xT", [P, KT, S])
        at_xg = where[0]
        xgH = place("xgH", [P, KT, S], F32R)
        xgL = place("xgL", [P, KT, S], F32R)
        raw = place("raw", [P, 2, CHUNK])
        wH = place("wH", [P, 2, CHUNK], F32R)
        wL = place("wL", [P, 2, CHUNK], F32R)
        rinv = place("rinv", [P, S])
        msq = place("msq", [P, S])
        sqsum = place("sqsum", [P, S])
        sq = place("sq", [P, 2, S])
        xgt = place("xgt", [P, 2, S])
        evt = place("evt", [P, 2, S])
        at_kv = where[0]
        KTs = [place("memK0", [P, XH, M])]
        VMs = [place("memV0", [P, MT, XW])]
        KTs.append(place("memK1", [P, XH, M], at=at_kv))
        VMs.append(place("memV1", [P, MT, XW], at=at_kv + 4 * XH * M))
        memN = place("memN", [P, KT, M])
        arena = where[0]
        actH = place("actH", [P, FT, S], F32R, at=arena)
        actL = place("actL", [P, FT, S], F32R, at=arena + 4 * FT * S)
        mixH = place("mixH", [P, MIXT, S], F32R)
        mixL = place("mixL", [P, MIXT, S], F32R)
        at_val = where[0]
        val = place("val", [P, ST, D])
        at_heads = where[0]
        qb = place("qb", [P, 2, S])
        fb = place("fb", [P, 2, S])
        kb = place("kb", [P, 2, S])
        gb = place("gb", [P, 2, S])
        at_tail = where[0]
        tb = place("tb", [P, S])
        vh = place("vh", [P, 2, ST, P])
        osq = place("osq", [P, S])
        oinv = place("oinv", [P, S])
        mixt = place("mixt", [P, S])
        att = place("att", [P, ST, S], at=at_kv)
        vbias = place("vbias", [P, D], at=at_tail)
        xq = place("xq", [P, XH, S], at=at_heads)
        prob = place("prob", [P, ST, M], at=at_heads + 4 * XH * S)
        probT = place("probT", [P, MT, S], at=at_heads + 4 * XH * S + 4 * ST * M)
        memH = place("memH", [P, KT, M], F32R, at=arena)
        memL = place("memL", [P, KT, M], F32R, at=arena + 4 * KT * M)
        mrow = place("mrow", [P, MT, D], at=arena + 8 * KT * M)
        xrow = place("xrow", [P, ST, D], at=arena + 8 * KT * M + 4 * MT * D)
        vrow = place("vrow", [P, 4, P], at=arena + 8 * KT * M + 4 * MT * D + 4 * ST * D)
        msc = place("msc", [P, MT, D], at=at_val)
        y = place("y", [P, KT, S], at=at_val)
        PU = PAD + S + 2
        upad = place("upad", [P, PU], at=at_tail)
        upH = place("upH", [P, PU], F32R, at=at_tail + 4 * PU)
        upL = place("upL", [P, PU], F32R, at=at_tail + 8 * PU)
        gate = place("gate", [P, S], at=at_tail + 12 * PU)
        mu = place("mu", [P, S], at=at_tail + 12 * PU + 4 * S)
        NTE = max(pe_taps)
        ysum = mu
        y2 = place("y2", [P, S], at=at_mask)
        rsd = place("rsd", [P, S], at=at_mask)
        mid = place("mid", [P, S], at=at_mask + 4 * S)
        at_mixL = arena + 4 * MIXT * S
        assert 16 * NTE * P <= 4 * KT * S
        dgH = place("dgH", [P, 2, NTE, P], F32R, at=at_mixL)
        dgL = place("dgL", [P, 2, NTE, P], F32R, at=at_mixL + 8 * NTE * P)
        dwh = place("dwh", [P, TAPS * KT], F32R, at=at_tail + 12 * PU + 8 * S)
        dwl = place("dwl", [P, TAPS * KT])
        orow = place("orow", [P, ST, D], at=at_val)
        yT = place("yT", [P, KT, S], at=at_xg)
        assert max(where[0], arena + 8 * FT * S) <= nc.sbuf_usable_end, (where, nc.sbuf_usable_end)

        ps = ctx.enter_context(nc.psum_tensor("ps", [P, 8, 512], F32))

        landed = [sem("landed0"), sem("landed1")]
        hi_ready = sem("hi_ready")
        lo_ready = sem("lo_ready")
        chunk_done = sem("chunk_done")
        tile_free = sem("tile_free")
        s_rows, s_mem, s_x, s_vb = sem("s_rows"), sem("s_mem"), sem("s_x"), sem("s_vb")
        s_const, s_zero, s_pool = sem("s_const"), sem("s_zero"), sem("s_pool")
        s_tr, s_cst = sem("s_tr"), sem("s_cst")
        m_ss, m_ms, m_inv, m_row = sem("m_ss"), sem("m_ms"), sem("m_inv"), sem("m_row")
        m_tr, m_g, m_hi, m_lo = sem("m_tr"), sem("m_g"), sem("m_hi"), sem("m_lo")
        lbc = sem("lbc")
        lbe = sem("lbe")
        x_tr = sem("x_tr")
        kv_done = sem("kv_done")
        x_upd = sem("x_upd")
        xg_ready, xg_hi, xg_lo = sem("xg_ready"), sem("xg_hi"), sem("xg_lo")
        sq_ready, sq_sum = sem("sq_ready"), sem("sq_sum")
        stat_done = sem("stat_done")
        ms_ready = sem("ms_ready")
        r_ready = sem("r_ready")
        xq_ready = sem("xq_ready")
        sc_done, mx_ready, p_exp, p_norm = sem("sc_done"), sem("mx_ready"), sem("p_exp"), sem("p_norm")
        p_inv = sem("p_inv")
        pt_done, pt_ready, xo_done, xo_hi, xo_lo = (sem("pt_done"), sem("pt_ready"), sem("xo_done"),
                                                    sem("xo_hi"), sem("xo_lo"))
        v_done = sem("v_done")
        hc_ready = sem("hc_ready")
        h_act = sem("h_act")
        k_ready = sem("k_ready")
        lv_ready, lv_done, lv_taken = sem("lv_ready"), sem("lv_done"), sem("lv_taken")
        t_ready = sem("t_ready")
        o_done, o_sq, o_stat, o_ms, o_inv = sem("o_done"), sem("o_sq"), sem("o_stat"), sem("o_ms"), sem("o_inv")
        o_step = sem("o_step")
        mix_lo = sem("mix_lo")
        mix_hi = sem("mix_hi")
        silu_ready = sem("silu_ready")
        act_step, act_lo = sem("act_step"), sem("act_lo")
        c_sig, c_u, c_uhi, c_ulo, c_tap, c_y = (sem("c_sig"), sem("c_u"), sem("c_uhi"), sem("c_ulo"), sem("c_tap"),
                                                sem("c_y"))
        c_dw, c_diag, c_pe = sem("c_dw"), sem("c_diag"), sem("c_pe")
        k_free, q_free = sem("k_free"), sem("q_free")
        c_sum = sem("c_sum")
        c_mid_pe, c_mid = sem("c_mid_pe"), sem("c_mid")
        c_cent, c_sq, c_sqs = sem("c_cent"), sem("c_sq"), sem("c_sqs")
        c_mu, c_var, c_less = sem("c_mu"), sem("c_var"), sem("c_less")
        c_act, c_norm = sem("c_act"), sem("c_norm")
        f_y, f_tr, f_row, f_row2, s_out = sem("f_y"), sem("f_tr"), sem("f_row"), sem("f_row2"), sem("s_out")

        block = ctx.enter_context(nc.Block())

        HEADS_LOOP = (NH - 2) // 2

        def square_slot(k):
            return (sq if k % 4 < 2 else xgt)[:, k % 2, :]

        def tap_bank(r):
            return 7 if r == KT - 1 else 2 + r % 2

        def at_chunk(base, i=0, k=0):
            return base + i * k, base // 2 + i * (k // 2), base % 2

        @block.sync
        def _(sp):
            def fetch(n, source, shape):
                num, par = n
                if not isinstance(source.offset, int):
                    sp.lower_val(source.offset * 4)
                if not (isinstance(num, int) and num < 2):
                    sp.wait_ge(lo_ready, num - 1)
                sp.dma_start(raw[:, par, :].rearrange("p (k c) -> p k c", c=shape), source).then_inc(landed[par], 16)

            def columns(w, c0):
                return w.rearrange("(k p) c -> p k c", p=P)[:, :, bass.ds(c0, P)]

            def rows(w, k0, c0):
                return w.rearrange("(k p) c -> p k c", p=P)[:, bass.ds(k0, 2), c0:c0 + 512]

            sp.dma_start(mrow[:, :, :], mem[0].rearrange("(t p) d -> p t d", p=P)).then_inc(s_mem, 16)
            for c in range(2 * XH):
                n = first["kv0"] + c
                if c < XH:
                    fetch((n, n % 2), columns(w_kv[0], c * P), P)
                else:
                    fetch((n, n % 2), rows(w_kv[0], 2 * (c - XH), XW), 512)
                if n == 1:
                    for t in range(ST):
                        sp.dma_start(xrow[:, t, :], x[0, t * P:(t + 1) * P, :]).then_inc(s_x, 16)
                    sp.dma_start(vbias[:, :], a_b[0:1, 2 * D:3 * D].partition_broadcast(P)[:, 0, :]).then_inc(s_vb, 16)
            for layer in range(2):
                if layer == 0:
                    n = first["xq0"]
                    for c in range(XH):
                        fetch((n + c, c % 2), columns(a_w[0], 4 * D + c * P), P)
                    n = first["val"]
                    for c in range(2 * GT):
                        fetch((n + c, c % 2), rows(a_w[0], 2 * (c % GT), 2 * D + 512 * (c // GT)), 512)
                    n = first["head"]
                    with sp.Fori(0, NH // 2) as i:
                        for h in range(2):
                            for j, kind in enumerate((1, 0, 3)):
                                c = 3 * h + j
                                fetch((n + c + i * 6, c % 2), columns(a_w[0], kind * D + h * P + i * (2 * P)), P)
                else:
                    for r in range(KT):
                        for pos, kind, c in rounds[r]:
                            n = first["mix1"] + pos
                            if kind == "V":
                                fetch((n, n % 2), rows(w_kv[1], 2 * c, XW), 512)
                            elif kind == "K":
                                fetch((n, n % 2), columns(w_kv[1], c * P), P)
                            else:
                                fetch((n, n % 2), columns(b_w[0], {"gate": D, "value": 0, "q": 2 * D}[kind] + c * P), P)
                n = first[f"out{layer}"]
                for c, (g, k) in enumerate(out_order[layer]):
                    fetch((n + c, c % 2), rows(w_out[layer], 2 * k, 512 * g), 512)
                n = first[f"gu{layer}"]
                with sp.Fori(0, FT) as i:
                    for j in range(2):
                        fetch((n + j + i * 2, j), columns(w_gu[layer], j * FH + i * P), P)
                n = first[f"down{layer}"]
                pairs = FT // 2
                with sp.Fori(0, (pairs - 1) // 2) as i:
                    for j in range(2):
                        fetch((n + j + i * 2, j), rows(w_down[layer], (2 * j) + i * 4, 0), 512)
                fetch((n + pairs - 1, 0), rows(w_down[layer], 2 * (pairs - 1), 0), 512)
                fetch((n + pairs, 1), rows(w_down[layer], 0, 512), 512)
                with sp.Fori(0, (pairs - 1) // 2) as i:
                    for j in range(2):
                        fetch((n + pairs + 1 + j + i * 2, j), rows(w_down[layer], 2 + (2 * j) + i * 4, 512), 512)
            for t in range(ST):
                sp.wait_ge(f_row, t + 1)
                sp.wait_ge(f_row2, t + 1)
                sp.dma_start(out[0, t * P:(t + 1) * P, :], orow[:, t, :]).then_inc(s_out, 16)
            sp.wait_ge(s_out, 16 * ST)

        @block.gpsimd
        def _(pool):
            step = [0]

            def link(ins):
                step[0] += 1
                ins.then_inc(s_pool, 1)
                pool.wait_ge(s_pool, step[0])

            link(nc.gpsimd.memset(ident[:, :], 1.0))
            link(nc.gpsimd.affine_select(out=ident[:, :], in_=ident[:, :], compare_op=ALU.is_equal, fill=0.0,
                                         base=0, pattern=[[-1, P]], channel_multiplier=1))
            nc.gpsimd.memset(ones[:, :], 1.0).then_inc(s_const, 1)
            link(nc.gpsimd.memset(mask[:, :, :], 0.0))
            link(nc.gpsimd.tensor_copy(mask[:, 0, :], ident[:, :]))
            for lv in range(1, MASKED):
                L = 1 << (lv - 1)
                nb = P // (2 * L)
                odd = mask[:, lv, :].rearrange("p (n two l) -> p n two l", two=2, l=L)[:, :, 1, :]
                link(nc.gpsimd.memset(odd, 1.0))
                link(nc.gpsimd.affine_select(out=odd, in_=odd, compare_op=ALU.is_ge, fill=0.0, base=0,
                                             pattern=[[-2 * L, nb], [0, L]], channel_multiplier=1))
                link(nc.gpsimd.affine_select(out=odd, in_=odd, compare_op=ALU.is_ge, fill=0.0, base=L - 1,
                                             pattern=[[2 * L, nb], [0, L]], channel_multiplier=-1))
            nc.gpsimd.memset(small[:, 127:128], 0.0).then_inc(s_const, 1)

            def sum_squares(norm, k0, k1):
                for k in range(max(k0, 1), k1):
                    pool.wait_ge(sq_ready, KT * norm + k + 1)
                    if k > 1:
                        pool.wait_ge(sq_sum, (KT - 1) * norm + k - 1)
                    nc.gpsimd.tensor_tensor(sqsum[:, :], sqsum[:, :], sq[:, k % 2, :], ALU.add).then_inc(sq_sum, 1)

            def lo(base, i=0, k=0):
                num, half, par = at_chunk(base, i, k)
                pool.wait_ge(hi_ready, num + 1)
                nc.gpsimd.tensor_tensor(wL[:, par, :], raw[:, par, :], wH[:, par, :].bitcast(F32),
                                        ALU.subtract).then_inc(lo_ready, 1)

            sum_squares(0, 0, KT)
            pool.wait_ge(xo_lo, XH)
            pool.wait_ge(xo_done, XH)
            nc.gpsimd.memset(att[:, :, :], 0.0).then_inc(s_zero, 1)
            n = first["head"]
            pool.wait_ge(lo_ready, n + 2)
            with pool.Fori(0, 3 * NH // 2) as i:
                lo(n + 2, i, 2)
                lo(n + 3, i, 2)
            sum_squares(1, 0, KT)
            sum_squares(2, 0, KT)
            for m in range(0, KT, KT // 2):
                pool.wait_ge(m_hi, KT + m + KT // 2)
                nc.gpsimd.tensor_tensor(memL[:, m:m + KT // 2, :], memN[:, m:m + KT // 2, :],
                                        memH[:, m:m + KT // 2, :].bitcast(F32), ALU.subtract).then_inc(m_lo, KT // 2)
            nc.gpsimd.memset(upad[:, 0:PAD], 0.0)
            nc.gpsimd.memset(upad[:, PAD + S:PU], 0.0).then_inc(s_zero, 1)
            pool.wait_ge(lo_ready, first["mix1"] + 2)
            pool.wait_ge(c_dw, 1)

            def sum_tile(k):
                pool.wait_ge(c_y, k + 1)
                if k > 1:
                    pool.wait_ge(c_sum, k - 1)
                nc.gpsimd.tensor_tensor(ysum[:, :], (y[:, 0, :] if k == 1 else ysum[:, :]), y[:, k, :],
                                        ALU.add).then_inc(c_sum, 1)

            def centre_tile(k):
                pool.wait_ge(c_mid, 1)
                pool.wait_ge(c_sum, k)
                nc.gpsimd.tensor_tensor(y[:, k, :], y[:, k, :], mid[:, :], ALU.subtract).then_inc(c_cent, 1)

            def square_sum(k):
                pool.wait_ge(c_sq, k + 1)
                if k > 1:
                    pool.wait_ge(c_sqs, k - 1)
                nc.gpsimd.tensor_tensor(sqsum[:, :], (square_slot(0) if k == 1 else sqsum[:, :]), square_slot(k),
                                        ALU.add).then_inc(c_sqs, 1)

            def diagonals(r):
                if r >= 2:
                    pool.wait_ge(c_pe, r - 1)
                n = pe_taps[r]
                for dg, weights, at in ((dgH, cst, col["dw"]), (dgL, dwl, 0)):
                    w = weights[:, at:at + TAPS * KT].rearrange("p (t k) -> p t k", k=KT)[:, TAPS - n:, r:r + 1]
                    ins = nc.gpsimd.tensor_tensor(dg[:, r % 2, 0:n, :], ident[:, :].unsqueeze(1).broadcast_to([P, n, P]),
                                                  w.broadcast_to([P, n, P]), ALU.mult)
                ins.then_inc(c_diag, 1)

            diagonals(0)
            for r in range(KT):
                for pos, kind, c in rounds[r]:
                    lo(first["mix1"] + pos + 2)
                    if kind == "gate":
                        for k in (centre[r - 1] if r else []):
                            if k:
                                square_sum(k)
                        if r == KT - 1:
                            centre_tile(centre[r][0])
                        else:
                            for k in centre[r]:
                                centre_tile(k)
                            diagonals(r + 1)
                        if r >= 2:
                            sum_tile(r - 1)
                        if r == KT - 1:
                            for k in centre[r][1:]:
                                centre_tile(k)
                pool.wait_ge(c_uhi, r + 1)
                if r:
                    pool.wait_ge(c_pe, r)
                nc.gpsimd.tensor_tensor(upL[:, :], upad[:, :], upH[:, :].bitcast(F32), ALU.subtract).then_inc(c_ulo, 1)
            for k in centre[KT - 1]:
                square_sum(k)
            sum_squares(3, 0, KT)
            sum_squares(4, 0, KT)

        @block.scalar
        def _(act):
            def hi(base, i=0, k=0):
                num, half, par = at_chunk(base, i, k)
                if isinstance(num, int) and num >= NCH:
                    return
                act.wait_ge(landed[par], half * 16 + 16)
                if not isinstance(num, int) or num >= 2:
                    act.wait_ge(chunk_done, num - 1)
                nc.scalar.activation(wH[:, par, :], raw[:, par, :], ACT.Copy).then_inc(hi_ready, 1)

            def prep(norm, k):
                done = KT * norm + k
                if norm < 4:
                    act.wait_ge(xg_ready, done + 1)
                    nc.scalar.activation(xgH[:, k, :], xgt[:, k % 2, :], ACT.Copy).then_inc(xg_hi, 1)
                else:
                    act.wait_ge(x_upd, done + 1)
                if k == 0:
                    if norm:
                        act.wait_ge(stat_done, norm)
                elif k >= 3:
                    act.wait_ge(sq_sum, (KT - 1) * norm + k - 2)
                nc.scalar.activation(sqsum[:, :] if k == 0 else sq[:, k % 2, :], xT[:, k, :],
                                     ACT.Square).then_inc(sq_ready, 1)

            def root(norm):
                act.wait_ge(ms_ready, norm + 1)
                if norm in (0, 4):
                    ins = nc.scalar.activation(small[:, 68:68 + ST], small[:, 64:64 + ST], ACT.Sqrt)
                if norm == 4:
                    ins.then_inc(r_ready, 1)
                    return
                nc.scalar.activation(rinv[:, :], msq[:, :], ACT.Sqrt).then_inc(r_ready, 1)

            def attn_exp(layer, h):
                a = XH * layer + h
                act.wait_ge(mx_ready, a + 1)
                if a:
                    act.wait_ge(pt_done, a)
                for t in range(ST):
                    ins = nc.scalar.activation(prob[:, t, :], ps[:, 6 + t // 2, (t % 2) * M:(t % 2 + 1) * M], ACT.Exp,
                                               bias=small[:, 80 + t:81 + t], scale=XSCALE,
                                               accum_out=small[:, 84 + t:85 + t])
                ins.then_inc(p_exp, 1)
                if layer:
                    act.wait_ge(p_inv, h + 1)
                    for t in range(ST):
                        ins = nc.scalar.activation(prob[:, t, :], prob[:, t, :], ACT.Copy, scale=small[:, 92 + t:93 + t])
                    ins.then_inc(p_norm, 1)

            def attn_pt(layer, h):
                a = XH * layer + h
                act.wait_ge(pt_done, a + 1)
                if a:
                    act.wait_ge(xo_done, a)
                nc.scalar.activation(probT[:, :, :], ps[:, 4:6, :], ACT.Copy).then_inc(pt_ready, 1)

            def attn_out(layer, h):
                a = XH * layer + h
                act.wait_ge(xo_done, a + 1)
                nc.scalar.activation(mixH[:, KT + h, :], ps[:, 4, :], ACT.Copy).then_inc(xo_hi, 1)

            for group, row, rows, n in vec_rows:
                act.dma_start(vrow[row:row + n, group, :], rows).then_inc(s_rows, 16)
            act.wait_ge(s_mem, 16)
            for t in range(MT):
                nc.scalar.activation(msc[:, t, :], mrow[:, t, :], ACT.Square,
                                     accum_out=small[:, t:t + 1]).then_inc(m_ss, 1)
            hi(0)
            hi(1)
            act.wait_ge(m_ms, 1)
            nc.scalar.activation(small[:, 4:4 + MT], small[:, 2:2 + MT], ACT.Sqrt).then_inc(m_inv, 1)
            for k in range(KT):
                act.wait_ge(m_g, k + 1)
                nc.scalar.activation(memH[:, k, :], memN[:, k, :], ACT.Copy).then_inc(m_hi, 1)
            act.wait_ge(lbc, 3 + NLB)
            nc.scalar.activation(small[:, 16:16 + NLB * NH], small[:, 16:16 + NLB * NH], ACT.Exp).then_inc(lbe, 1)
            for c in range(2 * XH):
                hi(first["kv0"] + c + 2)
                prep(0, c)

            for layer in range(2):
                if layer == 0:
                    n = first["xq0"]
                    for c in range(XH):
                        hi(n + c + 2)
                        if c == 0:
                            root(0)
                        act.wait_ge(tile_free, tile0["xq0"] + c + 1)
                        b = col["a_b"] + 4 * KT + c
                        nc.scalar.activation(xq[:, c, :], evt[:, c % 2, :], ACT.Identity, bias=cst[:, b:b + 1]).then_inc(xq_ready, 1)
                    n = first["val"]
                    for h in range(XH):
                        attn_exp(0, h)
                        hi(n + 2 * h + 2)
                        attn_pt(0, h)
                        hi(n + 2 * h + 3)
                        attn_out(0, h)

                    def head_out(h):
                        act.wait_ge(o_done, h + 1)
                        nc.scalar.activation(osq[:, :], ps[:, 4, :], ACT.Square).then_inc(o_sq, 1)
                        act.wait_ge(o_ms, h + 1)
                        nc.scalar.activation(oinv[:, :], oinv[:, :], ACT.Sqrt).then_inc(o_inv, 1)

                    def head(b, i=0, k=0):
                        h, q = b + i * k, b % 2
                        if b >= 2:
                            head_out(h - 2)
                        for j, (func, dst, c) in enumerate(((ACT.Sigmoid, fb, 1), (ACT.Silu, qb, 0), (ACT.Silu, gb, 3))):
                            hi(first["head"] + 3 * b + j + 2, i, 3 * k)
                            if b >= 2 and j == 0:
                                act.wait_ge(lv_taken, (h - 1) * LV)
                            if b >= 2 and j == 2:
                                act.wait_ge(mix_lo, h - 1)
                            if j == 0:
                                act.wait_ge(hc_ready, h + 1)
                            act.wait_ge(tile_free, tile0["head"] + 3 * h + j + 1)
                            nc.scalar.activation(dst[:, q, :], evt[:, (b + j) % 2, :], func,
                                                 bias=hc[:, q, c:c + 1]).then_inc(h_act, 1)

                    head(0)
                    head(1)
                    with act.Fori(0, HEADS_LOOP) as i:
                        head(2, i, 2)
                        head(3, i, 2)
                else:
                    def query_bias(c):
                        act.wait_ge(q_free, c + 1)
                        b = col["b_b"] + 2 * KT + c
                        nc.scalar.activation(xq[:, c, :], xgt[:, c % 2, :], ACT.Identity, bias=cst[:, b:b + 1]).then_inc(xq_ready, 1)

                    def square(k):
                        act.wait_ge(c_cent, k + 1)
                        if k >= 4:
                            act.wait_ge(c_sqs, max(k - 4, 1))
                        nc.scalar.activation(square_slot(k), y[:, k, :], ACT.Square).then_inc(c_sq, 1)

                    for r in range(KT):
                        for pos, kind, c in rounds[r]:
                            hi(first["mix1"] + pos + 2)
                            if kind == "gate" and r > XH:
                                attn_pt(1, r - XH - 1)
                            if kind == "K":
                                act.wait_ge(chunk_done, first["mix1"] + pos + 1)
                                nc.scalar.activation(KTs[1][:, c, :], ps[:, 6, 0:M], ACT.Copy).then_inc(k_free, 1)
                            if kind == "V" and c == XH - 1:
                                act.wait_ge(chunk_done, first["mix1"] + pos + 1)
                                nc.scalar.activation(VMs[1][:, :, :], ps[:, 4:4 + MT, :], ACT.Copy).then_inc(kv_done, 1)
                            if kind == "value":
                                if r == 0:
                                    root(2)
                                act.wait_ge(tile_free, tile0["mix1"] + 2 * r + 1)
                                if r:
                                    act.wait_ge(c_u, r)
                                b = col["b_b"] + KT + r
                                nc.scalar.activation(gate[:, :], evt[:, 0, :], ACT.Sigmoid, bias=cst[:, b:b + 1]).then_inc(c_sig, 1)
                                if 1 <= r <= XH:
                                    query_bias(r - 1)
                                act.wait_ge(c_u, r + 1)
                                if r:
                                    act.wait_ge(c_pe, r)
                                nc.scalar.activation(upH[:, :], upad[:, :], ACT.Copy).then_inc(c_uhi, 1)
                                if r > XH:
                                    attn_out(1, r - XH - 1)
                                if r >= XH:
                                    attn_exp(1, r - XH)
                                if r == XH:
                                    act.wait_ge(c_mid_pe, 1)
                                    nc.scalar.activation(mid[:, :], ps[:, 5, :], ACT.Copy, scale=1.0 / (MID * P)).then_inc(c_mid, 1)
                                for k in centre[r]:
                                    square(k)

                n = first[f"out{layer}"]
                NG = MIXT // 2
                for c in range(2 * NG):
                    if layer == 0 and c == 0:
                        head_out(NH - 2)
                    if layer == 0 and c == 3:
                        head_out(NH - 1)
                    hi(n + c + 2)
                    if layer == 1 and c == 0:
                        attn_pt(1, XH - 1)
                        square(KT - 1)
                        attn_out(1, XH - 1)
                    if layer == 1 and c == 1:
                        act.wait_ge(c_norm, 1)
                        nc.scalar.activation(rsd[:, :], msq[:, :], ACT.Sqrt).then_inc(c_act, 1)
                    if layer == 1 and 1 <= c <= 3:
                        for k in {1: range(0, 6), 2: range(6, 8), 3: range(0)}[c]:
                            act.wait_ge(c_norm, k + 2)
                            if k >= 2:
                                act.wait_ge(mix_lo, NH + k - 1)
                            nc.scalar.activation(evt[:, k % 2, :], xgt[:, k % 2, :], ACT.Silu,
                                                 scale=cst[:, col["lng"] + k:col["lng"] + k + 1],
                                                 bias=cst[:, col["lnb"] + k:col["lnb"] + k + 1]).then_inc(c_act, 1)
                            act.wait_ge(c_act, k + 2)
                            nc.scalar.activation(mixH[:, k, :], evt[:, k % 2, :], ACT.Copy).then_inc(mix_hi, 1)
                    for k in {NG - 1: (0, 1), NG: (2, 3), 2 * NG - 1: range(GT, KT)}.get(c, ()):
                        prep(2 * layer + 1, k)

                def ffn(b, i):
                    j = b + i
                    hi(first[f"gu{layer}"] + 2 * b + 2, i, 2)
                    if b == 0:
                        root(2 * layer + 1)
                    act.wait_ge(tile_free, tile0[f"gu{layer}"] + 2 * j + 1)
                    if b or layer:
                        act.wait_ge(act_step, 2 * (FT * layer + j) - 1)
                    nc.scalar.activation(xgt[:, 0, :], evt[:, 0, :], ACT.Silu).then_inc(silu_ready, 1)
                    hi(first[f"gu{layer}"] + 2 * b + 3, i, 2)

                ffn(0, 0)
                with act.Fori(0, FT - 1) as i:
                    ffn(1, i)

                n = first[f"down{layer}"]
                pairs = FT // 2
                norm = 2 * layer + 2
                with act.Fori(0, (pairs - 1) // 2) as i:
                    hi(n + 2, i, 2)
                    hi(n + 3, i, 2)
                hi(n + pairs - 1 + 2)
                prep(norm, 0)
                prep(norm, 1)
                hi(n + pairs + 2)
                prep(norm, 2)
                prep(norm, 3)
                with act.Fori(0, (pairs - 3) // 2) as i:
                    hi(n + pairs + 1 + 2, i, 2)
                    hi(n + pairs + 2 + 2, i, 2)
                hi(n + 2 * pairs)
                hi(n + 2 * pairs + 1)
                for k in range(GT, KT):
                    prep(norm, k)
                if layer == 0:
                    for m in range(0, KT, KT // 2):
                        nc.scalar.activation(memH[:, m:m + KT // 2, :], memN[:, m:m + KT // 2, :],
                                             ACT.Copy).then_inc(m_hi, KT // 2)
            root(4)
            act.wait_ge(r_ready, 5)
            for t in range(ST):
                act.wait_ge(f_tr, KT)
                nc.scalar.activation(orow[:, t, GT * P:].rearrange("p (k c) -> p k c", c=P), ps[:, GT:KT, t * P:(t + 1) * P],
                                     ACT.Copy, scale=small[:, 68 + t:69 + t]).then_inc(f_row2, 1)

        @block.vector
        def _(dve):
            V = nc.vector
            own = [0]

            def link(ins):
                own[0] += 1
                ins.then_inc(lbc, 1)
                dve.wait_ge(lbc, own[0])

            def lo(base, i=0, k=0):
                num, half, par = at_chunk(base, i, k)
                if isinstance(num, int) and num >= NCH:
                    return
                dve.wait_ge(hi_ready, num + 1)
                V.tensor_tensor(wL[:, par, :], raw[:, par, :], wH[:, par, :].bitcast(F32),
                                ALU.subtract).then_inc(lo_ready, 1)

            def gain(norm, k):
                done = KT * norm + k
                if norm == 4:
                    dve.wait_ge(x_upd, done + 1)
                    V.tensor_scalar(yT[:, k, :], xT[:, k, :], cst[:, col["fin"] + k:col["fin"] + k + 1], None,
                                    ALU.mult).then_inc(f_y, 1)
                    return
                name = ("mix0", "ffn0", "mix1", "ffn1")[norm]
                dve.wait_ge(x_upd, done + 1)
                if done >= 2:
                    dve.wait_ge(xg_hi, done - 1)
                    dve.wait_ge(xg_lo, done - 1)
                V.tensor_scalar(xgt[:, k % 2, :], xT[:, k, :], cst[:, col[name] + k:col[name] + k + 1], None,
                                ALU.mult).then_inc(xg_ready, 1)

            def gain_lo(norm, k):
                if norm == 4:
                    return
                dve.wait_ge(xg_hi, KT * norm + k + 1)
                V.tensor_tensor(xgL[:, k, :], xgt[:, k % 2, :], xgH[:, k, :].bitcast(F32),
                                ALU.subtract).then_inc(xg_lo, 1)

            def renew(norm, ks):
                for k in ks:
                    V.tensor_tensor(xT[:, k, :], ps[:, k, :], xT[:, k, :], ALU.add).then_inc(x_upd, 1)
                    gain(norm, k)
                    if k > ks[0]:
                        gain_lo(norm, k - 1)
                gain_lo(norm, ks[-1])

            def mean_square(norm):
                dve.wait_ge(stat_done, norm + 1)
                if norm in (0, 4):
                    link(V.tensor_scalar(small[:, 64:64 + ST], ps[:, 7 if norm else 3, 0:ST], 1.0 / D, EPS, ALU.mult, ALU.add))
                    ins = V.reciprocal(small[:, 64:64 + ST], small[:, 64:64 + ST])
                if norm == 4:
                    ins.then_inc(ms_ready, 1)
                    return
                link(V.tensor_scalar(msq[:, :], ps[:, 4 if norm == 2 else 2, :], 1.0 / D, EPS, ALU.mult, ALU.add))
                V.reciprocal(msq[:, :], msq[:, :]).then_inc(ms_ready, 1)

            def scaled(par):
                return V.tensor_tensor(evt[:, par, :], ps[:, par, :], rinv[:, :], ALU.mult)

            def attn_max(layer, h):
                a = XH * layer + h
                dve.wait_ge(sc_done, a + 1)
                link(V.reduce_max(small[:, 88:88 + ST], ps[:, 6:8, :].rearrange("p b (t m) -> p (b t) m", m=M), AX_X))
                V.tensor_scalar(small[:, 80:80 + ST], small[:, 88:88 + ST], -XSCALE, None,
                                ALU.mult).then_inc(mx_ready, 1)

            def attn_norm(layer, h):
                a = XH * layer + h
                dve.wait_ge(p_exp, a + 1)
                if layer:
                    V.reciprocal(small[:, 92:92 + ST], small[:, 84:84 + ST]).then_inc(p_inv, 1)
                    return
                link(V.reciprocal(small[:, 92:92 + ST], small[:, 84:84 + ST]))
                V.tensor_tensor(prob[:, :, :], prob[:, :, :],
                                small[:, 92:92 + ST].unsqueeze(2).broadcast_to([P, ST, M]),
                                ALU.mult).then_inc(p_norm, 1)

            def attn_lo(layer, h):
                a = XH * layer + h
                dve.wait_ge(xo_hi, a + 1)
                V.tensor_tensor(mixL[:, KT + h, :], ps[:, 4, :], mixH[:, KT + h, :].bitcast(F32),
                                ALU.subtract).then_inc(xo_lo, 1)

            dve.wait_ge(m_ss, MT)
            link(V.tensor_scalar(small[:, 2:2 + MT], small[:, 0:MT], 1.0 / D, EPS, ALU.mult, ALU.add))
            V.reciprocal(small[:, 2:2 + MT], small[:, 2:2 + MT]).then_inc(m_ms, 1)
            dve.wait_ge(s_tr, 1)
            V.tensor_copy(cst[:, :], ps[:, 3, 0:NCOL]).then_inc(s_cst, 1)
            dve.wait_ge(m_inv, 1)
            for t in range(MT):
                V.tensor_scalar(mrow[:, t, :], mrow[:, t, :], small[:, 4 + t:5 + t], None, ALU.mult).then_inc(m_row, 1)
            lo(0)
            lo(1)
            dve.wait_ge(s_cst, 1)
            for k in range(KT):
                dve.wait_ge(m_tr, k + 1)
                V.tensor_scalar(memN[:, k, :], ps[:, 4 + k % 4, 0:M], cst[:, col["mem"] + k:col["mem"] + k + 1],
                                None, ALU.mult).then_inc(m_g, 1)
                dve.wait_ge(m_hi, k + 1)
                V.tensor_tensor(memL[:, k, :], memN[:, k, :], memH[:, k, :].bitcast(F32),
                                ALU.subtract).then_inc(m_lo, 1)
            table = [cst[:, col[f"lb{r}"]:col[f"lb{r}"] + NH] for r in range(NLB)]
            shifted = small[:, 16:16 + NLB * NH].rearrange("p (r h) -> p r h", h=NH)
            top = small[:, 8:8 + NH]
            link(V.tensor_tensor(top, table[0], table[1], ALU.max))
            link(V.tensor_tensor(top, top, table[2], ALU.max))
            for r in range(NLB):
                link(V.tensor_tensor(shifted[:, r, :], table[r], top, ALU.subtract))
            dve.wait_ge(lbe, 1)
            link(V.tensor_tensor(top, shifted[:, 0, :], shifted[:, 1, :], ALU.add))
            link(V.tensor_tensor(top, top, shifted[:, 2, :], ALU.add))
            link(V.reciprocal(top, top))
            link(V.tensor_tensor(headc[:, 4, :], shifted[:, 0, :], top, ALU.mult))
            link(V.tensor_scalar(headc[:, 5, :], headc[:, 4, :], -1.0, 1.0, ALU.mult, ALU.add))
            link(V.tensor_copy(headc[:, 0:4, :], cst[:, col["a_b"]:col["a_b"] + 4 * NH].rearrange("p (k h) -> p k h", h=NH)))

            link(V.tensor_copy(dwh[:, :], cst[:, col["dw"]:col["dw"] + TAPS * KT]))
            V.tensor_tensor(dwl[:, :], cst[:, col["dw"]:col["dw"] + TAPS * KT], dwh[:, :].bitcast(F32), ALU.subtract).then_inc(c_dw, 1)

            for c in range(2 * XH):
                n = first["kv0"] + c
                lo(n + 2)
                dve.wait_ge(chunk_done, n + 1)
                if c < XH:
                    V.tensor_copy(KTs[0][:, c, :], ps[:, c % 2, 0:M]).then_inc(tile_free, 1)
                elif c == 2 * XH - 1:
                    V.tensor_copy(VMs[0][:, :, :], ps[:, 4:4 + MT, :]).then_inc(kv_done, 1)
                dve.wait_ge(x_tr, c + 1)
                V.tensor_copy(xT[:, c, :], ps[:, 2 + c % 2, :]).then_inc(x_upd, 1)
                gain(0, c)
                gain_lo(0, c)

            for layer in range(2):
                if layer == 0:
                    n = first["xq0"]
                    for c in range(XH):
                        lo(n + c + 2)
                        if c == 0:
                            mean_square(0)
                            dve.wait_ge(r_ready, 1)
                        if c >= 2:
                            dve.wait_ge(xq_ready, c - 1)
                        dve.wait_ge(chunk_done, n + c + 1)
                        scaled(c % 2).then_inc(tile_free, 1)
                    n = first["val"]
                    dve.wait_ge(s_vb, 16)
                    for h in range(XH):
                        attn_max(0, h)
                        attn_norm(0, h)
                        lo(n + 2 * h + 2)
                        lo(n + 2 * h + 3)
                        c = 2 * h + 1
                        if c % GT == GT - 1:
                            dve.wait_ge(chunk_done, n + c + 1)
                            for t in range(ST):
                                V.scalar_tensor_tensor(out=val[:, t, 512 * (c // GT):512 * (c // GT + 1)], in0=ps[:, t, :],
                                                       scalar=small[:, 68 + t:69 + t],
                                                       in1=vbias[:, 512 * (c // GT):512 * (c // GT + 1)],
                                                       op0=ALU.mult, op1=ALU.add).then_inc(v_done, 1)
                        attn_lo(0, h)

                    def sums(lv):
                        o = sum(S >> m for m in range(1, lv))
                        return tb[:, o:o + (S >> lv)]

                    def level(lv, h, q):
                        if lv == 0:
                            dve.wait_ge(s_zero, 1)
                        else:
                            dve.wait_ge(lv_taken, h * LV + lv)
                        dve.wait_ge(lv_done, h * LV + lv + 1)
                        A, B = qb[:, q, :], kb[:, q, :]
                        if lv == 0:
                            V.tensor_tensor(A, A, fb[:, q, :], ALU.mult).then_inc(lv_ready, 1)
                        elif lv <= 8:
                            L = 1 << (lv - 1)
                            nb = S // (2 * L)
                            T = (fb[:, q, :] if lv == 1 else sums(lv - 1)).rearrange("p (n two) -> p n two", two=2)
                            Ao = A.rearrange("p (n two l) -> p n two l", two=2, l=L)[:, :, 1, :]
                            Be = B.rearrange("p (n two l) -> p n two l", two=2, l=L)[:, :, 0, :]
                            V.tensor_tensor(Ao, Ao, T[:, :, 0:1].broadcast_to([P, nb, L]), ALU.mult)
                            ins = V.tensor_tensor(Be, Be, T[:, :, 1:2].broadcast_to([P, nb, L]), ALU.mult)
                            if lv <= 7:
                                ins = V.tensor_tensor(sums(lv), T[:, :, 0], T[:, :, 1], ALU.mult)
                            ins.then_inc(lv_ready, 1)
                        bank = ps[:, 6 + lv % 2, :]
                        if lv < MASKED:
                            V.copy_predicated(att_view(0, ST * P + P, ST), mask[:, lv, :].bitcast(U32).unsqueeze(1).broadcast_to([P, ST, P]),
                                              bank.rearrange("p (b t) -> p b t", t=P)).then_inc(lv_taken, 1)
                        elif lv == MASKED:
                            V.tensor_copy(att_view(P, 2 * (S + P), 2), bank[:, 0:2 * P].rearrange("p (b t) -> p b t", t=P)).then_inc(lv_taken, 1)
                        else:
                            V.tensor_copy(att[:, 0:2, 2 * P:4 * P], bank.rearrange("p (b t) -> p b t", t=2 * P)).then_inc(lv_taken, 1)

                    def att_view(offset, step, count):
                        return bass.AP(tensor=att[:, :, :].tensor, offset=offset, ap=[[ST * S, P], [step, count], [1, P]])

                    def out_ms(h):
                        dve.wait_ge(o_stat, h + 1)
                        V.tensor_scalar(oinv[:, :], ps[:, 5, :], 1.0 / P, EPS, ALU.mult, ALU.add).then_inc(o_step, 1)
                        dve.wait_ge(o_step, 4 * h + 1)
                        V.reciprocal(oinv[:, :], oinv[:, :]).then_inc(o_ms, 1)

                    def out_split(h, q):
                        dve.wait_ge(o_inv, h + 1)
                        V.tensor_tensor(mixt[:, :], ps[:, 4, :], oinv[:, :], ALU.mult).then_inc(o_step, 1)
                        dve.wait_ge(o_step, 4 * h + 2)
                        V.scalar_tensor_tensor(out=mixt[:, :], in0=mixt[:, :], scalar=cst[:, col["a_on"]:col["a_on"] + 1],
                                               in1=gb[:, q, :], op0=ALU.mult, op1=ALU.mult).then_inc(o_step, 1)
                        dve.wait_ge(o_step, 4 * h + 3)
                        V.tensor_scalar(mixH[:, bass.ds(h, 1), :], mixt[:, :].unsqueeze(1), 1.0, None, ALU.mult).then_inc(o_step, 1)
                        dve.wait_ge(o_step, 4 * h + 4)
                        V.tensor_tensor(mixL[:, bass.ds(h, 1), :], mixt[:, :].unsqueeze(1),
                                        mixH[:, bass.ds(h, 1), :].bitcast(F32), ALU.subtract).then_inc(mix_lo, 1)

                    def head(b, i=0, k=0):
                        h, q = b + i * k, b % 2
                        if b >= 2:
                            dve.wait_ge(h_act, 3 * h - 3)
                        V.tensor_scalar(hc[:, q, :].unsqueeze(2), headc[:, :, bass.ds(h, 1)], 1.0, None, ALU.mult).then_inc(hc_ready, 1)
                        if b == 0:
                            dve.wait_ge(xq_ready, XH)
                            dve.wait_ge(v_done, 2 * ST)
                        for j in range(3):
                            for lv in range(4 * j, min(4 * j + 4, LV)) if b else ():
                                level(lv, h - 1, 1 - q)
                                if b >= 2 and lv == 0:
                                    out_ms(h - 2)
                                if b >= 2 and lv == 2:
                                    out_split(h - 2, q)
                                if lv == 5:
                                    forget(h, q)
                            if 3 * b + j >= 2:
                                dve.wait_ge(h_act, 3 * h + j - 1)
                            dve.wait_ge(chunk_done, first["head"] + 3 * h + j + 1)
                            scaled((b + j) % 2).then_inc(tile_free, 1)
                            if b == 0 and j == 1:
                                forget(h, q)
                        V.tensor_scalar(vh[:, q, :, :], val[:, :, bass.ds(h * P, P)], 1.0, None, ALU.mult).then_inc(k_ready, 1)

                    def forget(h, q):
                        dve.wait_ge(hc_ready, h + 1)
                        dve.wait_ge(h_act, 3 * h + 1)
                        V.tensor_scalar(fb[:, q, :], fb[:, q, :], hc[:, q, 5:6], hc[:, q, 4:5], ALU.mult, ALU.add).then_inc(t_ready, 1)
                        dve.wait_ge(t_ready, h + 1)
                        V.tensor_scalar(kb[:, q, :], fb[:, q, :], -1.0, 1.0, ALU.mult, ALU.add)

                    head(0)
                    head(1)
                    with dve.Fori(0, HEADS_LOOP) as i:
                        head(2, i, 2)
                        head(3, i, 2)
                else:
                    tapped = [0]

                    def taps(r, t0, t1):
                        for t in range(t0, t1):
                            w = cst[:, col["dw"] + t * KT + r:col["dw"] + t * KT + r + 1]
                            u = upad[:, t:t + S]
                            if t == 0:
                                b = col["dwb"] + r
                                ins = V.tensor_scalar(y[:, r, :], u, w, cst[:, b:b + 1], ALU.mult, ALU.add)
                            elif t == 1:
                                ins = V.tensor_scalar(y2[:, :], u, w, None, ALU.mult)
                            else:
                                dve.wait_ge(c_tap, tapped[0] - 1)
                                to = y2[:, :] if t % 2 else y[:, r, :]
                                ins = V.scalar_tensor_tensor(out=to, in0=u, scalar=w, in1=to, op0=ALU.mult, op1=ALU.add)
                            ins.then_inc(c_tap, 1)
                            tapped[0] += 1

                    def add_taps(r):
                        dve.wait_ge(c_tap, tapped[0])
                        dve.wait_ge(c_pe, r + 1)
                        V.tensor_tensor(y[:, r, :], ps[:, tap_bank(r), :], y[:, r, :], ALU.add).then_inc(c_y, 1)

                    mean_square(2)
                    dve.wait_ge(r_ready, 3)
                    dve.wait_ge(silu_ready, FT)
                    dve.wait_ge(s_zero, 2)
                    for r in range(KT):
                        n = first["mix1"] + rounds[r][0][0]
                        last = TAPS - pe_taps[r]
                        if r:
                            dve.wait_ge(c_sig, r)
                            dve.wait_ge(c_u, r)
                        dve.wait_ge(chunk_done, n + 1)
                        scaled(0).then_inc(tile_free, 1)
                        dve.wait_ge(chunk_done, n + 2)
                        scaled(1).then_inc(tile_free, 1)
                        if r:
                            add_taps(r - 1)
                        dve.wait_ge(c_sig, r + 1)
                        dve.wait_ge(tile_free, tile0["mix1"] + 2 * r + 2)
                        if r:
                            dve.wait_ge(c_ulo, r)
                        b = col["b_b"] + r
                        V.scalar_tensor_tensor(out=upad[:, PAD:PAD + S], in0=evt[:, 1, :], scalar=cst[:, b:b + 1],
                                               in1=gate[:, :], op0=ALU.add, op1=ALU.mult).then_inc(c_u, 1)
                        dve.wait_ge(c_u, r + 1)
                        taps(r, 0, 4)
                        if r >= XH:
                            attn_max(1, r - XH)
                        taps(r, 4, 8)
                        if r > XH:
                            attn_lo(1, r - XH - 1)
                        if r >= XH:
                            attn_norm(1, r - XH)
                        taps(r, 8, last)
                        dve.wait_ge(c_tap, tapped[0])
                        V.tensor_tensor(y[:, r, :], y[:, r, :], y2[:, :], ALU.add).then_inc(c_tap, 1)
                        tapped[0] += 1
                        for pos, kind, c in rounds[r]:
                            if kind == "q":
                                dve.wait_ge(chunk_done, first["mix1"] + pos + 1)
                                if c >= 2:
                                    dve.wait_ge(xq_ready, XH + c - 1)
                                V.tensor_tensor(xgt[:, c % 2, :], ps[:, 7, :], rinv[:, :], ALU.mult).then_inc(q_free, 1)

                def less(k):
                    V.tensor_tensor(y[:, k, :], y[:, k, :], mu[:, :], ALU.subtract).then_inc(c_less, 1)

                n = first[f"out{layer}"]
                NG = MIXT // 2
                for c in range(2 * NG):
                    if layer == 0 and c < 3:
                        for lv in range(4 * c, min(4 * c + 4, LV)):
                            level(lv, NH - 1, (NH - 1) % 2)
                            if lv == 0:
                                out_ms(NH - 2)
                            if lv == 2:
                                out_split(NH - 2, NH % 2)
                    if layer == 0 and c == 3:
                        out_ms(NH - 1)
                        out_split(NH - 1, (NH - 1) % 2)
                    if c == 0:
                        dve.wait_ge(lo_ready, n + c + 2)
                    lo(n + c + 2)
                    if layer == 1 and c == 0:
                        add_taps(KT - 1)
                        dve.wait_ge(c_y, KT)
                        dve.wait_ge(c_sum, KT - 2)
                        V.tensor_tensor(ysum[:, :], ysum[:, :], y[:, KT - 1, :], ALU.add).then_inc(c_sum, 1)
                        dve.wait_ge(c_sum, KT - 1)
                        V.tensor_tensor(y[:, KT - 1, :], y[:, KT - 1, :], mid[:, :], ALU.subtract).then_inc(c_cent, 1)
                        dve.wait_ge(c_sq, KT)
                        dve.wait_ge(c_sqs, KT - 2)
                        V.tensor_tensor(sqsum[:, :], sqsum[:, :], square_slot(KT - 1), ALU.add).then_inc(c_sqs, 1)
                        attn_lo(1, XH - 1)
                        dve.wait_ge(c_mu, 1)
                        link(V.scalar_tensor_tensor(out=mu[:, :], in0=ps[:, 6, :], scalar=1.0 / D, in1=mid[:, :],
                                                    op0=ALU.mult, op1=ALU.subtract))
                        link(V.tensor_tensor(msq[:, :], mu[:, :], mu[:, :], ALU.mult))
                        dve.wait_ge(c_var, 1)
                        link(V.scalar_tensor_tensor(out=msq[:, :], in0=ps[:, 7, :], scalar=1.0 / D, in1=msq[:, :],
                                                    op0=ALU.mult, op1=ALU.subtract))
                        link(V.tensor_scalar(msq[:, :], msq[:, :], 0.0, EPS, ALU.max, ALU.add))
                        V.reciprocal(msq[:, :], msq[:, :]).then_inc(c_norm, 1)
                        for k in range(3):
                            less(k)
                    if layer == 1 and c == 1:
                        dve.wait_ge(c_act, 1)
                    if layer == 1 and 1 <= c <= 2:
                        for k in {1: range(0, 6), 2: range(6, 8)}[c]:
                            if k >= 2:
                                dve.wait_ge(c_act, k)
                            dve.wait_ge(c_less, k + 1)
                            V.tensor_tensor(xgt[:, k % 2, :], y[:, k, :], rsd[:, :], ALU.mult).then_inc(c_norm, 1)
                            if k + 3 < KT:
                                less(k + 3)
                            if k >= 1:
                                dve.wait_ge(mix_hi, k)
                                V.tensor_tensor(mixL[:, k - 1, :], evt[:, (k - 1) % 2, :], mixH[:, k - 1, :].bitcast(F32),
                                                ALU.subtract).then_inc(mix_lo, 1)
                        if c == 2:
                            dve.wait_ge(mix_hi, KT)
                            V.tensor_tensor(mixL[:, KT - 1, :], evt[:, (KT - 1) % 2, :], mixH[:, KT - 1, :].bitcast(F32),
                                            ALU.subtract).then_inc(mix_lo, 1)
                    ks = {NG - 1: (0, 1), NG: (2, 3), 2 * NG - 1: tuple(range(GT, KT))}.get(c)
                    if ks:
                        dve.wait_ge(chunk_done, n + c + 1 if c != NG else n + NG)
                        renew(2 * layer + 1, ks)

                def ffn(b, i):
                    j = b + i
                    m = FT * layer + j
                    lo(first[f"gu{layer}"] + 2 * b + 2, i, 2)
                    if b == 0:
                        mean_square(2 * layer + 1)
                        dve.wait_ge(r_ready, 2 * layer + 2)
                        if layer == 0:
                            dve.wait_ge(h_act, 3 * NH)
                        else:
                            dve.wait_ge(mix_hi, KT)
                    else:
                        dve.wait_ge(silu_ready, m)
                    dve.wait_ge(chunk_done, first[f"gu{layer}"] + 2 * j + 1)
                    scaled(0).then_inc(tile_free, 1)
                    lo(first[f"gu{layer}"] + 2 * b + 3, i, 2)
                    dve.wait_ge(chunk_done, first[f"gu{layer}"] + 2 * j + 2)
                    scaled(1).then_inc(tile_free, 1)
                    dve.wait_ge(silu_ready, m + 1)
                    dve.wait_ge(tile_free, tile0[f"gu{layer}"] + 2 * j + 2)
                    V.tensor_tensor(xgt[:, 1, :], evt[:, 1, :], xgt[:, 0, :], ALU.mult).then_inc(act_step, 1)
                    dve.wait_ge(act_step, 2 * m + 1)
                    V.tensor_scalar(actH[:, bass.ds(j, 1), :], xgt[:, 1, :].unsqueeze(1), 1.0, None, ALU.mult).then_inc(act_step, 1)
                    dve.wait_ge(act_step, 2 * m + 2)
                    V.tensor_tensor(actL[:, bass.ds(j, 1), :], xgt[:, 1, :].unsqueeze(1), actH[:, bass.ds(j, 1), :].bitcast(F32),
                                    ALU.subtract).then_inc(act_lo, 1)
                    dve.wait_ge(act_lo, m + 1)

                ffn(0, 0)
                with dve.Fori(0, FT - 1) as i:
                    ffn(1, i)

                n = first[f"down{layer}"]
                pairs = FT // 2
                norm = 2 * layer + 2
                with dve.Fori(0, (pairs - 1) // 2) as i:
                    lo(n + 2, i, 2)
                    lo(n + 3, i, 2)
                lo(n + pairs - 1 + 2)
                dve.wait_ge(chunk_done, n + pairs)
                renew(norm, (0, 1))
                lo(n + pairs + 2)
                renew(norm, (2, 3))
                with dve.Fori(0, (pairs - 3) // 2) as i:
                    lo(n + pairs + 1 + 2, i, 2)
                    lo(n + pairs + 2 + 2, i, 2)
                lo(n + 2 * pairs)
                lo(n + 2 * pairs + 1)
                dve.wait_ge(chunk_done, n + 2 * pairs)
                renew(norm, tuple(range(GT, KT)))
            mean_square(4)
            dve.wait_ge(r_ready, 5)
            for t in range(ST):
                V.tensor_scalar(orow[:, t, 0:GT * P].rearrange("p (k c) -> p k c", c=P), ps[:, 0:GT, t * P:(t + 1) * P],
                                small[:, 68 + t:69 + t], None, ALU.mult).then_inc(f_row, 1)

        @block.tensor
        def _(pe):
            mm = nc.tensor.matmul

            def exact(out_ap, left, right, start, stop):
                mm(out_ap, left[0], right[0], start=start, stop=False)
                mm(out_ap, left[0], right[1], start=False, stop=False)
                return mm(out_ap, left[1], right[0], start=False, stop=stop)

            def tile_chunk(base, number, i=0, k=0, other=None, width=S, between=None, ready=None, bank=None):
                num, half, par = at_chunk(base, i, k)
                H, L = other or (xgH, xgL)
                if number is not None and (not isinstance(number, int) or number >= 2):
                    pe.wait_ge(tile_free, number - 1)
                bank = par if bank is None else bank
                pe.wait_ge(lo_ready, num + 1)
                for kt in range(KT):
                    if ready is not None:
                        pe.wait_ge(xg_lo, KT * ready + kt + 1)
                    w = slice(kt * P, (kt + 1) * P)
                    ins = exact(ps[:, bank, 0:width], (wH[:, par, w], wL[:, par, w]), (H[:, kt, :], L[:, kt, :]),
                                kt == 0, kt == KT - 1)
                    if kt == KT - 1:
                        ins.then_inc(chunk_done, 1)
                    if between is not None:
                        between(kt)

            def group_chunk(base, bank, acts, start, stop, i=0, k=0, between=None):
                num, half, par = at_chunk(base, i, k)
                pe.wait_ge(lo_ready, num + 1)
                for kk in range(2):
                    right = acts(kk)
                    for t in range(GT):
                        w = slice(kk * 512 + t * P, kk * 512 + (t + 1) * P)
                        ins = exact(ps[:, bank + t, :], (wH[:, par, w], wL[:, par, w]), right,
                                    start and kk == 0, stop and kk == 1)
                        if kk == 1 and t == GT - 1:
                            ins.then_inc(chunk_done, 1)
                        if between is not None and t % 2:
                            between(2 * kk + t // 2)

            def stat(norm):
                pe.wait_ge(sq_sum, (KT - 1) * (norm + 1))
                if norm in (0, 4):
                    for t in range(ST):
                        ins = mm(ps[:, 7 if norm else 3, t:t + 1], sqsum[:, t * P:(t + 1) * P], ones[:, 0:1], start=True, stop=True)
                if norm == 4:
                    ins.then_inc(stat_done, 1)
                    return
                mm(ps[:, 4 if norm == 2 else 2, :], ones[:, :], sqsum[:, :], start=True, stop=True).then_inc(stat_done, 1)

            def turn_back(k):
                for t in range(ST):
                    ins = nc.tensor.transpose(ps[:, k, t * P:(t + 1) * P], yT[:, k, t * P:(t + 1) * P], ident[:, :])
                ins.then_inc(f_tr, 1)

            def attn_scores(layer, h):
                a = XH * layer + h
                pe.wait_ge(xq_ready, a + 1)
                if a:
                    pe.wait_ge(p_norm, a)
                for t in range(ST):
                    ins = mm(ps[:, 6 + t // 2, (t % 2) * M:(t % 2 + 1) * M], xq[:, h, t * P:(t + 1) * P], KTs[layer][:, h, :],
                             start=True, stop=True)
                ins.then_inc(sc_done, 1)

            def attn_turn(layer, h):
                a = XH * layer + h
                pe.wait_ge(p_norm, a + 1)
                if a:
                    pe.wait_ge(xo_lo, a)
                for m in range(MT):
                    for t in range(ST):
                        ins = nc.tensor.transpose(ps[:, 4 + m, t * P:(t + 1) * P], prob[:, t, m * P:(m + 1) * P], ident[:, :])
                ins.then_inc(pt_done, 1)

            def attn_values(layer, h):
                a = XH * layer + h
                pe.wait_ge(pt_ready, a + 1)
                for m in range(MT):
                    ins = mm(ps[:, 4, :], VMs[layer][:, m, h * P:(h + 1) * P], probT[:, m, :], start=(m == 0), stop=(m == MT - 1))
                ins.then_inc(xo_done, 1)

            def tile_taps(r):
                pe.wait_ge(c_diag, r + 1)
                pe.wait_ge(c_ulo, r + 1)
                if r >= 2:
                    pe.wait_ge(c_y, r - 1)
                for i in range(pe_taps[r]):
                    t = TAPS - pe_taps[r] + i
                    ins = exact(ps[:, tap_bank(r), :], (dgH[:, r % 2, i, :], dgL[:, r % 2, i, :]), (upH[:, t:t + S], upL[:, t:t + S]),
                                i == 0, i == pe_taps[r] - 1)
                ins.then_inc(c_pe, 1)

            pe.wait_ge(s_const, 1)
            pe.wait_ge(s_rows, 16 * len(vec_rows))
            o = 0
            for g, n in enumerate(rows_in):
                ins = nc.tensor.transpose(ps[:, 3, o:o + n], vrow[0:n, g, :], ident[0:n, 0:n])
                o += n
            ins.then_inc(s_tr, 1)
            pe.wait_ge(m_row, MT)
            for k in range(KT):
                if k >= 4:
                    pe.wait_ge(m_g, k - 3)
                for t in range(MT):
                    ins = nc.tensor.transpose(ps[:, 4 + k % 4, t * P:(t + 1) * P], mrow[:, t, k * P:(k + 1) * P], ident[:, :])
                ins.then_inc(m_tr, 1)
            pe.wait_ge(m_lo, KT)

            def memory_values(num, c):
                pe.wait_ge(lo_ready, num + 1)
                par = num % 2
                for kk in range(2):
                    k = 2 * c + kk
                    w = slice(kk * 512, (kk + 1) * 512)
                    for t in range(MT):
                        f = slice(t * P, (t + 1) * P)
                        ins = exact(ps[:, 4 + t, :], (memH[:, k, f], memL[:, k, f]), (wH[:, par, w], wL[:, par, w]),
                                    k == 0, k == KT - 1)
                ins.then_inc(chunk_done, 1)

            n = first["kv0"]
            for c in range(2 * XH):
                if c < XH:
                    tile_chunk(n + c, tile0["kv0"] + c, other=(memH, memL), width=M)
                else:
                    memory_values(n + c, c - XH)
                if c == 0:
                    pe.wait_ge(s_x, 16 * ST)
                    pe.wait_ge(s_cst, 1)
                if c >= 2:
                    pe.wait_ge(x_upd, c - 1)
                for t in range(ST):
                    ins = nc.tensor.transpose(ps[:, 2 + c % 2, t * P:(t + 1) * P], xrow[:, t, c * P:(c + 1) * P], ident[:, :])
                ins.then_inc(x_tr, 1)

            for layer in range(2):
                if layer == 0:
                    n = first["xq0"]
                    for c in range(XH):
                        tile_chunk(n + c, tile0["xq0"] + c, ready=0 if c == 0 else None)
                        if c == 0:
                            stat(0)
                if layer == 0:
                    n = first["val"]
                    pe.wait_ge(tile_free, tile0["head"])
                    pe.wait_ge(ms_ready, 1)
                    pe.wait_ge(kv_done, 1)
                    for c in range(2 * GT):
                        if c % 2 == 0:
                            attn_scores(0, c // 2)
                        else:
                            attn_turn(0, c // 2)
                        if c == GT:
                            pe.wait_ge(v_done, ST)
                        pe.wait_ge(lo_ready, n + c + 1)
                        par = c % 2
                        for kk in range(2):
                            k = 2 * (c % GT) + kk
                            w = slice(kk * 512, (kk + 1) * 512)
                            for t in range(ST):
                                f = slice(t * P, (t + 1) * P)
                                ins = exact(ps[:, t, :], (xgH[:, k, f], xgL[:, k, f]), (wH[:, par, w], wL[:, par, w]),
                                            k == 0, k == KT - 1)
                        ins.then_inc(chunk_done, 1)
                        if c % 2:
                            attn_values(0, c // 2)
                    pe.wait_ge(v_done, 2 * ST)
                    pe.wait_ge(xo_lo, XH)

                    def level(lv, h, q, first_head):
                        if lv == 0:
                            pe.wait_ge(k_ready, h + 1)
                            pe.wait_ge(h_act, 3 * h + 2)
                            if not first_head:
                                pe.wait_ge(lv_taken, h * LV)
                        else:
                            pe.wait_ge(lv_ready, h * (LV - 1) + lv)
                        bank = ps[:, 6 + lv % 2, :]
                        A, B = qb[:, q, :], kb[:, q, :]
                        if lv < MASKED:
                            for b in range(ST):
                                f = slice(b * P, (b + 1) * P)
                                ins = mm(bank[:, f], B[:, f], A[:, f], start=True, stop=True)
                        elif lv == MASKED:
                            for b in range(2):
                                ins = mm(bank[:, b * P:(b + 1) * P], B[:, 2 * b * P:(2 * b + 1) * P],
                                         A[:, (2 * b + 1) * P:(2 * b + 2) * P], start=True, stop=True)
                        else:
                            for b in range(2):
                                ins = mm(bank[:, 2 * b * P:2 * (b + 1) * P], B[:, b * P:(b + 1) * P], A[:, 2 * P:4 * P],
                                         start=True, stop=True)
                        ins.then_inc(lv_done, 1)

                    def head_values(h, q, first_head):
                        pe.wait_ge(lv_taken, (h + 1) * LV)
                        if not first_head:
                            pe.wait_ge(mix_lo, h)
                        for t in range(ST):
                            ins = mm(ps[:, 4, t * P:S], vh[:, q, t, :], att[:, t, t * P:S], start=(t == 0), stop=(t == ST - 1))
                        ins.then_inc(o_done, 1)

                    def head_stat(h, first_head):
                        pe.wait_ge(o_sq, h + 1)
                        if not first_head:
                            pe.wait_ge(o_ms, h)
                        mm(ps[:, 5, :], ones[:, :], osq[:, :], start=True, stop=True).then_inc(o_stat, 1)

                    def places(place, h, b):
                        if b >= 2 and place == 0:
                            head_stat(h - 2, b == 2 and isinstance(h, int))
                        if b >= 1 and place < LV:
                            level(place, h - 1, 1 - b % 2, b == 1)
                        if b >= 1 and place == 11:
                            head_values(h - 1, 1 - b % 2, b == 1)

                    def head(b, i=0, k=0):
                        h = b + i * k
                        for j in range(3):
                            tile_chunk(first["head"] + 3 * b + j, tile0["head"] + 3 * h + j, i, 3 * k,
                                       between=lambda kt: places(4 * j + kt // 2, h, b) if kt % 2 else None)

                    head(0)
                    head(1)
                    with pe.Fori(0, HEADS_LOOP) as i:
                        head(2, i, 2)
                        head(3, i, 2)
                else:
                    pe.wait_ge(tile_free, tile0["mix1"])
                    for r in range(KT):
                        for pos, kind, c in rounds[r]:
                            num = first["mix1"] + pos
                            if kind in ("gate", "value"):
                                bank = int(kind == "value")
                                tile_chunk(num, tile0["mix1"] + 2 * r + bank, bank=bank, ready=2 if num == first["mix1"] else None)
                                if pos == 0:
                                    stat(2)
                                if kind == "gate" and r:
                                    tile_taps(r - 1)
                                if kind == "gate" and r > XH:
                                    if r == XH + 1:
                                        pe.wait_ge(c_mid, 1)
                                    attn_turn(1, r - XH - 1)
                                if kind == "value" and r > XH:
                                    attn_values(1, r - XH - 1)
                            elif kind == "V":
                                if c == 0:
                                    pe.wait_ge(ms_ready, 3)
                                memory_values(num, c)
                            else:
                                if c:
                                    pe.wait_ge(k_free if kind == "K" else q_free, c)
                                mem_in = (memH, memL) if kind == "K" else None
                                if kind == "K" and c == 0:
                                    pe.wait_ge(m_lo, 2 * KT)
                                tile_chunk(num, None, bank=6 if mem_in else 7, other=mem_in, width=M if mem_in else S)
                        if r >= XH:
                            if r == XH:
                                pe.wait_ge(kv_done, 2)
                                pe.wait_ge(k_free, XH)
                                pe.wait_ge(q_free, XH)
                            attn_scores(1, r - XH)
                        if r == XH:
                            pe.wait_ge(c_sum, MID - 1)
                            mm(ps[:, 5, :], ones[:, :], ysum[:, :], start=True, stop=True).then_inc(c_mid_pe, 1)
                    pe.wait_ge(c_y, KT - 1)

                n = first[f"out{layer}"]
                NG = MIXT // 2
                pe.wait_ge(tile_free, tile0[f"gu{layer}"])
                for c, (g, kp) in enumerate(out_order[layer]):
                    if kp >= KT // 2 and (layer, c) != (1, 1):
                        pe.wait_ge(xo_lo, XH * layer + 2 * (kp - KT // 2) + 2)
                    elif kp < KT // 2:
                        pe.wait_ge(mix_lo, NH * layer + 2 * kp + 2)
                    beside = None
                    if layer == 0 and c < 3:
                        beside = lambda p: places(4 * c + p, NH, NH)
                    if layer == 0 and c == 3:
                        beside = lambda p: head_stat(NH - 1, False) if p == 0 else None
                    if layer == 1 and c == 1:
                        pe.wait_ge(p_norm, 2 * XH)
                        tile_taps(KT - 1)
                        attn_turn(1, XH - 1)
                        pe.wait_ge(c_sum, KT - 1)
                        mm(ps[:, 6, :], ones[:, :], ysum[:, :], start=True, stop=True).then_inc(c_mu, 1)
                        pe.wait_ge(c_y, KT)
                        pe.wait_ge(c_sqs, KT - 1)
                        mm(ps[:, 7, :], ones[:, :], sqsum[:, :], start=True, stop=True).then_inc(c_var, 1)
                        attn_values(1, XH - 1)
                        pe.wait_ge(xo_lo, 2 * XH)
                    group_chunk(n + c, GT * g, lambda kk: (mixH[:, 2 * kp + kk, :], mixL[:, 2 * kp + kk, :]),
                                c % NG == 0, c % NG == NG - 1, between=beside)

                n = first[f"gu{layer}"]
                t0 = tile0[f"gu{layer}"]
                tile_chunk(n, t0, ready=2 * layer + 1)
                stat(2 * layer + 1)
                tile_chunk(n + 1, t0 + 1)
                with pe.Fori(0, FT - 1) as i:
                    tile_chunk(n + 2, t0 + 2 + 2 * i, i, 2)
                    tile_chunk(n + 3, t0 + 3 + 2 * i, i, 2)

                n = first[f"down{layer}"]
                pairs = FT // 2

                def hidden(kp):
                    return lambda kk: (actH[:, kp * 2 + kk, :], actL[:, kp * 2 + kk, :])

                def hidden_at(base, i):
                    return lambda kk: tuple(a[:, bass.ds(i * 4 + base + kk, 1), :].rearrange("p a s -> p (a s)") for a in (actH, actL))

                pe.wait_ge(tile_free, t0 + 2 * FT)
                pe.wait_ge(act_lo, FT * layer + FT - 1)
                group_chunk(n, 0, hidden(0), True, False)
                pe.wait_ge(act_lo, FT * layer + FT)
                group_chunk(n + 1, 0, hidden(1), False, False)
                with pe.Fori(0, (pairs - 3) // 2) as i:
                    group_chunk(n + 2, 0, hidden_at(4, i), False, False, i, 2)
                    group_chunk(n + 3, 0, hidden_at(6, i), False, False, i, 2)
                group_chunk(n + pairs - 1, 0, hidden(pairs - 1), False, True)
                group_chunk(n + pairs, GT, hidden(0), True, False)
                with pe.Fori(0, (pairs - 3) // 2) as i:
                    group_chunk(n + pairs + 1, GT, hidden_at(2, i), False, False, i, 2)
                    group_chunk(n + pairs + 2, GT, hidden_at(4, i), False, False, i, 2)
                if layer == 1:
                    pe.wait_ge(f_y, GT)
                    for k in range(GT):
                        turn_back(k)
                group_chunk(n + 2 * pairs - 2, GT, hidden(pairs - 2), False, False)
                group_chunk(n + 2 * pairs - 1, GT, hidden(pairs - 1), False, True)
            for k in range(GT, KT):
                pe.wait_ge(f_y, k + 1)
                if k == KT - 1:
                    stat(4)
                    pe.wait_ge(ms_ready, 5)
                turn_back(k)


_INS = ["x", "mem", "norm_mix_g", "norm_ffn_g", "w_out", "xattn_w_kv", "ffn_w_gu", "ffn_w_down", "mem_norm_g",
        "final_norm_g", "a_w_in", "a_b_in", "a_lb_table", "a_onorm_g", "b_w_in", "b_b_in", "b_dw_w", "b_dw_b",
        "b_ln_g", "b_ln_b"]


def kernel(**inputs):
    import numpy as np
    import concourse.bacc as bacc
    from concourse.bass_utils import run_bass_kernel_spmd

    nc = bacc.Bacc("TRN2", target_bir_lowering=False, num_devices=1)
    arrays, args = {}, []
    for name in _INS:
        a = np.ascontiguousarray(inputs[name])
        arrays[f"in_{name}"] = a
        args.append(nc.dram_tensor(f"in_{name}", a.shape, mybir.dt.from_np(a.dtype), kind="ExternalInput").ap())
    shape = np.asarray(inputs["x"]).shape
    args.append(nc.dram_tensor("out_0", shape, F32, kind="ExternalOutput").ap())
    trunk(nc, *args)
    r = run_bass_kernel_spmd(nc, [arrays], core_ids=[0])
    return r.results[0]["out_0"]
```

```python
from contextlib import ExitStack

import concourse.bass as bass
from concourse import mybir

F32 = mybir.dt.float32
F32R = mybir.dt.float32r
U32 = mybir.dt.uint32
ALU = mybir.AluOpType
ACT = mybir.ActivationFunctionType
AX_X = mybir.AxisListType.X

P = 128
EPS = 1e-6
CHUNK = 1024


def trunk(nc, x, mem, g_mix, g_ffn, w_out, w_kv, w_gu, w_down, g_mem, g_fin,
          a_w, a_b, a_lb, a_on, b_w, b_b, b_dw, b_dwb, b_lng, b_lnb, out):
    S, D = x.shape[1], x.shape[2]
    M = mem.shape[1]
    KT = D // P
    ST = S // P
    MT = M // P
    XH = 4
    XW = XH * P
    NH = D // P
    FH = w_down.shape[1]
    FT = FH // P
    MIXT = KT + XH
    TAPS = b_dw.shape[1]
    PAD = TAPS - 1
    NLB = a_lb.shape[0]
    GT = 4
    LV = 10
    MASKED = 8
    XSCALE = float(P) ** -0.5

    extra = [[(kv, k), ("q", c), (kv, k + 1)] for kv, k, c in (("K", 0, 0), ("K", 2, 1), ("V", 0, 2), ("V", 2, 3))]
    extra += [[]] * (KT - XH)
    rounds, pos = [], 0
    for r in range(KT):
        kinds = [("gate", r), ("value", r)] + extra[r]
        rounds.append([(pos + i, kind, c) for i, (kind, c) in enumerate(kinds)])
        pos += len(kinds)
    MID = KT // 2
    centre = [[]] * 5 + [[0, 1], [2, 3], [4, 5, 6]]
    pe_taps = [2, 2, 2, 2, 7, 8, 8, 14]
    sizes = [("kv0", 2 * XH), ("xq0", XH), ("val", 2 * GT), ("head", 3 * NH),
             ("out0", MIXT), ("gu0", 2 * FT), ("down0", FT),
             ("mix1", pos), ("out1", MIXT), ("gu1", 2 * FT), ("down1", FT)]
    first, NCH = {}, 0
    for name, n in sizes:
        first[name] = NCH
        NCH += n
    tile0, nt = {}, 0
    for name, n in (("kv0", XH), ("xq0", XH), ("head", 3 * NH), ("gu0", 2 * FT),
                    ("mix1", 2 * KT), ("gu1", 2 * FT)):
        tile0[name] = nt
        nt += n
    X_PAIRS = list(range(KT // 2, MIXT // 2))
    M_PAIRS = list(range(KT // 2))
    out_order = [[(g, k) for g in range(2) for k in X_PAIRS + M_PAIRS],
                 [(0, k) for k in X_PAIRS + M_PAIRS] + [(1, k) for k in X_PAIRS + M_PAIRS]]

    vec_rows, col, at = [], {}, 0
    for name, ap in (("mix0", g_mix[0]), ("mix1", g_mix[1]), ("ffn0", g_ffn[0]), ("ffn1", g_ffn[1]),
                     ("mem", g_mem), ("fin", g_fin), ("a_b", a_b[0]), ("lb0", a_lb[0]), ("lb1", a_lb[1]),
                     ("lb2", a_lb[2]), ("a_on", a_on[0])):
        n = ap.shape[0] // P
        vec_rows.append((0, at, ap.rearrange("(r c) -> r c", c=P), n))
        col[name] = at
        at += n
    rows_in = [at]
    base = at
    at = 0
    for name, ap in (("b_b", b_b[0]), ("dwb", b_dwb[0]), ("lng", b_lng[0]), ("lnb", b_lnb[0])):
        n = ap.shape[0] // P
        vec_rows.append((1, at, ap.rearrange("(r c) -> r c", c=P), n))
        col[name] = base + at
        at += n
    rows_in.append(at)
    base += at
    dw_rows = b_dw[0].rearrange("t (r c) -> (t r) c", c=P)
    half = TAPS * KT // 2
    for g in range(2):
        vec_rows.append((2 + g, 0, dw_rows[g * half:(g + 1) * half], half))
        rows_in.append(half)
    col["dw"] = base
    NCOL = base + 2 * half

    with ExitStack() as ctx:
        where = [nc.sbuf_base + (-nc.sbuf_base) % 64]

        def place(name, shape, dt=F32, at=None):
            size = 4
            for n in shape[1:]:
                size *= n
            at = at and at + (-at) % 32
            if at is None:
                at = where[0]
                where[0] += size + (-size) % 32
            return nc.alloc_sbuf_tensor_at(name, shape, dt, offset=at)

        def sem(name):
            return ctx.enter_context(nc.semaphore(name))

        ident = place("ident", [P, P])
        ones = place("ones", [P, P])
        at_mask = where[0]
        mask = place("mask", [P, MASKED, P])
        cst = place("cst", [P, NCOL])
        headc = place("headc", [P, 6, NH])
        hc = place("hc", [P, 2, 6])
        small = place("small", [P, 128])
        xT = place("xT", [P, KT, S])
        at_xg = where[0]
        xgH = place("xgH", [P, KT, S], F32R)
        xgL = place("xgL", [P, KT, S], F32R)
        raw = place("raw", [P, 2, CHUNK])
        wH = place("wH", [P, 2, CHUNK], F32R)
        wL = place("wL", [P, 2, CHUNK], F32R)
        rinv = place("rinv", [P, S])
        msq = place("msq", [P, S])
        sqsum = place("sqsum", [P, S])
        sq = place("sq", [P, 2, S])
        xgt = place("xgt", [P, 2, S])
        evt = place("evt", [P, 2, S])
        at_kv = where[0]
        KTs = [place("memK0", [P, XH, M]), place("memK1", [P, XH, M], at=at_kv)]
        VMs = [place("memV0", [P, MT, XW]), place("memV1", [P, MT, XW], at=at_kv + 4 * XH * M)]
        memN = place("memN", [P, KT, M])
        arena = where[0]
        actH = place("actH", [P, FT, S], F32R, at=arena)
        actL = place("actL", [P, FT, S], F32R, at=arena + 4 * FT * S)
        mixH = place("mixH", [P, MIXT, S], F32R)
        mixL = place("mixL", [P, MIXT, S], F32R)
        at_val = where[0]
        val = place("val", [P, ST, D])
        at_heads = where[0]
        qb = place("qb", [P, 2, S])
        fb = place("fb", [P, 2, S])
        kb = place("kb", [P, 2, S])
        gb = place("gb", [P, 2, S])
        at_tail = where[0]
        tb = place("tb", [P, S])
        vh = place("vh", [P, 2, ST, P])
        osq = place("osq", [P, S])
        oinv = place("oinv", [P, S])
        mixt = place("mixt", [P, S])
        att = place("att", [P, ST, S], at=at_kv)
        vbias = place("vbias", [P, D], at=at_tail)
        xq = place("xq", [P, XH, S], at=at_heads)
        prob = place("prob", [P, ST, M], at=at_heads + 4 * XH * S)
        probT = place("probT", [P, MT, S], at=at_heads + 4 * XH * S + 4 * ST * M)
        memH = place("memH", [P, KT, M], F32R, at=arena)
        memL = place("memL", [P, KT, M], F32R, at=arena + 4 * KT * M)
        mrow = place("mrow", [P, MT, D], at=arena + 8 * KT * M)
        xrow = place("xrow", [P, ST, D], at=arena + 8 * KT * M + 4 * MT * D)
        vrow = place("vrow", [P, 4, P], at=arena + 8 * KT * M + 4 * MT * D + 4 * ST * D)
        msc = place("msc", [P, MT, D], at=at_val)
        y = place("y", [P, KT, S], at=at_val)
        PU = PAD + S + 2
        upad = place("upad", [P, PU], at=at_tail)
        upH = place("upH", [P, PU], F32R, at=at_tail + 4 * PU)
        upL = place("upL", [P, PU], F32R, at=at_tail + 8 * PU)
        gate = place("gate", [P, S], at=at_tail + 12 * PU)
        mu = place("mu", [P, S], at=at_tail + 12 * PU + 4 * S)
        ysum = mu
        y2 = place("y2", [P, S], at=at_mask)
        rsd = place("rsd", [P, S], at=at_mask)
        mid = place("mid", [P, S], at=at_mask + 4 * S)
        NTE, NTL = max(pe_taps[:-1]), pe_taps[-1]
        at_mixL = arena + 4 * MIXT * S
        assert 16 * NTE * P <= 4 * KT * S and 8 * NTL * P <= 4 * KT * S
        dgH = place("dgH", [P, 2, NTE, P], F32R, at=at_mixL)
        dgL = place("dgL", [P, 2, NTE, P], F32R, at=at_mixL + 8 * NTE * P)
        diags = [(dgH[:, slot], dgL[:, slot]) for slot in (0, 1)]
        diags.append((place("dgHlast", [P, NTL, P], F32R, at=arena)[:, :, :],
                      place("dgLlast", [P, NTL, P], F32R, at=arena + 4 * NTL * P)[:, :, :]))
        dwh = place("dwh", [P, TAPS * KT], F32R, at=at_tail + 12 * PU + 8 * S)
        dwl = place("dwl", [P, TAPS * KT])
        orow = place("orow", [P, ST, D], at=at_val)
        yT = place("yT", [P, KT, S], at=at_xg)
        assert max(where[0], arena + 8 * FT * S) <= nc.sbuf_usable_end, (where, nc.sbuf_usable_end)

        ps = ctx.enter_context(nc.psum_tensor("ps", [P, 8, 512], F32))

        landed = [sem("landed0"), sem("landed1")]
        hi_ready = sem("hi_ready")
        lo_ready = sem("lo_ready")
        chunk_done = sem("chunk_done")
        sum_done = sem("sum_done")
        tile_free = sem("tile_free")
        s_rows, s_mem, s_x, s_vb = sem("s_rows"), sem("s_mem"), sem("s_x"), sem("s_vb")
        s_const, s_zero, s_pool = sem("s_const"), sem("s_zero"), sem("s_pool")
        s_tr, s_cst = sem("s_tr"), sem("s_cst")
        m_ss, m_ms, m_inv, m_row = sem("m_ss"), sem("m_ms"), sem("m_inv"), sem("m_row")
        m_tr, m_g, m_hi, m_lo = sem("m_tr"), sem("m_g"), sem("m_hi"), sem("m_lo")
        lbc = sem("lbc")
        lbe = sem("lbe")
        x_tr = sem("x_tr")
        kv_done = sem("kv_done")
        x_upd = sem("x_upd")
        xg_ready, xg_hi, xg_lo = sem("xg_ready"), sem("xg_hi"), sem("xg_lo")
        sq_ready, sq_sum = sem("sq_ready"), sem("sq_sum")
        stat_done = sem("stat_done")
        ms_ready = sem("ms_ready")
        r_ready = sem("r_ready")
        xq_ready = sem("xq_ready")
        sc_done, mx_ready, p_exp, p_norm = sem("sc_done"), sem("mx_ready"), sem("p_exp"), sem("p_norm")
        p_inv = sem("p_inv")
        pt_done, pt_ready, xo_done, xo_hi, xo_lo = (sem("pt_done"), sem("pt_ready"), sem("xo_done"),
                                                    sem("xo_hi"), sem("xo_lo"))
        v_done = sem("v_done")
        hc_ready = sem("hc_ready")
        h_act = sem("h_act")
        k_ready = sem("k_ready")
        lv_ready, lv_done, lv_taken = sem("lv_ready"), sem("lv_done"), sem("lv_taken")
        f_ready = sem("f_ready")
        o_done, o_sq, o_stat, o_ms, o_inv = sem("o_done"), sem("o_sq"), sem("o_stat"), sem("o_ms"), sem("o_inv")
        o_gated, o_pre, o_mul, o_hi = sem("o_gated"), sem("o_pre"), sem("o_mul"), sem("o_hi")
        mix_lo = sem("mix_lo")
        mix_hi = sem("mix_hi")
        silu_ready = sem("silu_ready")
        act_step, act_lo = sem("act_step"), sem("act_lo")
        c_sig, c_u, c_uhi, c_ulo, c_tap, c_y = (sem("c_sig"), sem("c_u"), sem("c_uhi"), sem("c_ulo"), sem("c_tap"),
                                                sem("c_y"))
        c_dw, c_diag, c_pe = sem("c_dw"), sem("c_diag"), sem("c_pe")
        k_free, q_free = sem("k_free"), sem("q_free")
        c_sum = sem("c_sum")
        c_mid_pe, c_mid = sem("c_mid_pe"), sem("c_mid")
        c_cent, c_sq, c_sqs = sem("c_cent"), sem("c_sq"), sem("c_sqs")
        c_mu, c_var, c_less = sem("c_mu"), sem("c_var"), sem("c_less")
        c_act, c_norm = sem("c_act"), sem("c_norm")
        f_y, f_tr, f_row, f_row2, s_out = sem("f_y"), sem("f_tr"), sem("f_row"), sem("f_row2"), sem("s_out")

        block = ctx.enter_context(nc.Block())

        MS_AT = (3, 4, 6, 8, 9)
        HEADS_LOOP = (NH - 4) // 2

        def square_slot(k):
            return (sq if k % 4 < 2 else xgt)[:, k % 2, :]

        def tap_bank(r):
            return 5 if r == KT - 1 else 2 + r % 2

        def turn_bank(layer, h):
            return 6 if layer and h == XH - 1 else 4

        def at_chunk(base, i=0, k=0):
            return base + i * k, base // 2 + i * (k // 2), base % 2

        @block.sync
        def _(sp):
            def fetch(n, source, shape):
                num, par = n
                if not isinstance(source.offset, int):
                    sp.lower_val(source.offset * 4)
                if not (isinstance(num, int) and num < 2):
                    sp.wait_ge(lo_ready, num - 1)
                sp.dma_start(raw[:, par, :].rearrange("p (k c) -> p k c", c=shape), source).then_inc(landed[par], 16)

            def columns(w, c0):
                return w.rearrange("(k p) c -> p k c", p=P)[:, :, bass.ds(c0, P)]

            def rows(w, k0, c0):
                return w.rearrange("(k p) c -> p k c", p=P)[:, bass.ds(k0, 2), c0:c0 + 512]

            sp.dma_start(mrow[:, :, :], mem[0].rearrange("(t p) d -> p t d", p=P)).then_inc(s_mem, 16)
            for group, row, source, n in vec_rows:
                sp.dma_start(vrow[row:row + n, group, :], source).then_inc(s_rows, 16)
            for c in range(2 * XH):
                n = first["kv0"] + c
                if c < XH:
                    fetch((n, n % 2), columns(w_kv[0], c * P), P)
                else:
                    fetch((n, n % 2), rows(w_kv[0], 2 * (c - XH), XW), 512)
                if n == 1:
                    for t in range(ST):
                        sp.dma_start(xrow[:, t, :], x[0, t * P:(t + 1) * P, :]).then_inc(s_x, 16)
                    sp.dma_start(vbias[:, :], a_b[0:1, 2 * D:3 * D].partition_broadcast(P)[:, 0, :]).then_inc(s_vb, 16)
            for layer in range(2):
                if layer == 0:
                    n = first["xq0"]
                    for c in range(XH):
                        fetch((n + c, c % 2), columns(a_w[0], 4 * D + c * P), P)
                    n = first["val"]
                    for c in range(2 * GT):
                        fetch((n + c, c % 2), rows(a_w[0], 2 * (c % GT), 2 * D + 512 * (c // GT)), 512)
                    n = first["head"]
                    with sp.Fori(0, NH // 2) as i:
                        for h in range(2):
                            for j, kind in enumerate((1, 0, 3)):
                                c = 3 * h + j
                                fetch((n + c + i * 6, c % 2), columns(a_w[0], kind * D + h * P + i * (2 * P)), P)
                else:
                    for r in range(KT):
                        for pos, kind, c in rounds[r]:
                            n = first["mix1"] + pos
                            if kind == "V":
                                fetch((n, n % 2), rows(w_kv[1], 2 * c, XW), 512)
                            elif kind == "K":
                                fetch((n, n % 2), columns(w_kv[1], c * P), P)
                            else:
                                fetch((n, n % 2), columns(b_w[0], {"gate": D, "value": 0, "q": 2 * D}[kind] + c * P), P)
                n = first[f"out{layer}"]
                for c, (g, k) in enumerate(out_order[layer]):
                    fetch((n + c, c % 2), rows(w_out[layer], 2 * k, 512 * g), 512)
                n = first[f"gu{layer}"]
                with sp.Fori(0, FT) as i:
                    for j in range(2):
                        fetch((n + j + i * 2, j), columns(w_gu[layer], j * FH + i * P), P)
                n = first[f"down{layer}"]
                pairs = FT // 2
                with sp.Fori(0, (pairs - 1) // 2) as i:
                    for j in range(2):
                        fetch((n + j + i * 2, j), rows(w_down[layer], (2 * j) + i * 4, 0), 512)
                fetch((n + pairs - 1, 0), rows(w_down[layer], 2 * (pairs - 1), 0), 512)
                fetch((n + pairs, 1), rows(w_down[layer], 0, 512), 512)
                with sp.Fori(0, (pairs - 1) // 2) as i:
                    for j in range(2):
                        fetch((n + pairs + 1 + j + i * 2, j), rows(w_down[layer], 2 + (2 * j) + i * 4, 512), 512)
            for t in range(ST):
                sp.wait_ge(f_row, t + 1)
                sp.wait_ge(f_row2, t + 1)
                sp.dma_start(out[0, t * P:(t + 1) * P, :], orow[:, t, :]).then_inc(s_out, 16)
            sp.wait_ge(s_out, 16 * ST)

        @block.gpsimd
        def _(pool):
            step = [0]

            def link(ins):
                step[0] += 1
                ins.then_inc(s_pool, 1)
                pool.wait_ge(s_pool, step[0])

            link(nc.gpsimd.memset(ident[:, :], 1.0))
            link(nc.gpsimd.affine_select(out=ident[:, :], in_=ident[:, :], compare_op=ALU.is_equal, fill=0.0,
                                         base=0, pattern=[[-1, P]], channel_multiplier=1))
            nc.gpsimd.memset(ones[:, :], 1.0).then_inc(s_const, 1)
            link(nc.gpsimd.memset(mask[:, :, :], 0.0))
            link(nc.gpsimd.tensor_copy(mask[:, 0, :], ident[:, :]))
            for lv in range(1, MASKED):
                L = 1 << (lv - 1)
                nb = P // (2 * L)
                odd = mask[:, lv, :].rearrange("p (n two l) -> p n two l", two=2, l=L)[:, :, 1, :]
                link(nc.gpsimd.memset(odd, 1.0))
                link(nc.gpsimd.affine_select(out=odd, in_=odd, compare_op=ALU.is_ge, fill=0.0, base=0,
                                             pattern=[[-2 * L, nb], [0, L]], channel_multiplier=1))
                link(nc.gpsimd.affine_select(out=odd, in_=odd, compare_op=ALU.is_ge, fill=0.0, base=L - 1,
                                             pattern=[[2 * L, nb], [0, L]], channel_multiplier=-1))
            nc.gpsimd.memset(small[:, 127:128], 0.0).then_inc(s_const, 1)

            def sum_squares(norm, k0, k1):
                for k in range(max(k0, 1), k1):
                    pool.wait_ge(sq_ready, KT * norm + k + 1)
                    if k > 1:
                        pool.wait_ge(sq_sum, (KT - 1) * norm + k - 1)
                    nc.gpsimd.tensor_tensor(sqsum[:, :], sqsum[:, :], sq[:, k % 2, :], ALU.add).then_inc(sq_sum, 1)

            def lo(base, i=0, k=0):
                num, half, par = at_chunk(base, i, k)
                pool.wait_ge(hi_ready, num + 1)
                nc.gpsimd.tensor_tensor(wL[:, par, :], raw[:, par, :], wH[:, par, :].bitcast(F32),
                                        ALU.subtract).then_inc(lo_ready, 1)

            sum_squares(0, 0, KT)
            pool.wait_ge(xo_lo, XH)
            pool.wait_ge(xo_done, XH)
            nc.gpsimd.memset(att[:, :, :], 0.0).then_inc(s_zero, 1)
            n = first["head"]
            pool.wait_ge(lo_ready, n + 2)
            with pool.Fori(0, 3 * NH // 2) as i:
                lo(n + 2, i, 2)
                lo(n + 3, i, 2)
            sum_squares(1, 0, KT)
            pool.wait_ge(lo_ready, first["gu0"] + 2)
            lo(first["gu0"] + 2)
            sum_squares(2, 0, KT)
            nc.gpsimd.memset(upad[:, 0:PAD], 0.0)
            nc.gpsimd.memset(upad[:, PAD + S:PU], 0.0).then_inc(s_zero, 1)
            pool.wait_ge(lo_ready, first["mix1"] + 2)
            pool.wait_ge(c_dw, 1)

            def sum_tile(k):
                pool.wait_ge(c_y, k + 1)
                if k > 1:
                    pool.wait_ge(c_sum, k - 1)
                nc.gpsimd.tensor_tensor(ysum[:, :], (y[:, 0, :] if k == 1 else ysum[:, :]), y[:, k, :],
                                        ALU.add).then_inc(c_sum, 1)

            def centre_tile(k):
                pool.wait_ge(c_mid, 1)
                pool.wait_ge(c_sum, k)
                nc.gpsimd.tensor_tensor(y[:, k, :], y[:, k, :], mid[:, :], ALU.subtract).then_inc(c_cent, 1)

            def square_sum(k):
                pool.wait_ge(c_sq, k + 1)
                if k > 1:
                    pool.wait_ge(c_sqs, k - 1)
                nc.gpsimd.tensor_tensor(sqsum[:, :], (square_slot(0) if k == 1 else sqsum[:, :]), square_slot(k),
                                        ALU.add).then_inc(c_sqs, 1)

            def diagonals(r):
                if r >= 2:
                    pool.wait_ge(c_pe, r - 1)
                n = pe_taps[r]
                dH, dL = diags[2 if r == KT - 1 else r % 2]
                for dg, weights, at in ((dH, cst, col["dw"]), (dL, dwl, 0)):
                    w = weights[:, at:at + TAPS * KT].rearrange("p (t k) -> p t k", k=KT)[:, TAPS - n:, r:r + 1]
                    ins = nc.gpsimd.tensor_tensor(dg[:, 0:n, :], ident[:, :].unsqueeze(1).broadcast_to([P, n, P]),
                                                  w.broadcast_to([P, n, P]), ALU.mult)
                ins.then_inc(c_diag, 1)

            diagonals(0)
            for r in range(KT):
                for pos, kind, c in rounds[r]:
                    lo(first["mix1"] + pos + 2)
                    if kind == "gate" and 0 < r < KT - 1:
                        for k in centre[r - 1]:
                            if k:
                                square_sum(k)
                        for k in centre[r]:
                            centre_tile(k)
                if r >= 2:
                    sum_tile(r - 1)
                pool.wait_ge(c_uhi, r + 1)
                if r:
                    pool.wait_ge(c_pe, r)
                nc.gpsimd.tensor_tensor(upL[:, :], upad[:, :], upH[:, :].bitcast(F32), ALU.subtract).then_inc(c_ulo, 1)
                if r < KT - 1:
                    diagonals(r + 1)
            for k in centre[KT - 2]:
                square_sum(k)
            for k in centre[KT - 1]:
                centre_tile(k)
            for k in centre[KT - 1]:
                square_sum(k)
            sum_squares(3, 0, KT)
            pool.wait_ge(lo_ready, first["gu1"] + 2)
            lo(first["gu1"] + 2)
            sum_squares(4, 0, KT)

        @block.scalar
        def _(act):
            def hi(base, i=0, k=0):
                num, half, par = at_chunk(base, i, k)
                if isinstance(num, int) and num >= NCH:
                    return
                act.wait_ge(landed[par], half * 16 + 16)
                if not isinstance(num, int) or num >= 2:
                    act.wait_ge(chunk_done, num - 1)
                nc.scalar.activation(wH[:, par, :], raw[:, par, :], ACT.Copy).then_inc(hi_ready, 1)

            def prep(norm, k):
                done = KT * norm + k
                if norm < 4:
                    act.wait_ge(xg_ready, done + 1)
                    nc.scalar.activation(xgH[:, k, :], xgt[:, k % 2, :], ACT.Copy).then_inc(xg_hi, 1)
                else:
                    act.wait_ge(x_upd, done + 1)
                if k == 0:
                    if norm:
                        act.wait_ge(stat_done, norm)
                elif k >= 3:
                    act.wait_ge(sq_sum, (KT - 1) * norm + k - 2)
                nc.scalar.activation(sqsum[:, :] if k == 0 else sq[:, k % 2, :], xT[:, k, :],
                                     ACT.Square).then_inc(sq_ready, 1)

            def root(norm):
                act.wait_ge(ms_ready, norm + 1)
                if norm in (0, 4):
                    ins = nc.scalar.activation(small[:, 68:68 + ST], small[:, 64:64 + ST], ACT.Sqrt)
                if norm == 4:
                    ins.then_inc(r_ready, 1)
                    return
                nc.scalar.activation(rinv[:, :], msq[:, :], ACT.Sqrt).then_inc(r_ready, 1)

            def attn_exp(layer, h):
                a = XH * layer + h
                act.wait_ge(mx_ready, a + 1)
                if a:
                    act.wait_ge(pt_done, a)
                for t in range(ST):
                    ins = nc.scalar.activation(prob[:, t, :], ps[:, 6 + t // 2, (t % 2) * M:(t % 2 + 1) * M], ACT.Exp,
                                               bias=small[:, 80 + t:81 + t], scale=XSCALE,
                                               accum_out=small[:, 84 + t:85 + t])
                ins.then_inc(p_exp, 1)
                if layer:
                    act.wait_ge(p_inv, h + 1)
                    for t in range(ST):
                        ins = nc.scalar.activation(prob[:, t, :], prob[:, t, :], ACT.Copy, scale=small[:, 92 + t:93 + t])
                    ins.then_inc(p_norm, 1)

            def attn_pt(layer, h):
                a = XH * layer + h
                act.wait_ge(pt_done, a + 1)
                if a:
                    act.wait_ge(xo_done, a)
                nc.scalar.activation(probT[:, :, :], ps[:, turn_bank(layer, h):turn_bank(layer, h) + MT, :], ACT.Copy).then_inc(pt_ready, 1)

            def attn_out(layer, h):
                a = XH * layer + h
                act.wait_ge(xo_done, a + 1)
                nc.scalar.activation(mixH[:, KT + h, :], ps[:, turn_bank(layer, h), :], ACT.Copy).then_inc(xo_hi, 1)

            act.wait_ge(s_mem, 16)
            for t in range(MT):
                nc.scalar.activation(msc[:, t, :], mrow[:, t, :], ACT.Square,
                                     accum_out=small[:, t:t + 1]).then_inc(m_ss, 1)
            act.wait_ge(m_ms, 1)
            nc.scalar.activation(small[:, 4:4 + MT], small[:, 2:2 + MT], ACT.Sqrt).then_inc(m_inv, 1)
            for k in range(KT):
                act.wait_ge(m_g, k + 1)
                nc.scalar.activation(memH[:, k, :], memN[:, k, :], ACT.Copy).then_inc(m_hi, 1)
                if k in (1, KT - 2):
                    hi(int(k > 1))
            for c in range(2 * XH):
                hi(first["kv0"] + c + 2)
                if c:
                    prep(0, c - 1)
                if c == XH:
                    act.wait_ge(lbc, 3 + NLB)
                    nc.scalar.activation(small[:, 16:16 + NLB * NH], small[:, 16:16 + NLB * NH], ACT.Exp).then_inc(lbe, 1)
            prep(0, KT - 1)

            for layer in range(2):
                if layer == 0:
                    n = first["xq0"]
                    for c in range(XH):
                        hi(n + c + 2)
                        if c == 0:
                            root(0)
                        act.wait_ge(tile_free, tile0["xq0"] + c + 1)
                        b = col["a_b"] + 4 * KT + c
                        nc.scalar.activation(xq[:, c, :], evt[:, c % 2, :], ACT.Identity, bias=cst[:, b:b + 1]).then_inc(xq_ready, 1)
                    n = first["val"]
                    for h in range(XH):
                        attn_exp(0, h)
                        hi(n + 2 * h + 2)
                        attn_pt(0, h)
                        hi(n + 2 * h + 3)
                        attn_out(0, h)

                    def head_squares(h):
                        act.wait_ge(o_done, h + 1)
                        nc.scalar.activation(osq[:, :], ps[:, 4, :], ACT.Square).then_inc(o_sq, 1)

                    def head_root(h):
                        act.wait_ge(o_ms, 4 * h + 4)
                        nc.scalar.activation(oinv[:, :], oinv[:, :], ACT.Sqrt).then_inc(o_inv, 1)

                    def head(b, i=0, k=0):
                        h, q = b + i * k, b % 2
                        if b >= 3:
                            head_root(h - 3)
                        if b >= 2:
                            head_squares(h - 2)
                        for j, (func, dst, c) in enumerate(((ACT.Sigmoid, fb, 1), (ACT.Silu, qb, 0), (ACT.Silu, gb, 3))):
                            hi(first["head"] + 3 * b + j + 2, i, 3 * k)
                            if b >= 2 and j == 0:
                                act.wait_ge(lv_taken, (h - 1) * LV)
                            if b >= 2 and j == 2:
                                act.wait_ge(o_gated, h - 1)
                            if j == 0:
                                act.wait_ge(hc_ready, h + 1)
                            act.wait_ge(tile_free, tile0["head"] + 3 * h + j + 1)
                            nc.scalar.activation(dst[:, q, :], evt[:, (b + j) % 2, :], func,
                                                 bias=hc[:, q, c:c + 1]).then_inc(h_act, 1)

                    for h in range(4):
                        head(h)
                    with act.Fori(0, HEADS_LOOP) as i:
                        head(4, i, 2)
                        head(5, i, 2)
                else:
                    def query_bias(c):
                        act.wait_ge(q_free, c + 1)
                        b = col["b_b"] + 2 * KT + c
                        nc.scalar.activation(xq[:, c, :], xgt[:, c % 2, :], ACT.Identity, bias=cst[:, b:b + 1]).then_inc(xq_ready, 1)

                    def unit_hi(r):
                        act.wait_ge(c_u, r + 1)
                        if r:
                            act.wait_ge(c_pe, r)
                        nc.scalar.activation(upH[:, :], upad[:, :], ACT.Copy).then_inc(c_uhi, 1)

                    def square(k):
                        act.wait_ge(c_cent, k + 1)
                        if k >= 4:
                            act.wait_ge(c_sqs, max(k - 4, 1))
                        nc.scalar.activation(square_slot(k), y[:, k, :], ACT.Square).then_inc(c_sq, 1)

                    for r in range(KT):
                        for pos, kind, c in rounds[r]:
                            hi(first["mix1"] + pos + 2)
                            if kind == "gate" and r == MID + 1:
                                act.wait_ge(c_mid_pe, 1)
                                nc.scalar.activation(mid[:, :], ps[:, 3, :], ACT.Copy, scale=1.0 / (MID * P)).then_inc(c_mid, 1)
                            if kind == "gate" and r > XH:
                                attn_pt(1, r - XH - 1)
                            if r < XH and pos == rounds[r][3][0]:
                                unit_hi(r)
                            if kind == "K":
                                act.wait_ge(chunk_done, first["mix1"] + pos + 1)
                                nc.scalar.activation(KTs[1][:, c, :], ps[:, 6, 0:M], ACT.Copy).then_inc(k_free, 1)
                            if kind == "V" and c == XH - 1:
                                act.wait_ge(chunk_done, first["mix1"] + pos + 1)
                                nc.scalar.activation(VMs[1][:, :, :], ps[:, 4:4 + MT, :], ACT.Copy).then_inc(kv_done, 1)
                            if kind == "value":
                                if r == 0:
                                    root(2)
                                act.wait_ge(tile_free, tile0["mix1"] + 2 * r + 1)
                                if r:
                                    act.wait_ge(c_u, r)
                                b = col["b_b"] + KT + r
                                nc.scalar.activation(gate[:, :], evt[:, 0, :], ACT.Sigmoid, bias=cst[:, b:b + 1]).then_inc(c_sig, 1)
                                if 1 <= r <= XH:
                                    query_bias(r - 1)
                                if r >= XH:
                                    unit_hi(r)
                                if r > XH:
                                    attn_out(1, r - XH - 1)
                                if r >= XH:
                                    attn_exp(1, r - XH)
                                for k in centre[r]:
                                    square(k)

                def swish(k0, k1):
                    for k in range(k0, k1):
                        act.wait_ge(c_norm, k + 2)
                        if k >= 2:
                            act.wait_ge(mix_lo, NH + k - 1)
                        nc.scalar.activation(evt[:, k % 2, :], xgt[:, k % 2, :], ACT.Silu,
                                             scale=cst[:, col["lng"] + k:col["lng"] + k + 1],
                                             bias=cst[:, col["lnb"] + k:col["lnb"] + k + 1]).then_inc(c_act, 1)
                        act.wait_ge(c_act, k + 2)
                        nc.scalar.activation(mixH[:, k, :], evt[:, k % 2, :], ACT.Copy).then_inc(mix_hi, 1)

                n = first[f"out{layer}"]
                NG = MIXT // 2
                for c in range(2 * NG):
                    if layer == 0 and c == 0:
                        head_root(NH - 3)
                        head_squares(NH - 2)
                    if layer == 0 and c == 3:
                        head_root(NH - 2)
                        head_squares(NH - 1)
                        head_root(NH - 1)
                    if layer == 1 and c == 0:
                        attn_pt(1, XH - 1)
                        square(KT - 1)
                    if layer == 1 and c == 1:
                        swish(0, 2)
                    if c < 2 * NG - 1:
                        hi(n + c + 2)
                    if layer == 1 and c == 0:
                        attn_out(1, XH - 1)
                        act.wait_ge(c_norm, 1)
                        nc.scalar.activation(rsd[:, :], msq[:, :], ACT.Sqrt).then_inc(c_act, 1)
                    if layer == 1 and c == 1:
                        swish(2, 6)
                    if layer == 1 and c == 2:
                        swish(6, KT)
                    for k in {NG - 1: (0, 1), NG: (2, 3), 2 * NG - 1: range(GT, KT)}.get(c, ()):
                        prep(2 * layer + 1, k)
                    if c == 2 * NG - 1:
                        hi(n + c + 2)

                def ffn(b, i):
                    j = b + i
                    hi(first[f"gu{layer}"] + 2 * b + 2, i, 2)
                    if b == 0:
                        root(2 * layer + 1)
                    act.wait_ge(tile_free, tile0[f"gu{layer}"] + 2 * j + 1)
                    if b or layer:
                        act.wait_ge(act_step, 2 * (FT * layer + j) - 1)
                    nc.scalar.activation(xgt[:, 0, :], evt[:, 0, :], ACT.Silu).then_inc(silu_ready, 1)
                    hi(first[f"gu{layer}"] + 2 * b + 3, i, 2)

                ffn(0, 0)
                with act.Fori(0, FT - 1) as i:
                    ffn(1, i)

                n = first[f"down{layer}"]
                pairs = FT // 2
                norm = 2 * layer + 2
                with act.Fori(0, (pairs - 1) // 2) as i:
                    hi(n + 2, i, 2)
                    hi(n + 3, i, 2)
                hi(n + pairs - 1 + 2)
                prep(norm, 0)
                prep(norm, 1)
                hi(n + pairs + 2)
                prep(norm, 2)
                prep(norm, 3)
                with act.Fori(0, (pairs - 3) // 2) as i:
                    hi(n + pairs + 1 + 2, i, 2)
                    hi(n + pairs + 2 + 2, i, 2)
                hi(n + 2 * pairs)
                for k in range(GT, KT):
                    prep(norm, k)
                hi(n + 2 * pairs + 1)
                if layer == 0:
                    for m in range(0, KT, KT // 2):
                        nc.scalar.activation(memH[:, m:m + KT // 2, :], memN[:, m:m + KT // 2, :],
                                             ACT.Copy).then_inc(m_hi, KT // 2)
            root(4)
            act.wait_ge(r_ready, 5)
            for t in range(ST):
                act.wait_ge(f_tr, KT)
                nc.scalar.activation(orow[:, t, GT * P:].rearrange("p (k c) -> p k c", c=P), ps[:, GT:KT, t * P:(t + 1) * P],
                                     ACT.Copy, scale=small[:, 68 + t:69 + t]).then_inc(f_row2, 1)

        @block.vector
        def _(dve):
            V = nc.vector
            own = [0]

            def link(ins):
                own[0] += 1
                ins.then_inc(lbc, 1)
                dve.wait_ge(lbc, own[0])

            def lo(base, i=0, k=0):
                num, half, par = at_chunk(base, i, k)
                if isinstance(num, int) and num >= NCH:
                    return
                dve.wait_ge(hi_ready, num + 1)
                V.tensor_tensor(wL[:, par, :], raw[:, par, :], wH[:, par, :].bitcast(F32),
                                ALU.subtract).then_inc(lo_ready, 1)

            def gain(norm, k):
                done = KT * norm + k
                if norm == 4:
                    dve.wait_ge(x_upd, done + 1)
                    V.tensor_scalar(yT[:, k, :], xT[:, k, :], cst[:, col["fin"] + k:col["fin"] + k + 1], None,
                                    ALU.mult).then_inc(f_y, 1)
                    return
                name = ("mix0", "ffn0", "mix1", "ffn1")[norm]
                dve.wait_ge(x_upd, done + 1)
                if done >= 2:
                    dve.wait_ge(xg_hi, done - 1)
                    dve.wait_ge(xg_lo, done - 1)
                V.tensor_scalar(xgt[:, k % 2, :], xT[:, k, :], cst[:, col[name] + k:col[name] + k + 1], None,
                                ALU.mult).then_inc(xg_ready, 1)

            def gain_lo(norm, k):
                if norm == 4:
                    return
                dve.wait_ge(xg_hi, KT * norm + k + 1)
                V.tensor_tensor(xgL[:, k, :], xgt[:, k % 2, :], xgH[:, k, :].bitcast(F32),
                                ALU.subtract).then_inc(xg_lo, 1)

            def renew(norm, ks, last):
                for k in ks:
                    if k % GT < GT - 1:
                        dve.wait_ge(sum_done, (GT - 1) * (2 * (norm - 1) + k // GT) + k % GT + 1)
                    else:
                        dve.wait_ge(chunk_done, last)
                    V.tensor_tensor(xT[:, k, :], ps[:, k, :], xT[:, k, :], ALU.add).then_inc(x_upd, 1)
                    gain(norm, k)
                    if k > ks[0]:
                        gain_lo(norm, k - 1)
                gain_lo(norm, ks[-1])

            def mean_square(norm):
                dve.wait_ge(stat_done, norm + 1)
                if norm in (0, 4):
                    link(V.tensor_scalar(small[:, 64:64 + ST], ps[:, 7 if norm else 3, 0:ST], 1.0 / D, EPS, ALU.mult, ALU.add))
                    ins = V.reciprocal(small[:, 64:64 + ST], small[:, 64:64 + ST])
                if norm == 4:
                    ins.then_inc(ms_ready, 1)
                    return
                link(V.tensor_scalar(msq[:, :], ps[:, 4 if norm == 2 else 2, :], 1.0 / D, EPS, ALU.mult, ALU.add))
                V.reciprocal(msq[:, :], msq[:, :]).then_inc(ms_ready, 1)

            def scaled(par):
                return V.tensor_tensor(evt[:, par, :], ps[:, par, :], rinv[:, :], ALU.mult)

            def attn_max(layer, h):
                a = XH * layer + h
                dve.wait_ge(sc_done, a + 1)
                link(V.reduce_max(small[:, 88:88 + ST], ps[:, 6:8, :].rearrange("p b (t m) -> p (b t) m", m=M), AX_X))
                V.tensor_scalar(small[:, 80:80 + ST], small[:, 88:88 + ST], -XSCALE, None,
                                ALU.mult).then_inc(mx_ready, 1)

            def attn_norm(layer, h):
                a = XH * layer + h
                dve.wait_ge(p_exp, a + 1)
                if layer:
                    V.reciprocal(small[:, 92:92 + ST], small[:, 84:84 + ST]).then_inc(p_inv, 1)
                    return
                link(V.reciprocal(small[:, 92:92 + ST], small[:, 84:84 + ST]))
                V.tensor_tensor(prob[:, :, :], prob[:, :, :],
                                small[:, 92:92 + ST].unsqueeze(2).broadcast_to([P, ST, M]),
                                ALU.mult).then_inc(p_norm, 1)

            def attn_lo(layer, h):
                a = XH * layer + h
                dve.wait_ge(xo_hi, a + 1)
                V.tensor_tensor(mixL[:, KT + h, :], ps[:, turn_bank(layer, h), :], mixH[:, KT + h, :].bitcast(F32),
                                ALU.subtract).then_inc(xo_lo, 1)

            dve.wait_ge(m_ss, MT)
            link(V.tensor_scalar(small[:, 2:2 + MT], small[:, 0:MT], 1.0 / D, EPS, ALU.mult, ALU.add))
            V.reciprocal(small[:, 2:2 + MT], small[:, 2:2 + MT]).then_inc(m_ms, 1)
            dve.wait_ge(s_tr, 1)
            V.tensor_copy(cst[:, :], ps[:, 3, 0:NCOL]).then_inc(s_cst, 1)
            dve.wait_ge(m_inv, 1)
            for t in range(MT):
                V.tensor_scalar(mrow[:, t, :], mrow[:, t, :], small[:, 4 + t:5 + t], None, ALU.mult).then_inc(m_row, 1)
            dve.wait_ge(s_cst, 1)

            def memory_lo(k):
                dve.wait_ge(m_hi, k + 1)
                V.tensor_tensor(memL[:, k, :], memN[:, k, :], memH[:, k, :].bitcast(F32), ALU.subtract).then_inc(m_lo, 1)

            for k in range(KT):
                dve.wait_ge(m_tr, k + 1)
                V.tensor_scalar(memN[:, k, :], ps[:, 4 + k % 4, 0:M], cst[:, col["mem"] + k:col["mem"] + k + 1],
                                None, ALU.mult).then_inc(m_g, 1)
                if k:
                    memory_lo(k - 1)
                if k == 2:
                    lo(0)
            memory_lo(KT - 1)
            lo(1)
            for c in range(2 * XH):
                n = first["kv0"] + c
                lo(n + 2)
                dve.wait_ge(chunk_done, n + 1)
                if c < XH:
                    V.tensor_copy(KTs[0][:, c, :], ps[:, c % 2, 0:M]).then_inc(tile_free, 1)
                elif c == 2 * XH - 1:
                    V.tensor_copy(VMs[0][:, :, :], ps[:, 4:4 + MT, :]).then_inc(kv_done, 1)
                dve.wait_ge(x_tr, c + 1)
                V.tensor_copy(xT[:, c, :], ps[:, 2 + c % 2, :]).then_inc(x_upd, 1)
                gain(0, c)
                if c:
                    gain_lo(0, c - 1)
                if c == XH - 1:
                    table = [cst[:, col[f"lb{r}"]:col[f"lb{r}"] + NH] for r in range(NLB)]
                    shifted = small[:, 16:16 + NLB * NH].rearrange("p (r h) -> p r h", h=NH)
                    top = small[:, 8:8 + NH]
                    link(V.tensor_tensor(top, table[0], table[1], ALU.max))
                    link(V.tensor_tensor(top, top, table[2], ALU.max))
                    for r in range(NLB):
                        link(V.tensor_tensor(shifted[:, r, :], table[r], top, ALU.subtract))
                if c == XH:
                    dve.wait_ge(lbe, 1)
                    link(V.tensor_tensor(top, shifted[:, 0, :], shifted[:, 1, :], ALU.add))
                    link(V.tensor_tensor(top, top, shifted[:, 2, :], ALU.add))
                    link(V.reciprocal(top, top))
                    link(V.tensor_tensor(headc[:, 4, :], shifted[:, 0, :], top, ALU.mult))
                    link(V.tensor_scalar(headc[:, 5, :], headc[:, 4, :], -1.0, 1.0, ALU.mult, ALU.add))
                    link(V.tensor_copy(headc[:, 0:4, :], cst[:, col["a_b"]:col["a_b"] + 4 * NH].rearrange("p (k h) -> p k h", h=NH)))
                if c == XH + 1:
                    link(V.tensor_copy(dwh[:, :], cst[:, col["dw"]:col["dw"] + TAPS * KT]))
                    V.tensor_tensor(dwl[:, :], cst[:, col["dw"]:col["dw"] + TAPS * KT], dwh[:, :].bitcast(F32), ALU.subtract).then_inc(c_dw, 1)
            gain_lo(0, KT - 1)

            for layer in range(2):
                if layer == 0:
                    n = first["xq0"]
                    for c in range(XH):
                        lo(n + c + 2)
                        if c == 0:
                            mean_square(0)
                            dve.wait_ge(r_ready, 1)
                        if c >= 2:
                            dve.wait_ge(xq_ready, c - 1)
                        dve.wait_ge(chunk_done, n + c + 1)
                        scaled(c % 2).then_inc(tile_free, 1)
                    n = first["val"]
                    dve.wait_ge(s_vb, 16)
                    for h in range(XH):
                        attn_max(0, h)
                        attn_norm(0, h)
                        lo(n + 2 * h + 2)
                        lo(n + 2 * h + 3)
                        c = 2 * h + 1
                        if c % GT == GT - 1:
                            dve.wait_ge(chunk_done, n + c + 1)
                            for t in range(ST):
                                V.scalar_tensor_tensor(out=val[:, t, 512 * (c // GT):512 * (c // GT + 1)], in0=ps[:, t, :],
                                                       scalar=small[:, 68 + t:69 + t],
                                                       in1=vbias[:, 512 * (c // GT):512 * (c // GT + 1)],
                                                       op0=ALU.mult, op1=ALU.add).then_inc(v_done, 1)
                        attn_lo(0, h)

                    def sums(lv):
                        o = sum(S >> m for m in range(1, lv))
                        return tb[:, o:o + (S >> lv)]

                    def level(lv, h, q):
                        if lv == 0:
                            dve.wait_ge(s_zero, 1)
                        else:
                            dve.wait_ge(lv_taken, h * LV + lv)
                        dve.wait_ge(lv_done, h * LV + lv + 1)
                        A, B = qb[:, q, :], kb[:, q, :]
                        if lv == 0:
                            V.tensor_tensor(A, A, fb[:, q, :], ALU.mult).then_inc(lv_ready, 1)
                        elif lv <= 8:
                            L = 1 << (lv - 1)
                            nb = S // (2 * L)
                            T = (fb[:, q, :] if lv == 1 else sums(lv - 1)).rearrange("p (n two) -> p n two", two=2)
                            Ao = A.rearrange("p (n two l) -> p n two l", two=2, l=L)[:, :, 1, :]
                            Be = B.rearrange("p (n two l) -> p n two l", two=2, l=L)[:, :, 0, :]
                            V.tensor_tensor(Ao, Ao, T[:, :, 0:1].broadcast_to([P, nb, L]), ALU.mult)
                            ins = V.tensor_tensor(Be, Be, T[:, :, 1:2].broadcast_to([P, nb, L]), ALU.mult)
                            if lv <= 7:
                                ins = V.tensor_tensor(sums(lv), T[:, :, 0], T[:, :, 1], ALU.mult)
                            ins.then_inc(lv_ready, 1)
                        bank = ps[:, 6 + lv % 2, :]
                        if lv < MASKED:
                            V.copy_predicated(att_view(0, ST * P + P, ST), mask[:, lv, :].bitcast(U32).unsqueeze(1).broadcast_to([P, ST, P]),
                                              bank.rearrange("p (b t) -> p b t", t=P)).then_inc(lv_taken, 1)
                        elif lv == MASKED:
                            V.tensor_copy(att_view(P, 2 * (S + P), 2), bank[:, 0:2 * P].rearrange("p (b t) -> p b t", t=P)).then_inc(lv_taken, 1)
                        else:
                            V.tensor_copy(att[:, 0:2, 2 * P:4 * P], bank.rearrange("p (b t) -> p b t", t=2 * P)).then_inc(lv_taken, 1)

                    def att_view(offset, step, count):
                        return bass.AP(tensor=att[:, :, :].tensor, offset=offset, ap=[[ST * S, P], [step, count], [1, P]])

                    def out_gate(h, q, first_head):
                        dve.wait_ge(o_sq, h + 1)
                        dve.wait_ge(h_act, 3 * h + 3)
                        if not first_head:
                            dve.wait_ge(mix_lo, h)
                        V.scalar_tensor_tensor(out=mixt[:, :], in0=ps[:, 4, :], scalar=cst[:, col["a_on"]:col["a_on"] + 1],
                                               in1=gb[:, q, :], op0=ALU.mult, op1=ALU.mult).then_inc(o_gated, 1)

                    def out_ms(h, first_head, part):
                        if part == 0:
                            dve.wait_ge(o_stat, h + 1)
                            if not first_head:
                                dve.wait_ge(o_mul, h)
                            V.tensor_scalar(oinv[:, :], ps[:, 5, :], 1.0 / P, EPS, ALU.mult, ALU.add).then_inc(o_pre, 1)
                            return
                        dve.wait_ge(o_pre, h + 1)
                        quarter = oinv[:, (part - 1) * P:part * P]
                        V.reciprocal(quarter, quarter).then_inc(o_ms, 1)

                    def out_split(h, step):
                        if step == 0:
                            dve.wait_ge(o_inv, h + 1)
                            dve.wait_ge(o_gated, h + 1)
                            V.tensor_tensor(mixt[:, :], mixt[:, :], oinv[:, :], ALU.mult).then_inc(o_mul, 1)
                        if step == 1:
                            dve.wait_ge(o_mul, h + 1)
                            V.tensor_scalar(mixH[:, bass.ds(h, 1), :], mixt[:, :].unsqueeze(1), 1.0, None, ALU.mult).then_inc(o_hi, 1)
                        if step == 2:
                            dve.wait_ge(o_hi, h + 1)
                            V.tensor_tensor(mixL[:, bass.ds(h, 1), :], mixt[:, :].unsqueeze(1),
                                            mixH[:, bass.ds(h, 1), :].bitcast(F32), ALU.subtract).then_inc(mix_lo, 1)

                    def beside_level(lv, h, b):
                        if b >= 3 and lv < 3:
                            out_split(h - 3, lv)
                        if b >= 2 and lv == 7:
                            out_gate(h - 2, b % 2, b == 2)
                        if b >= 2 and lv in MS_AT:
                            out_ms(h - 2, b == 2, MS_AT.index(lv))

                    def head(b, i=0, k=0):
                        h, q = b + i * k, b % 2
                        if b >= 2:
                            dve.wait_ge(h_act, 3 * h - 3)
                        V.tensor_scalar(hc[:, q, :].unsqueeze(2), headc[:, :, bass.ds(h, 1)], 1.0, None, ALU.mult).then_inc(hc_ready, 1)
                        if b == 0:
                            dve.wait_ge(xq_ready, XH)
                            dve.wait_ge(v_done, 2 * ST)
                        for j in range(3):
                            for lv in range(4 * j, min(4 * j + 4, LV)) if b else ():
                                level(lv, h - 1, 1 - q)
                                beside_level(lv, h, b)
                                if lv == 5:
                                    forget(h, q)
                            if 3 * b + j >= 2:
                                dve.wait_ge(h_act, 3 * h + j - 1)
                            dve.wait_ge(chunk_done, first["head"] + 3 * h + j + 1)
                            scaled((b + j) % 2).then_inc(tile_free, 1)
                            if b == 0 and j == 1:
                                forget(h, q)
                        V.tensor_scalar(vh[:, q, :, :], val[:, :, bass.ds(h * P, P)], 1.0, None, ALU.mult).then_inc(k_ready, 1)

                    def forget(h, q):
                        dve.wait_ge(hc_ready, h + 1)
                        dve.wait_ge(h_act, 3 * h + 1)
                        V.tensor_scalar(fb[:, q, :], fb[:, q, :], hc[:, q, 5:6], hc[:, q, 4:5], ALU.mult, ALU.add).then_inc(f_ready, 1)
                        dve.wait_ge(f_ready, h + 1)
                        V.tensor_scalar(kb[:, q, :], fb[:, q, :], -1.0, 1.0, ALU.mult, ALU.add)

                    for h in range(4):
                        head(h)
                    with dve.Fori(0, HEADS_LOOP) as i:
                        head(4, i, 2)
                        head(5, i, 2)
                else:
                    tapped = [0]

                    def taps(r, t0, t1):
                        for t in range(t0, t1):
                            w = cst[:, col["dw"] + t * KT + r:col["dw"] + t * KT + r + 1]
                            u = upad[:, t:t + S]
                            if t == 0:
                                b = col["dwb"] + r
                                ins = V.tensor_scalar(y[:, r, :], u, w, cst[:, b:b + 1], ALU.mult, ALU.add)
                            elif t == 1:
                                ins = V.tensor_scalar(y2[:, :], u, w, None, ALU.mult)
                            else:
                                dve.wait_ge(c_tap, tapped[0] - 1)
                                to = y2[:, :] if t % 2 else y[:, r, :]
                                ins = V.scalar_tensor_tensor(out=to, in0=u, scalar=w, in1=to, op0=ALU.mult, op1=ALU.add)
                            ins.then_inc(c_tap, 1)
                            tapped[0] += 1

                    def add_taps(r):
                        dve.wait_ge(c_tap, tapped[0])
                        dve.wait_ge(c_pe, r + 1)
                        V.tensor_tensor(y[:, r, :], ps[:, tap_bank(r), :], y[:, r, :], ALU.add).then_inc(c_y, 1)

                    dve.wait_ge(m_hi, 2 * KT)
                    V.tensor_tensor(memL[:, :, :], memN[:, :, :], memH[:, :, :].bitcast(F32), ALU.subtract).then_inc(m_lo, KT)
                    mean_square(2)
                    dve.wait_ge(r_ready, 3)
                    dve.wait_ge(silu_ready, FT)
                    dve.wait_ge(s_zero, 2)
                    for r in range(KT):
                        n = first["mix1"] + rounds[r][0][0]
                        last = TAPS - pe_taps[r]
                        if r:
                            dve.wait_ge(c_sig, r)
                            dve.wait_ge(c_u, r)
                        dve.wait_ge(chunk_done, n + 1)
                        scaled(0).then_inc(tile_free, 1)
                        dve.wait_ge(chunk_done, n + 2)
                        scaled(1).then_inc(tile_free, 1)
                        if r >= XH:
                            add_taps(r - 1)
                        dve.wait_ge(c_sig, r + 1)
                        dve.wait_ge(tile_free, tile0["mix1"] + 2 * r + 2)
                        if r:
                            dve.wait_ge(c_ulo, r)
                        b = col["b_b"] + r
                        V.scalar_tensor_tensor(out=upad[:, PAD:PAD + S], in0=evt[:, 1, :], scalar=cst[:, b:b + 1],
                                               in1=gate[:, :], op0=ALU.add, op1=ALU.mult).then_inc(c_u, 1)
                        dve.wait_ge(c_u, r + 1)
                        taps(r, 0, 4)
                        if r >= XH:
                            attn_max(1, r - XH)
                        taps(r, 4, 8)
                        if 0 < r < XH:
                            add_taps(r - 1)
                        if r > XH:
                            attn_lo(1, r - XH - 1)
                        if r >= XH:
                            attn_norm(1, r - XH)
                        taps(r, 8, last)
                        dve.wait_ge(c_tap, tapped[0])
                        V.tensor_tensor(y[:, r, :], y[:, r, :], y2[:, :], ALU.add).then_inc(c_tap, 1)
                        tapped[0] += 1
                        for pos, kind, c in rounds[r]:
                            if kind == "q":
                                dve.wait_ge(chunk_done, first["mix1"] + pos + 1)
                                if c >= 2:
                                    dve.wait_ge(xq_ready, XH + c - 1)
                                V.tensor_tensor(xgt[:, c % 2, :], ps[:, 7, :], rinv[:, :], ALU.mult).then_inc(q_free, 1)

                def less(k):
                    V.tensor_tensor(y[:, k, :], y[:, k, :], mu[:, :], ALU.subtract).then_inc(c_less, 1)

                def mixed_lo(k):
                    dve.wait_ge(mix_hi, k + 1)
                    V.tensor_tensor(mixL[:, k, :], evt[:, k % 2, :], mixH[:, k, :].bitcast(F32),
                                    ALU.subtract).then_inc(mix_lo, 1)

                def normed(k0, k1):
                    for k in range(k0, k1):
                        if k >= 2:
                            dve.wait_ge(c_act, k)
                        dve.wait_ge(c_less, k + 1)
                        V.tensor_tensor(xgt[:, k % 2, :], y[:, k, :], rsd[:, :], ALU.mult).then_inc(c_norm, 1)
                        if k + 3 < KT:
                            less(k + 3)
                        if k >= 1:
                            mixed_lo(k - 1)

                n = first[f"out{layer}"]
                NG = MIXT // 2
                for c in range(2 * NG):
                    if layer == 0 and c < 3:
                        for lv in range(4 * c, min(4 * c + 4, LV)):
                            level(lv, NH - 1, (NH - 1) % 2)
                            beside_level(lv, NH, NH)
                    if layer == 0 and c == 3:
                        for step in range(3):
                            out_split(NH - 2, step)
                        out_gate(NH - 1, (NH - 1) % 2, False)
                        for part in range(5):
                            out_ms(NH - 1, False, part)
                        for step in range(3):
                            out_split(NH - 1, step)
                    if layer == 1 and c == 0:
                        add_taps(KT - 1)
                        dve.wait_ge(c_y, KT)
                        dve.wait_ge(c_sum, KT - 2)
                        V.tensor_tensor(ysum[:, :], ysum[:, :], y[:, KT - 1, :], ALU.add).then_inc(c_sum, 1)
                        dve.wait_ge(c_sum, KT - 1)
                        dve.wait_ge(c_sq, KT - 1)
                        V.tensor_tensor(y[:, KT - 1, :], y[:, KT - 1, :], mid[:, :], ALU.subtract).then_inc(c_cent, 1)
                        dve.wait_ge(c_sq, KT)
                        dve.wait_ge(c_sqs, KT - 2)
                        V.tensor_tensor(sqsum[:, :], sqsum[:, :], square_slot(KT - 1), ALU.add).then_inc(c_sqs, 1)
                        attn_lo(1, XH - 1)
                        dve.wait_ge(c_mu, 1)
                        link(V.scalar_tensor_tensor(out=mu[:, :], in0=ps[:, 5, :], scalar=1.0 / D, in1=mid[:, :],
                                                    op0=ALU.mult, op1=ALU.subtract))
                        link(V.tensor_tensor(msq[:, :], mu[:, :], mu[:, :], ALU.mult))
                        dve.wait_ge(c_var, 1)
                        link(V.scalar_tensor_tensor(out=msq[:, :], in0=ps[:, 4, :], scalar=1.0 / D, in1=msq[:, :],
                                                    op0=ALU.mult, op1=ALU.subtract))
                        link(V.tensor_scalar(msq[:, :], msq[:, :], 0.0, EPS, ALU.max, ALU.add))
                        V.reciprocal(msq[:, :], msq[:, :]).then_inc(c_norm, 1)
                        less(0)
                    if layer == 1 and c == 1:
                        less(1)
                        less(2)
                        dve.wait_ge(c_act, 1)
                        normed(0, 2)
                    if c == 0:
                        dve.wait_ge(lo_ready, n + c + 2)
                    if c < 2 * NG - 1:
                        lo(n + c + 2)
                    if layer == 1 and c == 1:
                        normed(2, 6)
                    if layer == 1 and c == 2:
                        normed(6, KT)
                        mixed_lo(KT - 1)
                    ks = {NG - 1: (0, 1), NG: (2, 3), 2 * NG - 1: tuple(range(GT, KT))}.get(c)
                    if ks:
                        renew(2 * layer + 1, ks, n + (NG if ks[0] < GT else 2 * NG))
                    if c == 2 * NG - 1:
                        lo(n + c + 2)

                def ffn(b, i):
                    j = b + i
                    m = FT * layer + j
                    if b:
                        lo(first[f"gu{layer}"] + 2 * b + 2, i, 2)
                    if b == 0:
                        mean_square(2 * layer + 1)
                        dve.wait_ge(r_ready, 2 * layer + 2)
                        if layer == 0:
                            dve.wait_ge(h_act, 3 * NH)
                        else:
                            dve.wait_ge(mix_hi, KT)
                    else:
                        dve.wait_ge(silu_ready, m)
                    dve.wait_ge(chunk_done, first[f"gu{layer}"] + 2 * j + 1)
                    scaled(0).then_inc(tile_free, 1)
                    if b == 0:
                        dve.wait_ge(lo_ready, first[f"gu{layer}"] + 3)
                    lo(first[f"gu{layer}"] + 2 * b + 3, i, 2)
                    dve.wait_ge(chunk_done, first[f"gu{layer}"] + 2 * j + 2)
                    scaled(1).then_inc(tile_free, 1)
                    dve.wait_ge(silu_ready, m + 1)
                    dve.wait_ge(tile_free, tile0[f"gu{layer}"] + 2 * j + 2)
                    V.tensor_tensor(xgt[:, 1, :], evt[:, 1, :], xgt[:, 0, :], ALU.mult).then_inc(act_step, 1)
                    dve.wait_ge(act_step, 2 * m + 1)
                    V.tensor_scalar(actH[:, bass.ds(j, 1), :], xgt[:, 1, :].unsqueeze(1), 1.0, None, ALU.mult).then_inc(act_step, 1)
                    dve.wait_ge(act_step, 2 * m + 2)
                    V.tensor_tensor(actL[:, bass.ds(j, 1), :], xgt[:, 1, :].unsqueeze(1), actH[:, bass.ds(j, 1), :].bitcast(F32),
                                    ALU.subtract).then_inc(act_lo, 1)
                    dve.wait_ge(act_lo, m + 1)

                ffn(0, 0)
                with dve.Fori(0, FT - 1) as i:
                    ffn(1, i)

                n = first[f"down{layer}"]
                pairs = FT // 2
                norm = 2 * layer + 2
                with dve.Fori(0, (pairs - 1) // 2) as i:
                    lo(n + 2, i, 2)
                    lo(n + 3, i, 2)
                lo(n + pairs - 1 + 2)
                renew(norm, (0, 1), n + pairs)
                lo(n + pairs + 2)
                renew(norm, (2, 3), n + pairs)
                with dve.Fori(0, (pairs - 3) // 2) as i:
                    lo(n + pairs + 1 + 2, i, 2)
                    lo(n + pairs + 2 + 2, i, 2)
                lo(n + 2 * pairs)
                renew(norm, tuple(range(GT, KT)), n + 2 * pairs)
                lo(n + 2 * pairs + 1)
            mean_square(4)
            dve.wait_ge(r_ready, 5)
            for t in range(ST):
                V.tensor_scalar(orow[:, t, 0:GT * P].rearrange("p (k c) -> p k c", c=P), ps[:, 0:GT, t * P:(t + 1) * P],
                                small[:, 68 + t:69 + t], None, ALU.mult).then_inc(f_row, 1)

        @block.tensor
        def _(pe):
            mm = nc.tensor.matmul

            def exact(out_ap, left, right, start, stop):
                mm(out_ap, left[0], right[0], start=start, stop=False)
                mm(out_ap, left[0], right[1], start=False, stop=False)
                return mm(out_ap, left[1], right[0], start=False, stop=stop)

            def tile_chunk(base, number, i=0, k=0, other=None, width=S, between=None, ready=None, bank=None):
                num, half, par = at_chunk(base, i, k)
                H, L = other or (xgH, xgL)
                if number is not None and (not isinstance(number, int) or number >= 2):
                    pe.wait_ge(tile_free, number - 1)
                bank = par if bank is None else bank
                pe.wait_ge(lo_ready, num + 1)
                for kt in range(KT):
                    if ready is not None:
                        pe.wait_ge(m_lo if other else xg_lo, KT * ready + kt + 1)
                    w = slice(kt * P, (kt + 1) * P)
                    ins = exact(ps[:, bank, 0:width], (wH[:, par, w], wL[:, par, w]), (H[:, kt, :], L[:, kt, :]),
                                kt == 0, kt == KT - 1)
                    if kt == KT - 1:
                        ins.then_inc(chunk_done, 1)
                    if between is not None:
                        between(kt)

            def group_chunk(base, bank, acts, start, stop, i=0, k=0, between=None, free=None):
                num, half, par = at_chunk(base, i, k)
                pe.wait_ge(lo_ready, num + 1)
                if stop:
                    right = [acts(0), acts(1)]
                    for t in range(GT):
                        for kk in range(2):
                            w = slice(kk * 512 + t * P, kk * 512 + (t + 1) * P)
                            ins = exact(ps[:, bank + t, :], (wH[:, par, w], wL[:, par, w]), right[kk], False, kk == 1)
                        ins.then_inc(sum_done if t < GT - 1 else chunk_done, 1)
                    return
                order = [(kk, t) for kk in range(2) for t in range(GT)]
                if free is not None:
                    order = [(kk, t) for banks in ((2, 3, 0), (1,)) for kk in range(2) for t in banks]
                right = [None, None]
                for step, (kk, t) in enumerate(order):
                    right[kk] = right[kk] or acts(kk)
                    if free is not None and kk == 0 and t < 2:
                        pe.wait_ge(tile_free, free - 1 + t)
                    w = slice(kk * 512 + t * P, kk * 512 + (t + 1) * P)
                    ins = exact(ps[:, bank + t, :], (wH[:, par, w], wL[:, par, w]), right[kk],
                                start and kk == 0, False)
                    if step == 2 * GT - 1:
                        ins.then_inc(chunk_done, 1)
                    if between is not None and step % 2:
                        between(step // 2)

            def stat(norm):
                pe.wait_ge(sq_sum, (KT - 1) * (norm + 1))
                if norm in (0, 4):
                    for t in range(ST):
                        ins = mm(ps[:, 7 if norm else 3, t:t + 1], sqsum[:, t * P:(t + 1) * P], ones[:, 0:1], start=True, stop=True)
                if norm == 4:
                    ins.then_inc(stat_done, 1)
                    return
                mm(ps[:, 4 if norm == 2 else 2, :], ones[:, :], sqsum[:, :], start=True, stop=True).then_inc(stat_done, 1)

            def turn_back(k):
                for t in range(ST):
                    ins = nc.tensor.transpose(ps[:, k, t * P:(t + 1) * P], yT[:, k, t * P:(t + 1) * P], ident[:, :])
                ins.then_inc(f_tr, 1)

            def attn_scores(layer, h):
                a = XH * layer + h
                pe.wait_ge(xq_ready, a + 1)
                if a:
                    pe.wait_ge(p_norm, a)
                for t in range(ST):
                    ins = mm(ps[:, 6 + t // 2, (t % 2) * M:(t % 2 + 1) * M], xq[:, h, t * P:(t + 1) * P], KTs[layer][:, h, :],
                             start=True, stop=True)
                ins.then_inc(sc_done, 1)

            def attn_turn(layer, h):
                a = XH * layer + h
                pe.wait_ge(p_norm, a + 1)
                if a:
                    pe.wait_ge(xo_lo, a)
                for m in range(MT):
                    for t in range(ST):
                        ins = nc.tensor.transpose(ps[:, turn_bank(layer, h) + m, t * P:(t + 1) * P], prob[:, t, m * P:(m + 1) * P], ident[:, :])
                ins.then_inc(pt_done, 1)

            def attn_values(layer, h):
                a = XH * layer + h
                pe.wait_ge(pt_ready, a + 1)
                for m in range(MT):
                    ins = mm(ps[:, turn_bank(layer, h), :], VMs[layer][:, m, h * P:(h + 1) * P], probT[:, m, :], start=(m == 0), stop=(m == MT - 1))
                ins.then_inc(xo_done, 1)

            def tile_taps(r):
                pe.wait_ge(c_diag, r + 1)
                pe.wait_ge(c_ulo, r + 1)
                if r >= 2:
                    pe.wait_ge(c_y, r - 1)
                dH, dL = diags[2 if r == KT - 1 else r % 2]
                for i in range(pe_taps[r]):
                    t = TAPS - pe_taps[r] + i
                    ins = exact(ps[:, tap_bank(r), :], (dH[:, i, :], dL[:, i, :]), (upH[:, t:t + S], upL[:, t:t + S]),
                                i == 0, i == pe_taps[r] - 1)
                ins.then_inc(c_pe, 1)

            pe.wait_ge(s_const, 1)
            pe.wait_ge(s_rows, 16 * len(vec_rows))
            o = 0
            for g, n in enumerate(rows_in):
                ins = nc.tensor.transpose(ps[:, 3, o:o + n], vrow[0:n, g, :], ident[0:n, 0:n])
                o += n
            ins.then_inc(s_tr, 1)
            pe.wait_ge(m_row, MT)
            for k in range(KT):
                if k >= 4:
                    pe.wait_ge(m_g, k - 3)
                for t in range(MT):
                    ins = nc.tensor.transpose(ps[:, 4 + k % 4, t * P:(t + 1) * P], mrow[:, t, k * P:(k + 1) * P], ident[:, :])
                ins.then_inc(m_tr, 1)

            def memory_values(num, c):
                pe.wait_ge(lo_ready, num + 1)
                par = num % 2
                for kk in range(2):
                    k = 2 * c + kk
                    w = slice(kk * 512, (kk + 1) * 512)
                    for t in range(MT):
                        f = slice(t * P, (t + 1) * P)
                        ins = exact(ps[:, 4 + t, :], (memH[:, k, f], memL[:, k, f]), (wH[:, par, w], wL[:, par, w]),
                                    k == 0, k == KT - 1)
                ins.then_inc(chunk_done, 1)

            n = first["kv0"]
            for c in range(2 * XH):
                if c < XH:
                    tile_chunk(n + c, tile0["kv0"] + c, other=(memH, memL), width=M, ready=None if c else 0)
                else:
                    memory_values(n + c, c - XH)
                if c == 0:
                    pe.wait_ge(s_x, 16 * ST)
                    pe.wait_ge(s_cst, 1)
                if c >= 2:
                    pe.wait_ge(x_upd, c - 1)
                for t in range(ST):
                    ins = nc.tensor.transpose(ps[:, 2 + c % 2, t * P:(t + 1) * P], xrow[:, t, c * P:(c + 1) * P], ident[:, :])
                ins.then_inc(x_tr, 1)

            for layer in range(2):
                if layer == 0:
                    n = first["xq0"]
                    for c in range(XH):
                        tile_chunk(n + c, tile0["xq0"] + c, ready=0 if c == 0 else None)
                        if c == 0:
                            stat(0)
                if layer == 0:
                    n = first["val"]
                    for c in range(2 * GT):
                        if c % 2 == 0:
                            attn_scores(0, c // 2)
                        else:
                            attn_turn(0, c // 2)
                        if c == 0:
                            pe.wait_ge(tile_free, tile0["head"])
                            pe.wait_ge(ms_ready, 1)
                            pe.wait_ge(kv_done, 1)
                        pe.wait_ge(lo_ready, n + c + 1)
                        par = c % 2
                        for kk in range(2):
                            k = 2 * (c % GT) + kk
                            w = slice(kk * 512, (kk + 1) * 512)
                            for t in range(ST):
                                if c == GT and kk == 0:
                                    pe.wait_ge(v_done, t + 1)
                                f = slice(t * P, (t + 1) * P)
                                ins = exact(ps[:, t, :], (xgH[:, k, f], xgL[:, k, f]), (wH[:, par, w], wL[:, par, w]),
                                            k == 0, k == KT - 1)
                        ins.then_inc(chunk_done, 1)
                        if c % 2:
                            attn_values(0, c // 2)
                    pe.wait_ge(v_done, ST + 2)

                    def level(lv, h, q, first_head):
                        if lv == 0:
                            pe.wait_ge(k_ready, h + 1)
                            pe.wait_ge(h_act, 3 * h + 2)
                            if not first_head:
                                pe.wait_ge(lv_taken, h * LV)
                        else:
                            pe.wait_ge(lv_ready, h * (LV - 1) + lv)
                        bank = ps[:, 6 + lv % 2, :]
                        A, B = qb[:, q, :], kb[:, q, :]
                        if lv < MASKED:
                            for b in range(ST):
                                f = slice(b * P, (b + 1) * P)
                                ins = mm(bank[:, f], B[:, f], A[:, f], start=True, stop=True)
                        elif lv == MASKED:
                            for b in range(2):
                                ins = mm(bank[:, b * P:(b + 1) * P], B[:, 2 * b * P:(2 * b + 1) * P],
                                         A[:, (2 * b + 1) * P:(2 * b + 2) * P], start=True, stop=True)
                        else:
                            for b in range(2):
                                ins = mm(bank[:, 2 * b * P:2 * (b + 1) * P], B[:, b * P:(b + 1) * P], A[:, 2 * P:4 * P],
                                         start=True, stop=True)
                        ins.then_inc(lv_done, 1)

                    def head_values(h, q, first_head):
                        pe.wait_ge(lv_taken, (h + 1) * LV)
                        if first_head:
                            pe.wait_ge(xo_lo, XH)
                        else:
                            pe.wait_ge(o_gated, h)
                        for t in range(ST):
                            ins = mm(ps[:, 4, t * P:S], vh[:, q, t, :], att[:, t, t * P:S], start=(t == 0), stop=(t == ST - 1))
                        ins.then_inc(o_done, 1)

                    def head_stat(h, first_head):
                        pe.wait_ge(o_sq, h + 1)
                        if not first_head:
                            pe.wait_ge(o_pre, h)
                        mm(ps[:, 5, :], ones[:, :], osq[:, :], start=True, stop=True).then_inc(o_stat, 1)

                    def places(place, h, b):
                        if b >= 1 and place < LV:
                            level(place, h - 1, 1 - b % 2, b == 1)
                        if b >= 2 and place == 2:
                            head_stat(h - 2, b == 2)
                        if b >= 1 and place == 11:
                            head_values(h - 1, 1 - b % 2, b == 1)

                    def head(b, i=0, k=0):
                        h = b + i * k
                        for j in range(3):
                            tile_chunk(first["head"] + 3 * b + j, tile0["head"] + 3 * h + j, i, 3 * k,
                                       between=lambda kt: places(4 * j + kt // 2, h, b) if kt % 2 else None)

                    for h in range(4):
                        head(h)
                    with pe.Fori(0, HEADS_LOOP) as i:
                        head(4, i, 2)
                        head(5, i, 2)
                else:
                    pe.wait_ge(tile_free, tile0["mix1"])
                    for r in range(KT):
                        for pos, kind, c in rounds[r]:
                            num = first["mix1"] + pos
                            if kind in ("gate", "value"):
                                bank = int(kind == "value")
                                tile_chunk(num, tile0["mix1"] + 2 * r + bank, bank=bank, ready=2 if num == first["mix1"] else None)
                                if pos == 0:
                                    stat(2)
                                if kind == "gate" and r == MID + 1:
                                    pe.wait_ge(c_y, MID)
                                    pe.wait_ge(c_sum, MID - 1)
                                    mm(ps[:, 3, :], ones[:, :], ysum[:, :], start=True, stop=True).then_inc(c_mid_pe, 1)
                                if kind == "gate" and r == MID + 2:
                                    pe.wait_ge(c_mid, 1)
                                if kind == "gate" and r >= XH:
                                    tile_taps(r - 1)
                                if kind == "gate" and r > XH:
                                    attn_turn(1, r - XH - 1)
                                if kind == "value" and r > XH:
                                    attn_values(1, r - XH - 1)
                            elif kind == "V":
                                if c == 0:
                                    pe.wait_ge(ms_ready, 3)
                                memory_values(num, c)
                                if pos == rounds[r][2][0]:
                                    tile_taps(r - 1)
                            else:
                                if c:
                                    pe.wait_ge(k_free if kind == "K" else q_free, c)
                                mem_in = (memH, memL) if kind == "K" else None
                                if kind == "K" and c == 0:
                                    pe.wait_ge(m_lo, 2 * KT)
                                tile_chunk(num, None, bank=6 if mem_in else 7, other=mem_in, width=M if mem_in else S)
                                if 0 < r < XH and pos == rounds[r][2][0]:
                                    tile_taps(r - 1)
                        if r >= XH:
                            if r == XH:
                                pe.wait_ge(kv_done, 2)
                                pe.wait_ge(k_free, XH)
                                pe.wait_ge(q_free, XH)
                            attn_scores(1, r - XH)
                    pe.wait_ge(c_y, KT - 1)

                n = first[f"out{layer}"]
                NG = MIXT // 2
                pe.wait_ge(tile_free, tile0[f"gu{layer}"])
                for c, (g, kp) in enumerate(out_order[layer]):
                    if kp >= KT // 2 and (layer, c) != (1, 1):
                        pe.wait_ge(xo_lo, XH * layer + 2 * (kp - KT // 2) + 2)
                    beside = None
                    if layer == 0 and c < 3:
                        beside = lambda p: places(4 * c + p, NH, NH)
                    if layer == 0 and c == 3:
                        beside = lambda p: head_stat(NH - 1, False) if p == 0 else None
                    if layer == 1 and c == 1:
                        tile_taps(KT - 1)
                        attn_turn(1, XH - 1)
                        attn_values(1, XH - 1)
                        pe.wait_ge(c_sum, KT - 1)
                        mm(ps[:, 5, :], ones[:, :], ysum[:, :], start=True, stop=True).then_inc(c_mu, 1)
                        pe.wait_ge(c_sqs, KT - 1)
                        mm(ps[:, 4, :], ones[:, :], sqsum[:, :], start=True, stop=True).then_inc(c_var, 1)
                        pe.wait_ge(xo_lo, 2 * XH)

                    def mixed(kk):
                        if kp < KT // 2:
                            pe.wait_ge(mix_lo, NH * layer + 2 * kp + kk + 1)
                        return mixH[:, 2 * kp + kk, :], mixL[:, 2 * kp + kk, :]

                    group_chunk(n + c, GT * g, mixed,
                                c % NG == 0, c % NG == NG - 1, between=beside)

                n = first[f"gu{layer}"]
                t0 = tile0[f"gu{layer}"]
                tile_chunk(n, t0, ready=2 * layer + 1)
                stat(2 * layer + 1)
                tile_chunk(n + 1, t0 + 1)
                with pe.Fori(0, FT - 1) as i:
                    tile_chunk(n + 2, t0 + 2 + 2 * i, i, 2)
                    tile_chunk(n + 3, t0 + 3 + 2 * i, i, 2)

                n = first[f"down{layer}"]
                pairs = FT // 2

                def hidden(kp):
                    return lambda kk: (actH[:, kp * 2 + kk, :], actL[:, kp * 2 + kk, :])

                def hidden_at(base, i):
                    return lambda kk: tuple(a[:, bass.ds(i * 4 + base + kk, 1), :].rearrange("p a s -> p (a s)") for a in (actH, actL))

                group_chunk(n, 0, hidden(0), True, False, free=t0 + 2 * FT)
                pe.wait_ge(act_lo, FT * layer + FT)
                group_chunk(n + 1, 0, hidden(1), False, False)
                with pe.Fori(0, (pairs - 3) // 2) as i:
                    group_chunk(n + 2, 0, hidden_at(4, i), False, False, i, 2)
                    group_chunk(n + 3, 0, hidden_at(6, i), False, False, i, 2)
                group_chunk(n + pairs - 1, 0, hidden(pairs - 1), False, True)
                group_chunk(n + pairs, GT, hidden(0), True, False)
                with pe.Fori(0, (pairs - 3) // 2) as i:
                    group_chunk(n + pairs + 1, GT, hidden_at(2, i), False, False, i, 2)
                    group_chunk(n + pairs + 2, GT, hidden_at(4, i), False, False, i, 2)
                if layer == 1:
                    pe.wait_ge(f_y, GT)
                    for k in range(GT):
                        turn_back(k)
                group_chunk(n + 2 * pairs - 2, GT, hidden(pairs - 2), False, False)
                group_chunk(n + 2 * pairs - 1, GT, hidden(pairs - 1), False, True)
            for k in range(GT, KT):
                pe.wait_ge(f_y, k + 1)
                if k == KT - 1:
                    stat(4)
                    pe.wait_ge(ms_ready, 5)
                turn_back(k)


_INS = ["x", "mem", "norm_mix_g", "norm_ffn_g", "w_out", "xattn_w_kv", "ffn_w_gu", "ffn_w_down", "mem_norm_g",
        "final_norm_g", "a_w_in", "a_b_in", "a_lb_table", "a_onorm_g", "b_w_in", "b_b_in", "b_dw_w", "b_dw_b",
        "b_ln_g", "b_ln_b"]


def kernel(**inputs):
    import numpy as np
    import concourse.bacc as bacc
    from concourse.bass_utils import run_bass_kernel_spmd

    nc = bacc.Bacc("TRN2", target_bir_lowering=False, num_devices=1)
    arrays, args = {}, []
    for name in _INS:
        a = np.ascontiguousarray(inputs[name])
        arrays[f"in_{name}"] = a
        args.append(nc.dram_tensor(f"in_{name}", a.shape, mybir.dt.from_np(a.dtype), kind="ExternalInput").ap())
    shape = np.asarray(inputs["x"]).shape
    args.append(nc.dram_tensor("out_0", shape, F32, kind="ExternalOutput").ap())
    trunk(nc, *args)
    r = run_bass_kernel_spmd(nc, [arrays], core_ids=[0])
    return r.results[0]["out_0"]
```
